# Optimizing a Trainium2 kernel written in Bass

```python
import jax, jax.numpy as jnp
from jax import lax
import numpy as np

D_MODEL = 1024
BATCH = 1
SEQ = 1024
DEPTH = 1
DEC_BATCH = 1
DEC_SEQ = 32
PAST_LEN = 256

CHUNK = 64
HEAD_DIM = 64
A_HEADS = D_MODEL // (2 * HEAD_DIM)
A_KV_HEADS = max(1, A_HEADS // 4)
WINDOW = 128
A_PREV_CHUNKS = -(-WINDOW // CHUNK)
A_ROWS = A_PREV_CHUNKS * CHUNK
B_HEADS = D_MODEL // (2 * HEAD_DIM)
B_PREV_CHUNKS = 8
B_ROWS = B_PREV_CHUNKS * CHUNK
REL_CLIP = 128
ROT_DIM = HEAD_DIM // 4
ROPE_THETA = 500000.0
N_GROUPS = 4
EXPERTS_PER_GROUP = 8
TOP_K = 2
EXPERT_FF = D_MODEL // 4
RMS_EPS = 1e-6
MASK_VALUE = -1e30
A_Q = A_HEADS * HEAD_DIM
A_KV = A_KV_HEADS * HEAD_DIM
B_W = B_HEADS * HEAD_DIM
IN_SPLITS = (A_Q, A_Q + A_KV, A_Q + 2 * A_KV, A_Q + 2 * A_KV + B_W, A_Q + 2 * A_KV + 2 * B_W)
IN_WIDTH = A_Q + 2 * A_KV + 3 * B_W
MIX_WIDTH = A_Q + B_W

kernel_name = 'hymba_swa_sink_chunkband_hmoe_step'

def _rmsnorm(x, g):
    xf = x.astype(jnp.float32)
    y = xf * lax.rsqrt(jnp.mean(xf * xf, axis=-1, keepdims=True) + RMS_EPS)
    return (y * g.astype(jnp.float32)).astype(x.dtype)

def _partial_rope(x, pos):
    half = ROT_DIM // 2
    inv_freq = ROPE_THETA ** (-jnp.arange(half, dtype=jnp.float32) / half)
    ang = pos.astype(jnp.float32)[:, None] * inv_freq[None, :]
    cos = jnp.cos(ang)[None, :, None, :]
    sin = jnp.sin(ang)[None, :, None, :]
    xf = x.astype(jnp.float32)
    x1 = xf[..., :half]
    x2 = xf[..., half:ROT_DIM]
    out = jnp.concatenate([x1 * cos - x2 * sin, x2 * cos + x1 * sin, xf[..., ROT_DIM:]], axis=-1)
    return out.astype(x.dtype)

def _attend(q, k, v, q_pos, k_pos, n_prev, sinks, rel_bias):
    n, lq, h, d = q.shape
    hk = k.shape[2]
    g = h // hk
    qg = q.reshape(n, lq, hk, g, d)
    s = jnp.einsum('nqjgd,nsjd->njgqs', qg, k, preferred_element_type=jnp.float32) * (d ** -0.5)
    qc = (q_pos // CHUNK)[:, None]
    kc = (k_pos // CHUNK)[None, :]
    valid = (k_pos[None, :] >= 0) & (kc <= qc) & (kc >= qc - n_prev)
    if rel_bias is not None:
        idx = jnp.clip(k_pos[None, :] - q_pos[:, None], -REL_CLIP, REL_CLIP) + REL_CLIP
        s = s + rel_bias[:, idx].astype(jnp.float32).reshape(hk, g, lq, -1)
    s = jnp.where(valid, s, MASK_VALUE)
    if sinks is not None:
        sk = sinks.astype(jnp.float32).reshape(hk, g, 1, 1)
        m = jnp.maximum(jnp.max(s, axis=-1, keepdims=True), sk)
        e = jnp.exp(s - m)
        p = e / (jnp.sum(e, axis=-1, keepdims=True) + jnp.exp(sk - m))
    else:
        p = jax.nn.softmax(s, axis=-1)
    o = jnp.einsum('njgqs,nsjd->nqjgd', p, v.astype(jnp.float32))
    return o.reshape(n, lq, h, d).astype(q.dtype)

def _chunk_band_attention(q, k, v, n_prev, sinks, rel_bias):
    n, s, h, d = q.shape
    pad = n_prev * CHUNK
    band = pad + CHUNK
    kp = jnp.pad(k, ((0, 0), (pad, 0), (0, 0), (0, 0)))
    vp = jnp.pad(v, ((0, 0), (pad, 0), (0, 0), (0, 0)))

    def one_chunk(c):
        start = c * CHUNK
        qc = lax.dynamic_slice_in_dim(q, start, CHUNK, axis=1)
        kc = lax.dynamic_slice_in_dim(kp, start, band, axis=1)
        vc = lax.dynamic_slice_in_dim(vp, start, band, axis=1)
        q_pos = start + jnp.arange(CHUNK)
        k_pos = start - pad + jnp.arange(band)
        return _attend(qc, kc, vc, q_pos, k_pos, n_prev, sinks, rel_bias)

    out = lax.map(one_chunk, jnp.arange(s // CHUNK))
    return jnp.moveaxis(out, 0, 1).reshape(n, s, h, d)

def _project(x, pos, norm1, w_in, q_norm_a, k_norm_a, q_norm_b, k_norm_b):
    n, l, _ = x.shape
    hx = _rmsnorm(x, norm1)
    z = jnp.einsum('nld,de->nle', hx, w_in)
    qa, ka, va, qb, kb, vb = jnp.split(z, IN_SPLITS, axis=-1)
    qa = qa.reshape(n, l, A_HEADS, HEAD_DIM)
    ka = ka.reshape(n, l, A_KV_HEADS, HEAD_DIM)
    va = va.reshape(n, l, A_KV_HEADS, HEAD_DIM)
    qb = qb.reshape(n, l, B_HEADS, HEAD_DIM)
    kb = kb.reshape(n, l, B_HEADS, HEAD_DIM)
    vb = vb.reshape(n, l, B_HEADS, HEAD_DIM)
    qa = _partial_rope(_rmsnorm(qa, q_norm_a), pos)
    ka = _partial_rope(_rmsnorm(ka, k_norm_a), pos)
    qb = _rmsnorm(qb, q_norm_b)
    kb = _rmsnorm(kb, k_norm_b)
    return qa, ka, va, qb, kb, vb

def _hier_moe(x, w_rg, b_rg, w_re, b_re, w_gate, w_up, w_down):
    n, l, dm = x.shape
    t = x.reshape(n * l, dm)
    g_logits = jnp.einsum('td,dg->tg', t, w_rg, preferred_element_type=jnp.float32) + b_rg.astype(jnp.float32)
    g_prob = jax.nn.softmax(g_logits, axis=-1)
    g_top_p, g_top = lax.top_k(g_prob, 1)
    e_logits = jnp.einsum('td,gde->tge', t, w_re, preferred_element_type=jnp.float32) + b_re.astype(jnp.float32)
    e_sel = jnp.take_along_axis(e_logits, g_top[:, :, None], axis=1)[:, 0]
    e_top_v, e_top = lax.top_k(e_sel, TOP_K)
    e_w = jax.nn.softmax(e_top_v, axis=-1) * g_top_p
    gate_in_group = jnp.einsum('tk,tke->te', e_w, jax.nn.one_hot(e_top, EXPERTS_PER_GROUP, dtype=jnp.float32))
    gate = jax.nn.one_hot(g_top[:, 0], N_GROUPS, dtype=jnp.float32)[:, :, None] * gate_in_group[:, None, :]
    out = jnp.zeros((n * l, dm), jnp.float32)
    for gi in range(N_GROUPS):
        for ei in range(EXPERTS_PER_GROUP):
            a = t @ w_gate[gi, ei]
            b = t @ w_up[gi, ei]
            hdn = jax.nn.silu(a) * b * gate[:, gi, ei, None].astype(t.dtype)
            out = out + jnp.matmul(hdn, w_down[gi, ei], preferred_element_type=jnp.float32)
    return out.astype(x.dtype).reshape(n, l, dm)

def _merge(x, oa, ob, out_norm_a, out_norm_b, w_out, norm2, w_rg, b_rg, w_re, b_re, w_gate, w_up, w_down):
    n, l, _ = x.shape
    oa = _rmsnorm(oa.reshape(n, l, A_Q), out_norm_a)
    ob = _rmsnorm(ob.reshape(n, l, B_W), out_norm_b)
    x = x + jnp.einsum('nle,ed->nld', jnp.concatenate([oa, ob], axis=-1), w_out)
    return x + _hier_moe(_rmsnorm(x, norm2), w_rg, b_rg, w_re, b_re, w_gate, w_up, w_down)

def _layer_prompt(x, proj, attn, post):
    _, s, _ = x.shape
    pos = jnp.arange(s)
    qa, ka, va, qb, kb, vb = _project(x, pos, *proj)
    sinks, rel_bias = attn
    oa = _chunk_band_attention(qa, ka, va, A_PREV_CHUNKS, sinks, None)
    ob = _chunk_band_attention(qb, kb, vb, B_PREV_CHUNKS, None, rel_bias)
    y = _merge(x, oa, ob, *post)
    return y, (ka[:, -A_ROWS:], va[:, -A_ROWS:], kb[:, -B_ROWS:], vb[:, -B_ROWS:])

def _layer_sample(x, ca_k, ca_v, cb_k, cb_v, proj, attn, post):
    _, l, _ = x.shape
    q_pos = PAST_LEN + jnp.arange(l)
    qa, ka, va, qb, kb, vb = _project(x, q_pos, *proj)
    sinks, rel_bias = attn
    wa = ca_k.shape[1]
    wb = cb_k.shape[1]
    oa = _attend(qa, jnp.concatenate([ca_k, ka], axis=1), jnp.concatenate([ca_v, va], axis=1),
                 q_pos, PAST_LEN - wa + jnp.arange(wa + l), A_PREV_CHUNKS, sinks, None)
    ob = _attend(qb, jnp.concatenate([cb_k, kb], axis=1), jnp.concatenate([cb_v, vb], axis=1),
                 q_pos, PAST_LEN - wb + jnp.arange(wb + l), B_PREV_CHUNKS, None, rel_bias)
    y = _merge(x, oa, ob, *post)
    return y, (ka, va, kb, vb)

def setup_inputs(seed: int = 0) -> dict:
    key = jax.random.key(seed)
    ks = jax.random.split(key, 26)
    f32 = jnp.float32

    def nrm(k, shape, scale=1.0):
        return jax.random.normal(k, shape, f32) * scale

    a_rows = min(A_ROWS, PAST_LEN)
    b_rows = min(B_ROWS, PAST_LEN)
    return {
        'x_prompt': nrm(ks[0], (BATCH, SEQ, D_MODEL)),
        'x_sample': nrm(ks[1], (DEC_BATCH, DEC_SEQ, D_MODEL)),
        'cache_a_k': nrm(ks[2], (DEPTH, DEC_BATCH, a_rows, A_KV_HEADS, HEAD_DIM)),
        'cache_a_v': nrm(ks[3], (DEPTH, DEC_BATCH, a_rows, A_KV_HEADS, HEAD_DIM)),
        'cache_b_k': nrm(ks[4], (DEPTH, DEC_BATCH, b_rows, B_HEADS, HEAD_DIM)),
        'cache_b_v': nrm(ks[5], (DEPTH, DEC_BATCH, b_rows, B_HEADS, HEAD_DIM)),
        'norm1': 1.0 + nrm(ks[6], (DEPTH, D_MODEL), 0.02),
        'w_in': nrm(ks[7], (DEPTH, D_MODEL, IN_WIDTH), D_MODEL ** -0.5),
        'q_norm_a': 1.0 + nrm(ks[8], (DEPTH, HEAD_DIM), 0.02),
        'k_norm_a': 1.0 + nrm(ks[9], (DEPTH, HEAD_DIM), 0.02),
        'q_norm_b': 1.0 + nrm(ks[10], (DEPTH, HEAD_DIM), 0.02),
        'k_norm_b': 1.0 + nrm(ks[11], (DEPTH, HEAD_DIM), 0.02),
        'sinks_a': nrm(ks[12], (DEPTH, A_HEADS), 1.0),
        'rel_bias_b': nrm(ks[13], (DEPTH, B_HEADS, 2 * REL_CLIP + 1), 0.5),
        'out_norm_a': 1.0 + nrm(ks[14], (DEPTH, A_Q), 0.02),
        'out_norm_b': 1.0 + nrm(ks[15], (DEPTH, B_W), 0.02),
        'w_out': nrm(ks[16], (DEPTH, MIX_WIDTH, D_MODEL), MIX_WIDTH ** -0.5),
        'norm2': 1.0 + nrm(ks[17], (DEPTH, D_MODEL), 0.02),
        'w_router_group': nrm(ks[18], (DEPTH, D_MODEL, N_GROUPS), D_MODEL ** -0.5),
        'b_router_group': nrm(ks[19], (DEPTH, N_GROUPS), 0.01),
        'w_router_expert': nrm(ks[20], (DEPTH, N_GROUPS, D_MODEL, EXPERTS_PER_GROUP), D_MODEL ** -0.5),
        'b_router_expert': nrm(ks[21], (DEPTH, N_GROUPS, EXPERTS_PER_GROUP), 0.01),
        'w_gate': nrm(ks[22], (DEPTH, N_GROUPS, EXPERTS_PER_GROUP, D_MODEL, EXPERT_FF), D_MODEL ** -0.5),
        'w_up': nrm(ks[23], (DEPTH, N_GROUPS, EXPERTS_PER_GROUP, D_MODEL, EXPERT_FF), D_MODEL ** -0.5),
        'w_down': nrm(ks[24], (DEPTH, N_GROUPS, EXPERTS_PER_GROUP, EXPERT_FF, D_MODEL), EXPERT_FF ** -0.5),
    }

def reference(x_prompt, x_sample, cache_a_k, cache_a_v, cache_b_k, cache_b_v,
              norm1, w_in, q_norm_a, k_norm_a, q_norm_b, k_norm_b, sinks_a, rel_bias_b,
              out_norm_a, out_norm_b, w_out, norm2, w_router_group, b_router_group,
              w_router_expert, b_router_expert, w_gate, w_up, w_down):
    y_p = x_prompt
    y_s = x_sample
    ak_p, av_p, bk_p, bv_p = [], [], [], []
    ak_s, av_s, bk_s, bv_s = [], [], [], []
    for layer in range(DEPTH):
        proj = (norm1[layer], w_in[layer], q_norm_a[layer], k_norm_a[layer], q_norm_b[layer], k_norm_b[layer])
        attn = (sinks_a[layer], rel_bias_b[layer])
        post = (out_norm_a[layer], out_norm_b[layer], w_out[layer], norm2[layer],
                w_router_group[layer], b_router_group[layer], w_router_expert[layer], b_router_expert[layer],
                w_gate[layer], w_up[layer], w_down[layer])
        y_p, st_p = _layer_prompt(y_p, proj, attn, post)
        y_s, st_s = _layer_sample(y_s, cache_a_k[layer], cache_a_v[layer], cache_b_k[layer], cache_b_v[layer],
                                  proj, attn, post)
        ak_p.append(st_p[0]); av_p.append(st_p[1]); bk_p.append(st_p[2]); bv_p.append(st_p[3])
        ak_s.append(st_s[0]); av_s.append(st_s[1]); bk_s.append(st_s[2]); bv_s.append(st_s[3])
    a_k_prompt = jnp.stack(ak_p, axis=0)
    a_v_prompt = jnp.stack(av_p, axis=0)
    b_k_prompt = jnp.stack(bk_p, axis=0)
    b_v_prompt = jnp.stack(bv_p, axis=0)
    a_k_sample = jnp.stack(ak_s, axis=0)
    a_v_sample = jnp.stack(av_s, axis=0)
    b_k_sample = jnp.stack(bk_s, axis=0)
    b_v_sample = jnp.stack(bv_s, axis=0)
    return (y_p, y_s, a_k_prompt, a_v_prompt, b_k_prompt, b_v_prompt,
            a_k_sample, a_v_sample, b_k_sample, b_v_sample)


_drawn_inputs = setup_inputs


def setup_inputs(seed=0):
    import zlib

    import numpy as np

    out = dict(_drawn_inputs(seed))
    spreads = {}
    factors = {'q_norm_a': 4.107,
     'q_norm_b': 8.88,
     'k_norm_b': 7.623,
     'sinks_a': 8.0,
     'out_norm_a': 10.653,
     'b_router_group': 28.294,
     'b_router_expert': 20.542,
     'out_norm_b': 8.0,
     'norm2': 4.264}
    for name, (base, spread) in spreads.items():
        noise = np.random.default_rng([zlib.crc32(name.encode()), seed]).standard_normal(out[name].shape)
        drawn = base * np.exp(spread * noise) if base else spread * noise
        out[name] = __import__('jax').numpy.asarray(drawn.astype(out[name].dtype))
    for name, factor in factors.items():
        out[name] = (out[name] * factor).astype(out[name].dtype)
    return out
```

```python
import numpy as np
import concourse.bass as bass
from concourse import mybir
from contextlib import ExitStack

F32 = mybir.dt.float32
BF16 = mybir.dt.bfloat16
I32 = mybir.dt.int32
ALU = mybir.AluOpType
ACT = mybir.ActivationFunctionType
AXX = mybir.AxisListType.X

D = 1024
P = 128
KD = D // P
SEQ, DEC = 1024, 32
NT = SEQ // P + 1
ROWS = NT * P
HD = 64
HEADS = 8
CACHE_A, CACHE_B = 128, 256
EPS = 1e-6
NG, NE, FF = 4, 32, 256
NR = NG + NE
NBLOCK = 48
NINFO = NBLOCK + 2
KW = 5 * P
EW = 2 * KD * FF + 2 * D
FAR = 1 << 20
BIG = 1e30

CHUNK = (512, 256, 512, 512, 512)
Z_BANK = (0, 1, 2, 3, 1)
CHUNK_AT = (0, 4096, 6144, 10240, 14336)


class Chain:

    def __init__(self, eng, sem):
        self.eng, self.sem, self.base, self.k, self.i, self.per = eng, sem, 0, 0, None, 0

    def enter(self, i, per):
        self.i, self.per, self.k, self.base = i, per, 0, self.base + self.k

    def leave(self, times):
        assert self.k == self.per, (self.k, self.per)
        self.base, self.k, self.i = self.base + times * self.per, 0, None

    def link(self, ins):
        ins.then_inc(self.sem, 1)
        self.k += 1
        v = self.base + self.k
        v = v if self.i is None else self.i * self.per + v
        self.eng.wait_ge(self.sem, v)


def tile_keys(t):
    if t == NT - 1:
        return ([(ROWS, CACHE_A), (SEQ, DEC)], [(ROWS, CACHE_B), (SEQ, DEC)])
    a, b = max(0, t - 1), max(0, t - 4)
    return ([(a * P, (t + 1 - a) * P)], [(b * P, (t + 1 - b) * P)])


def build(nc, d, o):
    ctx = ExitStack()
    with ctx:
        def sem(name):
            return ctx.enter_context(nc.semaphore(name))

        arena = ctx.enter_context(nc.sbuf_tensor("arena", [P, 52700], F32))
        ps = ctx.enter_context(nc.psum_tensor("ps", [P, 8 * 512], F32))
        top = [0]

        def place(n, at=None):
            a = top[0] if at is None else at
            if at is None:
                top[0] += n
            assert a + n <= 52700, (a, n)
            return arena[:, a:a + n]

        ident = place(P)
        g1 = place(KD)
        g64 = place(4 * HD).rearrange("p (a d) -> p a d", d=HD)
        rope = place(NT * 16).rearrange("p (t c) -> p t c", c=16)
        sinks = place(HEADS)
        rbias = place(NR)
        logits = place(NT * NR).rearrange("p (t c) -> p t c", c=NR)
        ssx, rsx = place(2), place(2)
        eps = place(1)
        ss26, rs26 = place(26), place(26)
        negm = place(2 * 16).rearrange("p (b c) -> p b c", b=2)
        mx = place(2)
        psum_e = place(2 * 16).rearrange("p (b c) -> p b c", b=2)
        esink = place(HEADS)
        rden = place(16)
        sso, rso = place(2), place(2)
        ss2, rs2 = place(1), place(1)
        ctl = place(64).bitcast(I32)
        info = place(NINFO * 4).bitcast(I32).rearrange("p (b c) -> p b c", c=4)
        gidx = place(4).bitcast(I32)
        sidx = place(4).bitcast(I32)
        qt = place(NT * D).rearrange("p (t g c) -> p t g c", t=NT, g=8)
        row = qt.rearrange("p t g c -> p t (g c)")
        free_from = top[0]
        KC = ROWS + CACHE_B
        ktb = place(4 * KC).rearrange("p (g c) -> p g c", g=4)
        KCA = ROWS + CACHE_A
        kta = place(KCA)
        vb = place((NT + 2) * 512).rearrange("p (t c) -> p t c", t=NT + 2)
        va = place((NT + 1) * P).rearrange("p (t c) -> p t c", t=NT + 1)
        region = top[0]
        w_in = place(KD * sum(CHUNK))
        xt = place(2 * D).rearrange("p (b k c) -> p b k c", b=2, k=KD)
        xr = place(2 * D).rearrange("p (b c) -> p b c", b=2)
        z = place(2 * 1664).rearrange("p (b c) -> p b c", b=2)
        sq = place(1664)
        top[0] = region
        bm = place(HEADS * KW).rearrange("p (h c) -> p h c", h=HEADS)
        maskb = place(KW)
        maska = place(2 * P)
        w_out = place(KD * D).rearrange("p (k c) -> p k c", k=KD)
        sp = place(2 * KW).rearrange("p (b c) -> p b c", b=2)
        pt = place(2 * KW).rearrange("p (b c) -> p b c", b=2)
        ot = place(D).rearrange("p (k c) -> p k c", k=KD)
        h2 = place(2 * D).rearrange("p (b c) -> p b c", b=2)
        h2t = place(D).rearrange("p (k c) -> p k c", k=KD)
        xc = place(2 * D).rearrange("p (b c) -> p b c", b=2)
        g_o = place(D)
        g2 = place(D)
        wr = place(KD * NR).rearrange("p (k c) -> p k c", k=KD)
        junk = place(D)
        top[0] = free_from
        c_tri32 = place(NE * NE).rearrange("p (a b) -> p a b", a=NE)
        c_steps = place(9)
        c_block = place(NINFO)
        c_turn = place(48).rearrange("p (a b) -> p a b", a=4)
        c_iota = place(NE)
        c_valid = place(NT)
        c_far = place(NT)
        c_token = place(NT * 2).rearrange("p (t k) -> p t k", k=2)
        c_dest = place(NT * 2).rearrange("p (t k) -> p t k", k=2)
        tri = place(64).bitcast(BF16)
        ones = place(64).bitcast(BF16)

        def rt(n):
            return place(NT * n).rearrange("p (t c) -> p t c", t=NT)
        gmx, gsum, gp, idx, v1, v2, e12, ww = (rt(1) for _ in range(8))
        geq, goh, gex = rt(NG), rt(NG), rt(NG)
        m32, eq, oh1, oh2, m2 = (rt(NE) for _ in range(5))
        mb = place(NT * NE // 2).bitcast(BF16).rearrange("p (t c) -> p t c", t=NT)
        cntv = place(NE)
        cmp9 = place(NE * 9).rearrange("p (a b) -> p a b", b=9)
        nblk, excl, incl, basev = place(NE), place(NE), place(NE), place(NE)
        prod = place(NE * NE).rearrange("p (a b) -> p a b", a=NE)
        cmpb = place(NINFO * NE).rearrange("p (a b) -> p a b", b=NE)
        cmpt = place(48).rearrange("p (a b) -> p a b", a=4)
        ctlf = place(64)
        slots = place(NT * 2).rearrange("p (t k) -> p t k", k=2)
        sloti = place(NT * 2).bitcast(I32).rearrange("p (t k) -> p t k", k=2)
        load4 = place(NT * 8).bitcast(I32).rearrange("p (t k c) -> p t k c", t=NT, k=2)
        fill = place(NINFO * 4).bitcast(I32).rearrange("p (b c) -> p b c", c=4)
        assert top[0] <= region
        dtop = [free_from]

        def dplace(n):
            dtop[0] += n
            return place(n, dtop[0] - n)
        wx = dplace(4 * EW).rearrange("p (b c) -> p b c", b=4)
        xg = dplace(4 * D).rearrange("p (b c) -> p b c", b=4)
        xgt = dplace(2 * D).rearrange("p (b k c) -> p b k c", b=2, k=KD)
        yb = dplace(4 * D).rearrange("p (b c) -> p b c", b=4)
        sil = dplace(FF).rearrange("p (b c) -> p b c", b=2)
        hd = dplace(FF).rearrange("p (b c) -> p b c", b=2)
        hdt = dplace(FF).rearrange("p (b c) -> p b c", b=2)
        ye = wx.rearrange("p b c -> p (b c)")[:, 0:4 * D].rearrange("p (b k c) -> p b k c", b=2, k=2)

        def bank(n, a=0, b=512):
            return ps[:, n * 512 + a:n * 512 + b]
        o_ps = bank(5)

        def scores_at(u, width):
            return 0 if u % 2 == 0 else (1024 if width <= 512 else 1024 + 512 - KW)

        h2d = nc.dram_tensor("h2_rows", [ROWS, D], F32).ap()
        tab = nc.dram_tensor("slot_table", [NINFO * P, 4], I32).ap()
        ykd = nc.dram_tensor("expert_rows", [2 * ROWS, D], F32).ap()

        s_const = sem("constants_loaded")
        s_win = [sem(f"w_in{c}_loaded") for c in range(5)]
        s_xt = [sem(f"xt{j}_loaded") for j in range(2)]
        s_xr = [sem(f"xrow{j}_loaded") for j in range(2)]
        s_cache = sem("caches_loaded")
        s_bload = sem("stage_b_loaded")
        s_xc = [sem(f"residual{j}_loaded") for j in range(2)]
        s_rload = sem("routing_constants_loaded")
        s_xg = sem("xt_scaled")
        s_eps = sem("eps_ready")
        s_ss26 = sem("head_squares_summed")
        s_rs26 = sem("head_rstd_ready")
        s_ssx = sem("x_squares_summed")
        s_rsx = sem("x_rstd_ready")
        s_z = sem("z_chunks_made")
        s_zev = sem("z_chunks_copied")
        s_zn = sem("z_normed")
        s_tr = sem("z_transposed")
        s_tea = sem("transposes_copied_by_act")
        s_tev = sem("transposes_copied_by_dve")
        s_bm = sem("bias_masked")
        s_qk = sem("scores_made")
        s_sp = sem("scores_biased")
        s_p = sem("probs_ready")
        s_pt = sem("probs_transposed")
        s_ptv = sem("probs_t_copied_by_dve")
        s_pta = sem("probs_t_copied_by_act")
        s_pv = sem("heads_summed")
        s_es = sem("sinks_exp")
        s_nsk = sem("sinks_shifted")
        s_on = sem("mixer_out_divided")
        s_so = sem("mixer_squares_summed")
        s_og = sem("mixer_out_normed")
        s_t1 = sem("mixer_out_transposed")
        s_ota = sem("ot_copied_by_act")
        s_otv = sem("ot_copied_by_dve")
        s_op = sem("out_projected")
        s_x2 = sem("residual_added")
        s_s2 = sem("residual_squares_summed")
        s_h2 = sem("h2_ready")
        s_h2o = [sem(f"h2_stored{j}") for j in range(2)]
        s_t2 = sem("h2_transposed")
        s_h2a = sem("h2t_copied_by_act")
        s_h2v = sem("h2t_copied_by_dve")
        s_r = sem("logits_made")
        s_rv = sem("logits_copied")
        s_gx = sem("group_shifted")
        s_gxe = sem("group_exp")
        s_v12 = sem("top2_difference")
        s_v12e = sem("top2_exp")
        s_mb = sem("membership_ready")
        s_cum = sem("positions_counted")
        s_fill = sem("fill_ready")
        s_tabf = sem("table_filled")
        s_slot = sem("slots_ready")
        s_scat = sem("table_scattered")
        s_w = [sem(f"expert_loaded{j}") for j in range(4)]
        s_g = [sem(f"rows_gathered{j}") for j in range(4)]
        s_gi = sem("indices_copied")
        s_xgz = sem("gather_buffers_cleared")
        s_bx = sem("rows_transposed")
        s_xa = sem("rows_t_copied_by_act")
        s_xv = sem("rows_t_copied_by_dve")
        s_gu = sem("gate_up_made")
        s_sil = sem("silu_ready")
        s_h = sem("hidden_ready")
        s_ht = sem("hidden_transposed")
        s_hta = sem("hidden_t_copied")
        s_y = sem("expert_out_made")
        s_ya = sem("expert_out_copied_by_act")
        s_yv = sem("expert_out_copied_by_dve")
        s_ysc = [sem(f"expert_out_scattered{j}") for j in range(4)]
        s_ydone = sem("all_scattered")
        s_ye = [sem(f"expert_pair{j}_loaded") for j in range(2)]
        s_fin = sem("rows_summed")
        s_out = [sem(f"rows_stored{j}") for j in range(2)]
        s_kv = sem("states_stored")
        s_dve = sem("dve_own")
        s_act = sem("act_own")
        s_pool = sem("pool_own")

        C_TR, C_H = 5, 3

        units = [(t, m, h) for t in range(NT) for m in (0, 1) for h in range(HEADS)]
        NU = len(units)

        def unit_info(u):
            t, m, h = units[u]
            segs = tile_keys(t)[m]
            tiles, c = [], 0
            for col, n in segs:
                for k in range(0, n, P):
                    tiles.append((c + k, (col + k) // P, min(P, n - k)))
                c += n
            return t, m, h, segs, tiles, c

        def first_bias(t, m):
            if t == NT - 1:
                return 0 if m == 0 else 2 * P
            return ((1 - min(t, 1)) if m == 0 else (4 - min(t, 4))) * P

        def slot_of(u):
            return units[u][0] - 1, u % 16

        block = ctx.enter_context(nc.Block())

        @block.sync
        def _(sp_):
            def load_x(t, j):
                sp_.dma_start(xt[:, j], d["xT"][t]).then_inc(s_xt[j], 16)
                sp_.dma_start(xr[:, j], d["x"][t]).then_inc(s_xr[j], 16)

            load_x(0, 0)
            with sp_.Fori(0, 4) as i:
                for j in range(2):
                    t = i * 2 + j
                    sp_.wait_ge(s_z, i * 10 + (5 * j + 1))
                    sp_.wait_ge(s_ssx, i * 10 + (5 * j + 1))
                    load_x(t + 1, 1 - j)
            sp_.wait_ge(s_z, 1 + 5 * NT)
            sp_.wait_ge(s_ssx, 1 + 5 * NT)
            sp_.wait_ge(s_zn, NT)
            sp_.wait_ge(s_tr, C_TR + 4 * NT)
            sp_.dma_start(bm, d["bias"]).then_inc(s_bload, 16)
            sp_.dma_start(maskb, d["maskb"]).then_inc(s_bload, 16)
            sp_.dma_start(maska, d["maska"]).then_inc(s_bload, 16)
            sp_.dma_start(g_o, d["g_o"].partition_broadcast(P)).then_inc(s_bload, 16)
            sp_.dma_start(w_out, d["w_out"]).then_inc(s_bload, 16)
            sp_.dma_start(g2, d["g2"].partition_broadcast(P)).then_inc(s_bload, 16)
            sp_.dma_start(wr, d["wr"]).then_inc(s_bload, 16)
            sp_.wait_ge(s_tea, 2 + 2 * NT)
            sp_.wait_ge(s_tev, 2 + 2 * NT)
            sp_.wait_ge(s_zev, 5 + 5 * NT)
            sp_.dma_start(o["kb_p"], ktb[:, :, SEQ - 512:SEQ]).then_inc(s_kv, 16)
            sp_.dma_start(o["ka_p"], kta[:, SEQ - P:SEQ]).then_inc(s_kv, 16)
            sp_.dma_start(o["vb_p"], vb[:, 4:8, :]).then_inc(s_kv, 16)
            sp_.dma_start(o["va_p"], va[:, 7, :]).then_inc(s_kv, 16)
            sp_.dma_start(o["kb_s"], ktb[:, :, SEQ:SEQ + DEC]).then_inc(s_kv, 16)
            sp_.dma_start(o["ka_s"], kta[:, SEQ:SEQ + DEC]).then_inc(s_kv, 16)
            sp_.dma_start(o["vb_s"], vb[0:DEC, 8, :]).then_inc(s_kv, 16)
            sp_.dma_start(o["va_s"], va[0:DEC, 8, :]).then_inc(s_kv, 16)
            for t in range(NT):
                if t >= 2:
                    sp_.wait_ge(s_x2, 2 * (t - 1))
                sp_.dma_start(xc[:, t % 2], d["x"][t]).then_inc(s_xc[t % 2], 16)
                if t >= 1:
                    sp_.wait_ge(s_h2, t)
                    sp_.dma_start(h2d[(t - 1) * P:t * P, :], h2[:, (t - 1) % 2]).then_inc(s_h2o[(t - 1) % 2], 16)
            sp_.wait_ge(s_h2, NT)
            sp_.dma_start(h2d[(NT - 1) * P:, :], h2[:, (NT - 1) % 2]).then_inc(s_h2o[(NT - 1) % 2], 16)
            sp_.wait_ge(s_pv, NU)
            sp_.wait_ge(s_kv, 16 * 8)
            for dst, name in ((c_tri32, "tri32"), (c_steps, "steps"), (c_block, "block"), (c_turn, "turn"), (c_iota, "iota")):
                sp_.dma_start(dst, d[name].partition_broadcast(P)).then_inc(s_rload, 16)
            for dst, name in ((c_valid, "valid"), (c_far, "far"), (c_token, "token"), (c_dest, "dest"),
                              (tri, "tri"), (ones, "ones")):
                sp_.dma_start(dst, d[name]).then_inc(s_rload, 16)
            sp_.wait_ge(s_fill, 1)
            sp_.dma_start(tab.rearrange("(b p) c -> p b c", p=P), fill).then_inc(s_tabf, 16)
            sp_.wait_ge(s_slot, 1)
            sp_.wait_ge(s_scat, 16 * 18)
            sp_.wait_ge(s_rv, NT)
            nb = sp_.value_load(ctl[0:1, NINFO:NINFO + 1], min_val=17, max_val=NBLOCK)
            with sp_.Fori(0, NBLOCK // 4) as i:
                for j in range(4):
                    with sp_.If(i * 4 + j < nb):
                        e = sp_.value_load(ctl[0:1, bass.ds(i * 4 + j, 1)], min_val=0, max_val=NE - 1)
                        sp_.wait_ge(s_y, i * 4 + j + 1)
                        sp_.dma_start(wx[:, j], d["wexp"][bass.ds(e, 1)].rearrange("a p c -> p (a c)")).then_inc(s_w[j], 16)
            sp_.wait_ge(s_ydone, 1)
            for t in range(NT):
                j, n = t % 2, P if t < NT - 1 else DEC
                if t >= 2:
                    sp_.wait_ge(s_fin, t - 1)
                for k in range(2):
                    sp_.dma_start(ye[0:n, j, k], ykd[k * ROWS + t * P:k * ROWS + t * P + n, :]).then_inc(s_ye[j], 16)
                if t >= 1:
                    sp_.wait_ge(s_fin, t)
                    sp_.dma_start(o["y_p"][(t - 1) * P:t * P, :], row[:, t - 1]).then_inc(s_out[0], 16)
            sp_.wait_ge(s_fin, NT)
            sp_.dma_start(o["y_s"], row[0:DEC, NT - 1]).then_inc(s_out[1], 16)
            sp_.wait_ge(s_out[0], 16 * 8)
            sp_.wait_ge(s_out[1], 16)

        @block.gpsimd
        def _(pool):
            nc.gpsimd.memset(eps, EPS).then_inc(s_eps, 1)
            pool.wait_ge(s_const, 16 * 6)
            gain = g1.unsqueeze(2).broadcast_to([P, KD, P])

            def scale_x(wait, j):
                pool.wait_ge(s_xt[j], wait)
                nc.gpsimd.tensor_tensor(xt[:, j], xt[:, j], gain, ALU.mult).then_inc(s_xg, 1)

            scale_x(16, 0)
            with pool.Fori(0, 4) as i:
                scale_x(i * 16 + 16, 1)
                scale_x(i * 16 + 32, 0)
            pool.wait_ge(s_pv, NU)
            pool.wait_ge(s_kv, 16 * 8)
            nc.gpsimd.memset(fill[:, :, 0:2], FAR)
            nc.gpsimd.memset(fill[:, :, 2:4], 0).then_inc(s_fill, 1)
            pool.wait_ge(s_rv, NT)
            pool.wait_ge(s_h2o[0], 16 * 5)
            pool.wait_ge(s_h2o[1], 16 * 4)
            nc.gpsimd.memset(xg, 0.0).then_inc(s_xgz, 1)
            pool.wait_ge(s_slot, 1)
            pool.wait_ge(s_tabf, 16)
            for t in range(NT):
                for k in range(2):
                    pool.indirect_dma_start(
                        out=tab, out_offset=bass.IndirectOffsetOnAxis(ap=sloti[:, t, k:k + 1], axis=0),
                        in_=load4[:, t, k, :], in_offset=None, bounds_check=NINFO * P - 1,
                        oob_is_err=False).then_inc(s_scat, 16)
            nb = pool.value_load(ctl[0:1, NINFO:NINFO + 1], min_val=17, max_val=NBLOCK)
            pool.wait_ge(s_scat, 16 * 18)
            cuts = [0, 12, 24, 36, NINFO]
            for j in range(4):
                pool.dma_start(info[:, cuts[j]:cuts[j + 1]],
                               tab.rearrange("(b p) c -> p b c", p=P)[:, cuts[j]:cuts[j + 1]]).then_inc(s_ysc[j], 16)
            for j in range(4):
                pool.wait_ge(s_ysc[j], 16)
            pool.wait_ge(s_xgz, 1)
            chain = Chain(pool, s_pool)
            row_bound, out_bound = pool.to_reg(ROWS - 1), pool.to_reg(2 * ROWS - 1)
            def gather(b, j):
                chain.link(nc.gpsimd.tensor_copy(gidx[:, j:j + 1], info[:, bass.ds(b, 1), 0:1].rearrange("p a b -> p (a b)")
                                                 if not isinstance(b, int) else info[:, b, 0:1]))
                pool.sem_inc(s_gi, 1)
                pool.indirect_dma_start(
                    out=xg[:, j], out_offset=None, in_=h2d,
                    in_offset=bass.IndirectOffsetOnAxis(ap=gidx[:, j:j + 1], axis=0),
                    bounds_check=row_bound, oob_is_err=False).then_inc(s_g[j], 16)

            gather(0, 0)
            gather(1, 1)
            with pool.Fori(0, NBLOCK // 4) as i:
                chain.enter(i, 8)
                for j in range(4):
                    b = i * 4 + j
                    with pool.If(b < nb):
                        pool.wait_ge(s_bx, b + 1)
                        gather(b + 2, (j + 2) % 4)
                        pool.wait_ge(s_ysc[j], i * 16 + 16)
                        chain.link(nc.gpsimd.tensor_copy(sidx[:, j:j + 1],
                                                         info[:, bass.ds(b, 1), 1:2].rearrange("p a b -> p (a b)")))
                        pool.wait_ge(s_ya, b + 2)
                        pool.wait_ge(s_yv, b + 2)
                        pool.sem_inc(s_gi, 1)
                        pool.indirect_dma_start(
                            out=ykd, out_offset=bass.IndirectOffsetOnAxis(ap=sidx[:, j:j + 1], axis=0),
                            in_=yb[:, j], in_offset=None, bounds_check=out_bound,
                            oob_is_err=False).then_inc(s_ysc[j], 16)
            scatters = [pool.value_load(ctl[0:1, NINFO + 1 + j:NINFO + 2 + j], min_val=16, max_val=16 * 16)
                        for j in range(4)]
            for j in range(4):
                pool.wait_ge(s_ysc[j], scatters[j])
            pool.sem_inc(s_ydone, 1)

        @block.scalar
        def _(act):
            for c in range(5):
                act.dma_start(w_in[:, CHUNK_AT[c]:CHUNK_AT[c] + KD * CHUNK[c]],
                              d["w_in"][:, CHUNK_AT[c]:CHUNK_AT[c] + KD * CHUNK[c]]).then_inc(s_win[c], 16)
                if c == 0:
                    act.dma_start(g1, d["g1"]).then_inc(s_const, 16)
                    act.dma_start(ident, d["ident"]).then_inc(s_const, 16)
                    act.dma_start(g64, d["g64"].partition_broadcast(P)).then_inc(s_const, 16)
                    act.dma_start(rope, d["rope"]).then_inc(s_const, 16)
                    act.dma_start(sinks, d["sinks"].partition_broadcast(P)).then_inc(s_const, 16)
                    act.dma_start(rbias, d["rbias"].partition_broadcast(P)).then_inc(s_const, 16)
            act.dma_start(ktb[:, :, ROWS:], d["ckb"]).then_inc(s_cache, 16)
            act.dma_start(kta[:, ROWS:], d["cka"]).then_inc(s_cache, 16)
            act.dma_start(vb[:, NT:, :], d["cvb"]).then_inc(s_cache, 16)
            act.dma_start(va[:, NT, :], d["cva"]).then_inc(s_cache, 16)
            chain = Chain(act, s_act)
            act.wait_ge(s_eps, 1)

            def rstd(out, ms):
                chain.link(nc.scalar.activation(out, ms, ACT.Ln, bias=eps))
                return nc.scalar.activation(out, out, ACT.Exp, scale=-0.5)

            act.sem_inc(s_zev, 5)
            act.sem_inc(s_tea, 2)
            act.sem_inc(s_ssx, 1)

            def square_x(wait, sq1, j):
                act.wait_ge(s_xr[j], wait)
                nc.scalar.activation(xr[:, j], xr[:, j], ACT.Square, scale=D ** -0.5,
                                     accum_out=ssx[:, j:j + 1]).then_inc(s_ssx, 5)
                act.wait_ge(s_ssx, sq1)
                rstd(rsx[:, j:j + 1], ssx[:, j:j + 1]).then_inc(s_rsx, 1)

            def chunks_out(t5, t4, t1, tt, j):
                act.wait_ge(s_rsx, t1)
                act.wait_ge(s_tr, t4)
                vbt = vb[:, tt, :] if isinstance(tt, int) else vb[:, bass.ds(tt, 1), :].rearrange("p a c -> p (a c)")
                vat = va[:, tt, :] if isinstance(tt, int) else va[:, bass.ds(tt, 1), :].rearrange("p a c -> p (a c)")
                for c, dst in enumerate((z[:, j, 0:512], None, z[:, j, 640:1152], z[:, j, 1152:1664], vbt)):
                    act.wait_ge(s_z, t5 + c + 2)
                    if c == 1:
                        nc.scalar.activation(z[:, j, 512:640], bank(1, 0, 128), ACT.Copy, scale=rsx[:, j:j + 1])
                        ins = nc.scalar.activation(vat, bank(1, 128, 256), ACT.Copy, scale=rsx[:, j:j + 1])
                    else:
                        ins = nc.scalar.activation(dst, bank(Z_BANK[c]), ACT.Copy, scale=rsx[:, j:j + 1])
                    ins.then_inc(s_zev, 1)

            def heads_rstd(t1):
                act.wait_ge(s_ss26, t1)
                rstd(rs26, ss26).then_inc(s_rs26, 1)

            def transposes_out(t4, tt, col):
                act.wait_ge(s_tr, t4 + C_TR + 1)
                q = qt[:, tt, 0:4, :] if isinstance(tt, int) else qt[:, bass.ds(tt, 1), 0:4, :].rearrange("p a g c -> p (a g) c")
                nc.scalar.activation(q, bank(5).rearrange("p (g c) -> p g c", g=4), ACT.Copy,
                                     scale=HD ** -0.5).then_inc(s_tea, 1)
                act.wait_ge(s_tr, t4 + C_TR + 2)
                nc.scalar.activation(ktb[:, :, bass.ds(col, P)], bank(6).rearrange("p (g c) -> p g c", g=4),
                                     ACT.Copy).then_inc(s_tea, 1)

            square_x(16, 6, 0)
            chunks_out(0, C_TR - 4, 1, 0, 0)
            heads_rstd(1)
            with act.Fori(0, 4) as i:
                chain.enter(i, 4)
                for j in range(2):
                    square_x(i * 16 + (16 if j == 0 else 32), i * 10 + (5 * j + 11), 1 - j)
                    chunks_out(i * 10 + 5 * (j + 1), i * 8 + (4 * j + C_TR), i * 2 + (j + 2), i * 2 + (j + 1), 1 - j)
                    transposes_out(i * 8 + 4 * j, i * 2 + j, i * 256 + j * P)
                    heads_rstd(i * 2 + (j + 2))
                chain.leave(4)
            transposes_out(4 * (NT - 1), NT - 1, (NT - 1) * P)

            def copy_pt(u):
                _, _, _, _, tiles, _ = unit_info(u)
                cut = (len(tiles) + 1) // 2
                act.wait_ge(s_pt, u + 1)
                rest = tiles[cut:]
                if not rest:
                    act.sem_inc(s_pta, 1)
                    return
                if u >= 2:
                    act.wait_ge(s_pv, u - 1)
                c0 = cut * P
                full = [x for x in rest if x[2] == P]
                ins = None
                if full:
                    c1 = c0 + len(full) * P
                    ins = nc.scalar.activation(pt[:, u % 2, c0:c1], bank(4, 0, c1 - c0), ACT.Copy)
                    c0 = c1
                if len(full) < len(rest):
                    n = rest[-1][2]
                    ins = nc.scalar.activation(pt[0:n, u % 2, c0:c0 + P], bank(4, len(full) * P, len(full) * P + P)[0:n],
                                               ACT.Copy)
                ins.then_inc(s_pta, 1)

            def squares_out(t, m):
                chain.link(nc.scalar.activation(junk[:, 0:512], row[:, t, 512 * m:512 * m + 512], ACT.Square,
                                                scale=512 ** -0.5, accum_out=sso[:, m:m + 1]))
                rstd(rso[:, m:m + 1], sso[:, m:m + 1]).then_inc(s_so, 1)

            def act_pieces(t, k):
                if t < 0:
                    return
                if k == 2:
                    act.wait_ge(s_t1, 2 * t + 1)
                    nc.scalar.activation(ot[:, 0:4], bank(6).rearrange("p (g c) -> p g c", g=4), ACT.Copy).then_inc(s_ota, 1)
                if k == 9:
                    act.wait_ge(s_x2, 2 * (t + 1))
                    chain.link(nc.scalar.activation(junk, row[:, t], ACT.Square, scale=D ** -0.5, accum_out=ss2))
                    rstd(rs2, ss2).then_inc(s_s2, 1)
                if k == 13:
                    act.wait_ge(s_t2, 2 * t + 1)
                    nc.scalar.activation(h2t[:, 0:4], bank(6).rearrange("p (g c) -> p g c", g=4), ACT.Copy).then_inc(s_h2a, 1)

            for u in range(NU):
                t, m, h, segs, tiles, width = unit_info(u)
                k = u % 16
                act.wait_ge(s_sp, u + 1)
                c = m * HEADS + h
                nc.scalar.activation(sp[:, u % 2, 0:width], sp[:, u % 2, 0:width], ACT.Exp,
                                     bias=negm[:, t % 2, c:c + 1], accum_out=psum_e[:, t % 2, c:c + 1]).then_inc(s_p, 1)
                if u >= 1:
                    copy_pt(u - 1)
                if k == 8:
                    act.wait_ge(s_on, 2 * t + 1)
                    squares_out(t, 0)
                if k == 7:
                    act.wait_ge(s_nsk, t + 1)
                    nc.scalar.activation(esink, esink, ACT.Exp).then_inc(s_es, 1)
                if k == 0 and t >= 1:
                    act.wait_ge(s_on, 2 * t)
                    squares_out(t - 1, 1)
                act_pieces(t - 1, k - 1)
            copy_pt(NU - 1)
            act.wait_ge(s_on, 2 * NT)
            squares_out(NT - 1, 1)
            for k in range(16):
                act_pieces(NT - 1, k)

            act.wait_ge(s_gx, 1)
            nc.scalar.activation(gex, gex, ACT.Exp).then_inc(s_gxe, 1)
            act.wait_ge(s_v12, 1)
            nc.scalar.activation(e12, e12, ACT.Exp).then_inc(s_v12e, 1)

            act.sem_inc(s_ya, 1)
            act.wait_ge(s_slot, 1)
            nb = act.value_load(ctl[0:1, NINFO:NINFO + 1], min_val=17, max_val=NBLOCK)

            def rows_t_out(b3, jj):
                act.wait_ge(s_bx, b3)
                nc.scalar.activation(xgt[:, jj, 0:4], bank(2).rearrange("p (g c) -> p g c", g=4), ACT.Copy).then_inc(s_xa, 1)

            rows_t_out(3, 0)
            with act.Fori(0, NBLOCK // 4) as i:
                for j in range(4):
                    b = i * 4 + j
                    with act.If(b < nb):
                        act.wait_ge(s_h, i * 8 + (2 * j + C_H))
                        for f in range(2):
                            act.wait_ge(s_gu, i * 8 + (2 * j + f + 1))
                            nc.scalar.activation(sil[:, f], bank(f, 0, P), ACT.Silu).then_inc(s_sil, 1)
                        rows_t_out(i * 4 + (j + 4), (j + 1) % 2)
                        act.wait_ge(s_ht, i * 4 + (j + 1))
                        nc.scalar.activation(hdt, bank(4, 0, 256).rearrange("p (f c) -> p f c", f=2), ACT.Copy).then_inc(s_hta, 1)
                        act.wait_ge(s_y, i * 4 + (j + 5))
                        act.wait_ge(s_ysc[j], i * 16 + 16)
                        nc.scalar.activation(yb[:, j, 0:512], bank(5), ACT.Copy).then_inc(s_ya, 1)

        @block.vector
        def _(dve):
            chain = Chain(dve, s_dve)
            link = chain.link
            dve.sem_inc(s_tev, 2)
            dve.wait_ge(s_const, 16 * 6)

            def norm_z(t5, tt, t1, j):
                dve.wait_ge(s_zev, t5 + 4 + 5)
                zj = z[:, j]
                zh = zj.rearrange("p (h c) -> p h c", c=HD)
                sqh = sq.rearrange("p (h c) -> p h c", c=HD)
                link(nc.vector.tensor_tensor(sq, zj, zj, ALU.mult))
                link(nc.vector.tensor_reduce(ss26, sqh, AXX, ALU.add))
                nc.vector.tensor_scalar(ss26, ss26, 1.0 / HD, None, ALU.mult).then_inc(s_ss26, 1)
                dve.wait_ge(s_rs26, t1)
                link(nc.vector.tensor_tensor(sqh, zh, rs26.unsqueeze(2).broadcast_to([P, 26, HD]), ALU.mult))
                for a, (h0, h1) in enumerate(((0, 8), (8, 10), (10, 18), (18, 26))):
                    ins = nc.vector.tensor_tensor(zh[:, h0:h1], sqh[:, h0:h1],
                                                  g64[:, a:a + 1, :].broadcast_to([P, h1 - h0, HD]), ALU.mult)
                link(ins)
                rp = rope[:, tt, :] if isinstance(tt, int) else rope[:, bass.ds(tt, 1), :].rearrange("p a c -> p (a c)")
                cos = rp[:, 0:8].unsqueeze(1).broadcast_to([P, 10, 8])
                sin = rp[:, 8:16].unsqueeze(1).broadcast_to([P, 10, 8])
                x1, x2 = zh[:, 0:10, 0:8], zh[:, 0:10, 8:16]
                tmp = sqh[:, 0:10]
                nc.vector.tensor_tensor(tmp[:, :, 0:8], x1, cos, ALU.mult)
                nc.vector.tensor_tensor(tmp[:, :, 8:16], x2, sin, ALU.mult)
                nc.vector.tensor_tensor(tmp[:, :, 16:24], x2, cos, ALU.mult)
                link(nc.vector.tensor_tensor(tmp[:, :, 24:32], x1, sin, ALU.mult))
                nc.vector.tensor_tensor(x1, tmp[:, :, 0:8], tmp[:, :, 8:16], ALU.subtract)
                nc.vector.tensor_tensor(x2, tmp[:, :, 16:24], tmp[:, :, 24:32], ALU.add).then_inc(s_zn, 1)

            def transposes_out(t4, tt, col):
                dve.wait_ge(s_tr, t4 + C_TR + 3)
                q = qt[:, tt, 4:8, :] if isinstance(tt, int) else qt[:, bass.ds(tt, 1), 4:8, :].rearrange("p a g c -> p (a g) c")
                nc.vector.tensor_scalar(q, bank(7).rearrange("p (g c) -> p g c", g=4), HD ** -0.5, None,
                                        ALU.mult).then_inc(s_tev, 1)
                dve.wait_ge(s_tr, t4 + C_TR + 4)
                nc.vector.tensor_copy(kta[:, bass.ds(col, P)], bank(4, 0, P)).then_inc(s_tev, 1)

            norm_z(0, 0, 1, 0)
            with dve.Fori(0, 4) as i:
                chain.enter(i, 10)
                for j in range(2):
                    dve.wait_ge(s_zn, i * 2 + (j + 1))
                    norm_z(i * 10 + 5 * (j + 1), i * 2 + (j + 1), i * 2 + (j + 2), 1 - j)
                    transposes_out(i * 8 + 4 * j, i * 2 + j, i * 256 + j * P)
                chain.leave(4)
            transposes_out(4 * (NT - 1), NT - 1, (NT - 1) * P)

            dve.wait_ge(s_bload, 16 * 7)
            nc.vector.tensor_tensor(bm, bm, maskb.unsqueeze(1).broadcast_to([P, HEADS, KW]), ALU.add).then_inc(s_bm, 1)
            dve.wait_ge(s_bm, 1)

            def copy_pt(u):
                _, _, _, _, tiles, _ = unit_info(u)
                cut = (len(tiles) + 1) // 2
                dve.wait_ge(s_pt, u + 1)
                if u >= 2:
                    dve.wait_ge(s_pv, u - 1)
                full = [x for x in tiles[:cut] if x[2] == P]
                assert len(full) == cut
                nc.vector.tensor_copy(pt[:, u % 2, 0:cut * P], bank(3, 0, cut * P)).then_inc(s_ptv, 1)

            def divide(t, m):
                dve.wait_ge(s_pv, 16 * t + 8 * (m + 1))
                s8 = psum_e[:, t % 2, 8 * m:8 * m + 8]
                r8 = rden[:, 8 * m:8 * m + 8]
                if m == 0:
                    dve.wait_ge(s_es, t + 1)
                    link(nc.vector.tensor_tensor(r8, s8, esink, ALU.add))
                    link(nc.vector.reciprocal(r8, r8))
                else:
                    link(nc.vector.reciprocal(r8, s8))
                nc.vector.tensor_tensor(row[:, t, 512 * m:512 * m + 512].rearrange("p (h c) -> p h c", c=HD),
                                        o_ps.rearrange("p (h c) -> p h c", c=HD),
                                        r8.unsqueeze(2).broadcast_to([P, 8, HD]), ALU.mult).then_inc(s_on, 1)

            def norm_out(t, m):
                dve.wait_ge(s_so, 2 * t + m + 1)
                part = row[:, t, 512 * m:512 * m + 512]
                nc.vector.scalar_tensor_tensor(part, part, rso[:, m:m + 1], g_o[:, 512 * m:512 * m + 512],
                                               ALU.mult, ALU.mult).then_inc(s_og, 1)

            def dve_pieces(t, k):
                if t < 0:
                    return
                if k == 2:
                    dve.wait_ge(s_t1, 2 * t + 2)
                    nc.vector.tensor_copy(ot[:, 4:8], bank(7).rearrange("p (g c) -> p g c", g=4)).then_inc(s_otv, 1)
                if k in (6, 8):
                    n = (k - 6) // 2
                    dve.wait_ge(s_op, 2 * t + n + 1)
                    if n == 0:
                        dve.wait_ge(s_xc[t % 2], 16 * (t // 2 + 1))
                    nc.vector.tensor_tensor(row[:, t, 512 * n:512 * n + 512], bank(6 + n),
                                            xc[:, t % 2, 512 * n:512 * n + 512], ALU.add).then_inc(s_x2, 1)
                if k == 10:
                    dve.wait_ge(s_s2, t + 1)
                    if t >= 2:
                        dve.wait_ge(s_h2o[t % 2], 16 * (t // 2))
                        dve.wait_ge(s_t2, 2 * (t - 1))
                    nc.vector.scalar_tensor_tensor(h2[:, t % 2], row[:, t], rs2, g2, ALU.mult, ALU.mult).then_inc(s_h2, 1)
                if k == 13:
                    dve.wait_ge(s_t2, 2 * t + 2)
                    nc.vector.tensor_copy(h2t[:, 4:8], bank(7).rearrange("p (g c) -> p g c", g=4)).then_inc(s_h2v, 1)
                if k == 14:
                    dve.wait_ge(s_r, t + 1)
                    nc.vector.tensor_tensor(logits[:, t], bank(6, 0, NR), rbias, ALU.add).then_inc(s_rv, 1)

            for u in range(NU):
                t, m, h, segs, tiles, width = unit_info(u)
                k = u % 16
                c = m * HEADS + h
                dve.wait_ge(s_qk, u + 1)
                if u >= 2:
                    dve.wait_ge(s_pt, u - 1)
                b0 = first_bias(t, m)
                at = scores_at(u, width)
                add = bm[:, h, b0:b0 + width] if m else maska[:, b0:b0 + width]
                link(nc.vector.tensor_tensor_reduce(
                    out=sp[:, u % 2, 0:width], in0=ps[:, at:at + width], in1=add, scale=1.0,
                    scalar=sinks[:, h:h + 1] if m == 0 else -3e38, op0=ALU.add, op1=ALU.max,
                    accum_out=mx[:, u % 2:u % 2 + 1]))
                nc.vector.tensor_scalar(negm[:, t % 2, c:c + 1], mx[:, u % 2:u % 2 + 1], -1.0, None,
                                        ALU.mult).then_inc(s_sp, 1)
                if u >= 1:
                    copy_pt(u - 1)
                if k == 7:
                    if t >= 1:
                        dve.wait_ge(s_on, 2 * t)
                    dve.wait_ge(s_sp, u + 1)
                    nc.vector.tensor_tensor(esink, sinks, negm[:, t % 2, 0:8], ALU.add).then_inc(s_nsk, 1)
                if k == 8:
                    divide(t, 0)
                if k == 9:
                    norm_out(t, 0)
                if k == 0 and t >= 1:
                    divide(t - 1, 1)
                if k == 1 and t >= 1:
                    norm_out(t - 1, 1)
                dve_pieces(t - 1, k - 1)
            copy_pt(NU - 1)
            divide(NT - 1, 1)
            norm_out(NT - 1, 1)
            for k in range(16):
                dve_pieces(NT - 1, k)

            dve.wait_ge(s_rload, 16 * 11)
            dve.wait_ge(s_rv, NT)
            dve.wait_ge(s_fill, 1)
            tt_, ts_, red = nc.vector.tensor_tensor, nc.vector.tensor_scalar, nc.vector.tensor_reduce
            gl = logits[:, :, 0:NG]
            el = logits[:, :, NG:NR]
            iota4 = c_iota[:, 0:NG].unsqueeze(1).broadcast_to([P, NT, NG])
            iota32 = c_iota.unsqueeze(1).broadcast_to([P, NT, NE])

            def wide(x, n):
                return x.broadcast_to([P, NT, n])

            def top_one(values, best, scratch, hot, iota, n):
                link(red(best, values, AXX, ALU.max))
                link(tt_(scratch, values, wide(best, n), ALU.is_lt))
                link(ts_(scratch, scratch, 1000.0, None, ALU.mult))
                link(tt_(scratch, scratch, iota, ALU.add))
                link(red(idx, scratch, AXX, ALU.min))
                link(tt_(hot, iota, wide(idx, n), ALU.is_equal))

            top_one(gl, gmx, geq, goh, iota4, NG)
            tt_(gex, gl, wide(gmx, NG), ALU.subtract).then_inc(s_gx, 1)
            link(ts_(geq, goh, BIG, -BIG, ALU.mult, ALU.add))
            e4 = el.rearrange("p t (g e) -> p t g e", g=NG)
            m4 = m32.rearrange("p t (g e) -> p t g e", g=NG)
            for g in range(NG):
                ins = tt_(m4[:, :, g], e4[:, :, g], wide(goh[:, :, g:g + 1], 8), ALU.mult)
            link(ins)
            for g in range(NG):
                ins = tt_(m4[:, :, g], m4[:, :, g], wide(geq[:, :, g:g + 1], 8), ALU.add)
            link(ins)
            top_one(m32, v1, eq, oh1, iota32, NE)
            link(ts_(m2, oh1, -2 * BIG, None, ALU.mult))
            link(tt_(m2, m2, m32, ALU.add))
            top_one(m2, v2, eq, oh2, iota32, NE)
            tt_(e12, v2, v1, ALU.subtract).then_inc(s_v12, 1)
            link(tt_(eq, oh1, oh2, ALU.add))
            tt_(mb, eq, wide(c_valid.unsqueeze(2), NE), ALU.mult).then_inc(s_mb, 1)
            dve.wait_ge(s_gxe, 1)
            link(red(gsum, gex, AXX, ALU.add))
            link(nc.vector.reciprocal(gp, gsum))
            dve.wait_ge(s_v12e, 1)
            link(ts_(v1, e12, 1.0, None, ALU.add))
            link(nc.vector.reciprocal(v1, v1))
            link(tt_(v1, v1, gp, ALU.mult))
            link(tt_(v2, v1, e12, ALU.mult))
            lf = load4.bitcast(F32)
            link(nc.vector.tensor_copy(lf[:, :, 0, 2:3], v1))
            link(nc.vector.tensor_copy(lf[:, :, 1, 2:3], v2))
            link(nc.vector.tensor_copy(load4[:, :, :, 0:1], c_token.unsqueeze(3)))
            link(nc.vector.tensor_copy(load4[:, :, :, 1:2], c_dest.unsqueeze(3)))
            link(nc.vector.memset(load4[:, :, :, 3:4], 0))
            dve.wait_ge(s_cum, 1)
            link(nc.vector.tensor_copy(cntv, ps[:, NT * NE:NT * NE + NE]))
            link(tt_(cmp9, cntv.unsqueeze(2).broadcast_to([P, NE, 9]),
                     c_steps.unsqueeze(1).broadcast_to([P, NE, 9]), ALU.is_gt))
            link(red(nblk, cmp9, AXX, ALU.add))
            link(tt_(prod, c_tri32, nblk.unsqueeze(1).broadcast_to([P, NE, NE]), ALU.mult))
            link(red(excl, prod, AXX, ALU.add))
            link(tt_(incl, excl, nblk, ALU.add))
            link(ts_(basev, excl, float(P), None, ALU.mult))
            pos = ps[:, 0:NT * NE].rearrange("p (t c) -> p t c", t=NT)
            link(tt_(m32, pos, basev.unsqueeze(1).broadcast_to([P, NT, NE]), ALU.add))
            for k, oh in enumerate((oh1, oh2)):
                link(tt_(eq, oh, m32, ALU.mult))
                link(red(slots[:, :, k:k + 1], eq, AXX, ALU.add))
                link(tt_(slots[:, :, k:k + 1], slots[:, :, k:k + 1], c_far.unsqueeze(2), ALU.add))
            link(nc.vector.tensor_copy(sloti, slots))
            link(tt_(cmpb, incl.unsqueeze(1).broadcast_to([P, NINFO, NE]),
                     c_block.unsqueeze(2).broadcast_to([P, NINFO, NE]), ALU.is_le))
            link(red(ctlf[:, 0:NINFO], cmpb, AXX, ALU.add))
            link(ts_(ctlf[:, 0:NINFO], ctlf[:, 0:NINFO], NE - 1.0, None, ALU.min))
            link(nc.vector.tensor_copy(ctlf[:, NINFO:NINFO + 1], incl[:, NE - 1:NE]))
            link(tt_(cmpt, c_turn, incl[:, NE - 1:NE].unsqueeze(1).broadcast_to([P, 4, 12]), ALU.is_lt))
            link(red(ctlf[:, NINFO + 1:NINFO + 5], cmpt, AXX, ALU.add))
            link(ts_(ctlf[:, NINFO + 1:NINFO + 5], ctlf[:, NINFO + 1:NINFO + 5], 16.0, 16.0, ALU.mult, ALU.add))
            nc.vector.tensor_copy(ctl[:, 0:NINFO + 5], ctlf[:, 0:NINFO + 5]).then_inc(s_slot, 1)

            dve.sem_inc(s_yv, 1)
            dve.sem_inc(s_h, C_H)
            dve.wait_ge(s_slot, 1)
            nb = dve.value_load(ctl[0:1, NINFO:NINFO + 1], min_val=17, max_val=NBLOCK)
            for j in range(4):
                dve.wait_ge(s_ysc[j], 16)
            inf = info.bitcast(F32)

            def rows_t_out(b3, jj):
                dve.wait_ge(s_bx, b3)
                nc.vector.tensor_copy(xgt[:, jj, 4:8], bank(3).rearrange("p (g c) -> p g c", g=4)).then_inc(s_xv, 1)

            rows_t_out(3, 0)
            with dve.Fori(0, NBLOCK // 4) as i:
                for j in range(4):
                    b = i * 4 + j
                    with dve.If(b < nb):
                        gate = inf[:, bass.ds(b, 1), 2:3].rearrange("p a b -> p (a b)")
                        for f in range(2):
                            dve.wait_ge(s_sil, i * 8 + (2 * j + f + 1))
                            nc.vector.scalar_tensor_tensor(hd[:, f], bank(f, P, 2 * P), gate,
                                                           sil[:, f], ALU.mult, ALU.mult).then_inc(s_h, 1)
                        rows_t_out(i * 4 + (j + 4), (j + 1) % 2)
                        dve.wait_ge(s_y, i * 4 + (j + 5))
                        dve.wait_ge(s_ysc[j], i * 16 + 16)
                        nc.vector.tensor_copy(yb[:, j, 512:1024], bank(6)).then_inc(s_yv, 1)

            dve.wait_ge(s_ydone, 1)
            for t in range(NT):
                j, n = t % 2, P if t < NT - 1 else DEC
                dve.wait_ge(s_ye[j], 32 * (t // 2 + 1))
                link(nc.vector.tensor_tensor(row[0:n, t], row[0:n, t], ye[0:n, j, 0], ALU.add))
                nc.vector.tensor_tensor(row[0:n, t], row[0:n, t], ye[0:n, j, 1], ALU.add).then_inc(s_fin, 1)

        @block.tensor
        def _(pe):
            mm = nc.tensor.matmul
            pe.sem_inc(s_z, 1)
            pe.sem_inc(s_tr, C_TR)

            def project(t5, t1, j, first=False):
                pe.wait_ge(s_xg, t1)
                for c in range(5):
                    if first:
                        pe.wait_ge(s_win[c], 16)
                    pe.wait_ge(s_zev, t5 + {1: 5, 4: 7}.get(c, c + 1))
                    for k in range(KD):
                        a = CHUNK_AT[c] + k * CHUNK[c]
                        ins = mm(bank(Z_BANK[c], 0, CHUNK[c]), xt[:, j, k, :], w_in[:, a:a + CHUNK[c]],
                                 start=(k == 0), stop=(k == KD - 1))
                    ins.then_inc(s_z, 1)

            def transposes(t2, t1, j):
                pe.wait_ge(s_zn, t1)
                for c0, n, bk, at, freed, v in ((0, 4, 5, 0, s_tea, 1), (1152, 4, 6, 0, s_tea, 2),
                                                (640, 4, 7, 0, s_tev, 1), (512, 1, 4, 0, s_tev, 2)):
                    pe.wait_ge(freed, t2 + v)
                    for g in range(n):
                        ins = nc.tensor.transpose(bank(bk, at + g * P, at + g * P + P), z[:, j, c0 + g * P:c0 + g * P + P], ident)
                    ins.then_inc(s_tr, 1)

            project(0, 1, 0, first=True)
            pe.wait_ge(s_const, 16 * 6)
            with pe.Fori(0, 4) as i:
                for j in range(2):
                    project(i * 10 + 5 * (j + 1), i * 2 + (j + 2), 1 - j)
                    transposes(i * 4 + 2 * j, i * 2 + (j + 1), j)
            transposes(2 * (NT - 1), NT, 0)

            def scores(u):
                if u >= NU:
                    return
                t, m, h, segs, tiles, width = unit_info(u)
                if u >= 2:
                    pe.wait_ge(s_sp, u - 1)
                half, g = (h // 4, h % 4) if m == 0 else (h % 2, 4 + h // 2)
                a = half * HD
                q = qt[a:a + HD, t, g, :]
                kt = kta[a:a + HD] if m == 0 else ktb[a:a + HD, g - 4]
                out0 = scores_at(u, width)
                c, runs = 0, []
                for col, n in segs:
                    k = 0
                    while k < n:
                        at = out0 + c + k
                        step = min(n - k, 512 - at % 512)
                        runs.append((at, step, col + k))
                        k += step
                    c += n
                for at, step, col in sorted(runs, key=lambda r: r[0] // 512 == 1):
                    if at // 512 == 1 and u >= 1:
                        pe.wait_ge(s_sp, u)
                    ins = mm(ps[:, at:at + step], q, kt[:, col:col + step], start=True, stop=True)
                ins.then_inc(s_qk, 1)

            def transpose_probs(u):
                t, m, h, segs, tiles, width = unit_info(u)
                pe.wait_ge(s_p, u + 1)
                if u >= 1:
                    pe.wait_ge(s_ptv, u)
                    pe.wait_ge(s_pta, u)
                cut = (len(tiles) + 1) // 2
                for i, (c, _, n) in enumerate(tiles):
                    dst = bank(3, i * P, i * P + P) if i < cut else bank(4, (i - cut) * P, (i - cut) * P + P)
                    ins = nc.tensor.transpose(dst[0:n], sp[:, u % 2, c:c + n], ident)
                ins.then_inc(s_pt, 1)

            def values(u):
                t, m, h, segs, tiles, width = unit_info(u)
                pe.wait_ge(s_ptv, u + 1)
                pe.wait_ge(s_pta, u + 1)
                if h == 0 and u >= 1:
                    pe.wait_ge(s_on, 2 * t + m)
                for i, (c, vt, n) in enumerate(tiles):
                    v = va[0:n, vt, (h // 4) * HD:(h // 4 + 1) * HD] if m == 0 else vb[0:n, vt, h * HD:(h + 1) * HD]
                    ins = mm(o_ps[:, h * HD:(h + 1) * HD], pt[0:n, u % 2, i * P:i * P + P], v,
                             start=(i == 0), stop=(i == len(tiles) - 1))
                ins.then_inc(s_pv, 1)

            def pe_pieces(t, k):
                if t < 0:
                    return
                if k == 1:
                    pe.wait_ge(s_og, 2 * (t + 1))
                    if t >= 1:
                        pe.wait_ge(s_rv, t)
                    for g in range(8):
                        ins = nc.tensor.transpose(bank(6 + g // 4, g % 4 * P, g % 4 * P + P), row[:, t, g * P:g * P + P], ident)
                        if g % 4 == 3:
                            ins.then_inc(s_t1, 1)
                if k in (3, 4, 6, 7):
                    n, half = (k - 3) // 3, (k - 3) % 3
                    if k == 3:
                        pe.wait_ge(s_ota, t + 1)
                        pe.wait_ge(s_otv, t + 1)
                    for g in range(4 * half, 4 * half + 4):
                        ins = mm(bank(6 + n), ot[:, g], w_out[:, g, 512 * n:512 * n + 512], start=(g == 0), stop=(g == 7))
                    if half:
                        ins.then_inc(s_op, 1)
                if k == 12:
                    pe.wait_ge(s_h2, t + 1)
                    for g in range(8):
                        ins = nc.tensor.transpose(bank(6 + g // 4, g % 4 * P, g % 4 * P + P), h2[:, t % 2, g * P:g * P + P], ident)
                        if g % 4 == 3:
                            ins.then_inc(s_t2, 1)
                if k == 14:
                    pe.wait_ge(s_h2a, t + 1)
                    pe.wait_ge(s_h2v, t + 1)
                    for g in range(8):
                        ins = mm(bank(6, 0, NR), h2t[:, g], wr[:, g], start=(g == 0), stop=(g == 7))
                    ins.then_inc(s_r, 1)

            pe.wait_ge(s_cache, 16 * 4)
            pe.wait_ge(s_bload, 16 * 7)
            pe.wait_ge(s_tea, 2 + 2 * NT)
            pe.wait_ge(s_tev, 2 + 2 * NT)
            scores(0)
            for u in range(NU):
                scores(u + 1)
                transpose_probs(u)
                if u >= 1:
                    values(u - 1)
                pe_pieces(units[u][0] - 1, u % 16 - 1)
                if u % 16 == 15:
                    pe_pieces(units[u][0] - 1, 15)
            values(NU - 1)
            for k in range(16):
                pe_pieces(NT - 1, k)

            pe.wait_ge(s_mb, 1)
            pe.wait_ge(s_rv, NT)
            for t in range(NT):
                for s in range(t + 1):
                    mm(ps[:, t * NE:t * NE + NE], tri if s == t else ones, mb[:, s], start=(s == 0), stop=(s == t))
            for s in range(NT):
                ins = mm(ps[:, NT * NE:NT * NE + NE], ones, mb[:, s], start=(s == 0), stop=(s == NT - 1))
            ins.then_inc(s_cum, 1)

            pe.sem_inc(s_y, 4)
            pe.sem_inc(s_bx, 2)
            pe.wait_ge(s_slot, 1)
            nb = pe.value_load(ctl[0:1, NINFO:NINFO + 1], min_val=17, max_val=NBLOCK)

            def rows_t(wait, jj):
                pe.wait_ge(s_g[jj], wait)
                for g in range(8):
                    ins = nc.tensor.transpose(bank(2 + g // 4, g % 4 * P, g % 4 * P + P), xg[:, jj, g * P:g * P + P], ident)
                ins.then_inc(s_bx, 1)

            rows_t(16, 0)
            with pe.Fori(0, NBLOCK // 4) as i:
                for j in range(4):
                    b = i * 4 + j
                    with pe.If(b < nb):
                        w = wx[:, j]
                        pe.wait_ge(s_w[j], i * 16 + 16)
                        pe.wait_ge(s_xa, i * 4 + (j + 1))
                        pe.wait_ge(s_xv, i * 4 + (j + 1))
                        pe.wait_ge(s_h, i * 8 + (2 * j + C_H))
                        for f in range(2):
                            for k in range(KD):
                                a = (f * KD + k) * FF
                                ins = mm(bank(f, 0, FF), xgt[:, j % 2, k], w[:, a:a + FF],
                                         start=(k == 0), stop=(k == KD - 1))
                            ins.then_inc(s_gu, 1)
                        rows_t(i * 16 + (32 if j == 3 else 16), (j + 1) % 4)
                        pe.wait_ge(s_h, i * 8 + (2 * j + 2 + C_H))
                        for f in range(2):
                            ins = nc.tensor.transpose(bank(4, f * P, f * P + P), hd[:, f], ident)
                        ins.then_inc(s_ht, 1)
                        pe.wait_ge(s_hta, i * 4 + (j + 1))
                        pe.wait_ge(s_ya, i * 4 + (j + 1))
                        pe.wait_ge(s_yv, i * 4 + (j + 1))
                        for n in range(2):
                            for f in range(2):
                                a = 2 * KD * FF + f * D + n * 512
                                ins = mm(bank(5 + n), hdt[:, f], w[:, a:a + 512], start=(f == 0), stop=(f == 1))
                        ins.then_inc(s_y, 1)


INS = ["xT", "x", "w_in", "g1", "ident", "g64", "rope", "sinks", "rbias", "ckb", "cka", "cvb", "cva", "bias", "maskb",
       "maska", "g_o", "w_out", "g2", "wr", "tri32", "steps", "block", "turn", "iota", "valid", "far", "token", "dest",
       "tri", "ones", "wexp"]
OUTS = {"y_p": [SEQ, D], "y_s": [DEC, D], "ka_p": [P, P], "va_p": [P, P], "kb_p": [P, 4, 512], "vb_p": [P, 4, 512],
        "ka_s": [P, DEC], "va_s": [DEC, P], "kb_s": [P, 4, DEC], "vb_s": [DEC, 512]}


def kernel(**inputs):
    import ml_dtypes
    import concourse.bacc as bacc
    from concourse.bass_utils import run_bass_kernel_spmd

    a = {k: np.asarray(v) for k, v in inputs.items()}
    f32 = np.float32
    L = {}
    x = np.zeros((ROWS, D), f32)
    x[:SEQ] = a["x_prompt"][0]
    x[SEQ:SEQ + DEC] = a["x_sample"][0]
    L["x"] = x.reshape(NT, P, D)
    L["xT"] = np.ascontiguousarray(L["x"].reshape(NT, P, KD, P).transpose(0, 3, 2, 1))
    w = a["w_in"][0]
    pair = [p + 4 * s for p in range(4) for s in range(2)]
    wqa = w[:, 0:512].reshape(D, 8, HD)[:, pair].reshape(D, 512)
    parts = [wqa, w[:, 512:768], w[:, 768:1280], w[:, 1280:1792], w[:, 1792:2304]]
    L["w_in"] = np.concatenate([c.reshape(KD, P, -1).transpose(1, 0, 2).reshape(P, -1) for c in parts], axis=1)
    L["g1"] = a["norm1"][0].reshape(KD, P).T
    L["ident"] = np.eye(P, dtype=f32)
    L["g64"] = np.stack([a["q_norm_a"][0], a["k_norm_a"][0], a["q_norm_b"][0], a["k_norm_b"][0]])
    inv = f32(500000.0) ** (-np.arange(8, dtype=f32) / f32(8))
    pos = np.zeros(ROWS, f32)
    pos[:SEQ] = np.arange(SEQ)
    pos[SEQ:SEQ + DEC] = 256 + np.arange(DEC)
    ang = (pos[:, None] * inv[None, :]).astype(f32)
    L["rope"] = np.concatenate([np.cos(ang), np.sin(ang)], axis=1).astype(f32).reshape(NT, P, 16).transpose(1, 0, 2)
    L["sinks"] = a["sinks_a"][0]
    L["rbias"] = np.concatenate([a["b_router_group"][0], a["b_router_expert"][0].reshape(-1)])
    L["ckb"] = a["cache_b_k"][0, 0].reshape(CACHE_B, 4, P).transpose(2, 1, 0)
    L["cka"] = a["cache_a_k"][0, 0].reshape(CACHE_A, P).T
    L["cvb"] = a["cache_b_v"][0, 0].reshape(2, P, 512).transpose(1, 0, 2)
    L["cva"] = a["cache_a_v"][0, 0].reshape(P, P)
    dist = np.clip(np.arange(KW)[None, :] - 4 * P - np.arange(P)[:, None], -128, 128) + 128
    L["bias"] = a["rel_bias_b"][0][:, dist].transpose(1, 0, 2)
    late_q = (np.arange(P) >= 64)[:, None]
    old = late_q & (np.arange(P) < 64)[None, :]
    new = ~late_q & (np.arange(P) >= 64)[None, :]
    none = np.zeros((P, 3 * P), bool)
    L["maskb"] = np.where(np.concatenate([old, none, new], axis=1), f32(-BIG), f32(0))
    L["maska"] = np.where(np.concatenate([old, new], axis=1), f32(-BIG), f32(0))
    L["g_o"] = np.concatenate([a["out_norm_a"][0], a["out_norm_b"][0]])
    L["w_out"] = a["w_out"][0].reshape(KD, P, D).transpose(1, 0, 2)
    L["g2"] = a["norm2"][0]
    wr = np.concatenate([a["w_router_group"][0]] + [a["w_router_expert"][0, g] for g in range(NG)], axis=1)
    L["wr"] = wr.reshape(KD, P, NR).transpose(1, 0, 2)
    L["tri32"] = np.tril(np.ones((NE, NE), f32), -1)
    L["steps"] = np.arange(9, dtype=f32) * P
    L["block"] = np.arange(NINFO, dtype=f32)
    L["turn"] = (np.arange(12)[None, :] * 4 + np.arange(4)[:, None]).astype(f32)
    L["iota"] = np.arange(NE, dtype=f32)
    tok = np.arange(NT)[None, :] * P + np.arange(P)[:, None]
    real = tok < SEQ + DEC
    L["valid"] = real.astype(f32)
    L["far"] = np.where(real, 0, FAR).astype(f32)
    L["token"] = np.stack([tok, tok], axis=2).astype(f32)
    L["dest"] = np.stack([tok, tok + ROWS], axis=2).astype(f32)
    L["tri"] = np.triu(np.ones((P, P), f32), 1).astype(ml_dtypes.bfloat16)
    L["ones"] = np.ones((P, P), ml_dtypes.bfloat16)
    gu = [a[n][0].reshape(NE, KD, P, 2, P) for n in ("w_gate", "w_up")]
    gu = np.stack(gu, axis=4).transpose(0, 2, 3, 1, 4, 5).reshape(NE, P, -1)
    dn = a["w_down"][0].reshape(NE, 2, P, D).transpose(0, 2, 1, 3).reshape(NE, P, -1)
    L["wexp"] = np.concatenate([gu, dn], axis=2)

    nc = bacc.Bacc("TRN2", target_bir_lowering=False, num_devices=1)
    arrays, d, o = {}, {}, {}
    for name in INS:
        arr = np.ascontiguousarray(L[name])
        arrays["in_" + name] = arr
        d[name] = nc.dram_tensor("in_" + name, arr.shape, mybir.dt.from_np(arr.dtype), kind="ExternalInput").ap()
    for name, shape in OUTS.items():
        o[name] = nc.dram_tensor("out_" + name, shape, F32, kind="ExternalOutput").ap()
    build(nc, d, o)
    res = run_bass_kernel_spmd(nc, [arrays], core_ids=[0]).results[0]
    r = {name: np.asarray(res["out_" + name]).reshape(shape) for name, shape in OUTS.items()}

    def keys_b(k, n):
        return np.ascontiguousarray(k.transpose(2, 1, 0)).reshape(1, 1, n, 8, HD)

    return (r["y_p"][None], r["y_s"][None],
            np.ascontiguousarray(r["ka_p"].T).reshape(1, 1, P, 2, HD), r["va_p"].reshape(1, 1, P, 2, HD),
            keys_b(r["kb_p"], 512), np.ascontiguousarray(r["vb_p"].transpose(1, 0, 2)).reshape(1, 1, 512, 8, HD),
            np.ascontiguousarray(r["ka_s"].T).reshape(1, 1, DEC, 2, HD), r["va_s"].reshape(1, 1, DEC, 2, HD),
            keys_b(r["kb_s"], DEC), r["vb_s"].reshape(1, 1, DEC, 8, HD))
```

```python
import numpy as np
import concourse.bass as bass
from concourse import mybir
from contextlib import ExitStack

F32 = mybir.dt.float32
BF16 = mybir.dt.bfloat16
I32 = mybir.dt.int32
ALU = mybir.AluOpType
ACT = mybir.ActivationFunctionType
AXX = mybir.AxisListType.X

D = 1024
P = 128
KD = D // P
SEQ, DEC = 1024, 32
NT = SEQ // P + 1
ROWS = NT * P
HD = 64
HEADS = 8
CACHE_A, CACHE_B = 128, 256
EPS = 1e-6
NG, NE, FF = 4, 32, 256
NR = NG + NE
NBLOCK = 48
NINFO = NBLOCK + 3
KW = 5 * P
EW = 2 * KD * FF + 2 * D
W_PART = ((0, KD * FF), (KD * FF, 2 * KD * FF), (2 * KD * FF, EW))
FAR = 1 << 20
BIG = 1e30

CHUNK = (512, 256, 512, 512, 512)
Z_BANK = (0, 1, 2, 3, 1)
CHUNK_AT = (0, 4096, 6144, 10240, 14336)


class Chain:

    def __init__(self, eng, sem):
        self.eng, self.sem, self.base, self.k, self.i, self.per = eng, sem, 0, 0, None, 0

    def enter(self, i, per):
        self.i, self.per, self.k, self.base = i, per, 0, self.base + self.k

    def leave(self, times):
        assert self.k == self.per, (self.k, self.per)
        self.base, self.k, self.i = self.base + times * self.per, 0, None

    def link(self, ins):
        ins.then_inc(self.sem, 1)
        self.k += 1
        v = self.base + self.k
        v = v if self.i is None else self.i * self.per + v
        self.eng.wait_ge(self.sem, v)


def tile_keys(t):
    if t == NT - 1:
        return ([(ROWS, CACHE_A), (SEQ, DEC)], [(ROWS, CACHE_B), (SEQ, DEC)])
    a, b = max(0, t - 1), max(0, t - 4)
    return ([(a * P, (t + 1 - a) * P)], [(b * P, (t + 1 - b) * P)])


def build(nc, d, o):
    ctx = ExitStack()
    with ctx:
        def sem(name):
            return ctx.enter_context(nc.semaphore(name))

        arena = ctx.enter_context(nc.sbuf_tensor("arena", [P, 52700], F32))
        ps = ctx.enter_context(nc.psum_tensor("ps", [P, 8 * 512], F32))
        top = [0]

        def place(n, at=None):
            a = top[0] if at is None else at
            if at is None:
                top[0] += n
            assert a + n <= 52700, (a, n)
            return arena[:, a:a + n]

        ident = place(P)
        g1 = place(KD)
        g64 = place(4 * HD).rearrange("p (a d) -> p a d", d=HD)
        rope = place(NT * 16).rearrange("p (t c) -> p t c", c=16)
        sinks = place(HEADS)
        rbias = place(NR)
        logits = place(NT * NR).rearrange("p (t c) -> p t c", c=NR)
        ssx, rsx = place(2), place(2)
        eps = place(1)
        ss26, rs26 = place(26), place(26)
        negm = place(2 * 16).rearrange("p (b c) -> p b c", b=2)
        mx = place(2)
        psum_e = place(2 * 16).rearrange("p (b c) -> p b c", b=2)
        esink = place(HEADS)
        rden = place(16)
        sso, rso = place(2), place(2)
        ss2, rs2 = place(1), place(1)
        ctl = place(64).bitcast(I32)
        slot_token = place(NINFO).bitcast(I32)
        slot_weight = place(NINFO)
        gidx = place(4).bitcast(I32)
        sidx = place(2).bitcast(I32)
        qt = place(NT * D).rearrange("p (t g c) -> p t g c", t=NT, g=8)
        row = qt.rearrange("p t g c -> p t (g c)")
        free_from = top[0]
        KC = ROWS + CACHE_B
        ktb = place(4 * KC).rearrange("p (g c) -> p g c", g=4)
        KCA = ROWS + CACHE_A
        kta = place(KCA)
        vb = place((NT + 2) * 512).rearrange("p (t c) -> p t c", t=NT + 2)
        va = place((NT + 1) * P).rearrange("p (t c) -> p t c", t=NT + 1)
        region = top[0]
        w_in = place(KD * sum(CHUNK))
        xt = place(2 * D).rearrange("p (b k c) -> p b k c", b=2, k=KD)
        xr = place(2 * D).rearrange("p (b c) -> p b c", b=2)
        z = place(2 * 1664).rearrange("p (b c) -> p b c", b=2)
        sq = place(1664)
        top[0] = region
        bm = place(HEADS * KW).rearrange("p (h c) -> p h c", h=HEADS)
        maskb = place(KW)
        maska = place(2 * P)
        w_out = place(KD * D).rearrange("p (k c) -> p k c", k=KD)
        sp = place(3 * KW).rearrange("p (b c) -> p b c", b=3)
        pt = place(2 * KW).rearrange("p (b c) -> p b c", b=2)
        ot = place(D).rearrange("p (k c) -> p k c", k=KD)
        h2 = place(2 * D).rearrange("p (b c) -> p b c", b=2)
        h2t = place(D).rearrange("p (k c) -> p k c", k=KD)
        xc = place(2 * D).rearrange("p (b c) -> p b c", b=2)
        g_o = place(D)
        g2 = place(D)
        wr = place(KD * NR).rearrange("p (k c) -> p k c", k=KD)
        junk = place(D)
        top[0] = free_from
        c_tri32 = place(NE * NE).rearrange("p (a b) -> p a b", a=NE)
        c_steps = place(9)
        c_block = place(NINFO)
        c_iota = place(NE)
        c_valid = place(NT)
        c_far = place(NT)
        c_token = place(NT * 2).rearrange("p (t k) -> p t k", k=2)
        c_row = place(P)
        tri = place(64).bitcast(BF16)
        ones = place(64).bitcast(BF16)

        def rt(n):
            return place(NT * n).rearrange("p (t c) -> p t c", t=NT)
        gmx, gsum, gp, idx, v1, v2, e12, ww = (rt(1) for _ in range(8))
        geq, goh, gex = rt(NG), rt(NG), rt(NG)
        m32, eq, oh1, oh2, m2 = (rt(NE) for _ in range(5))
        mb = place(NT * NE // 2).bitcast(BF16).rearrange("p (t c) -> p t c", t=NT)
        cntv = place(NE)
        cmp9 = place(NE * 9).rearrange("p (a b) -> p a b", b=9)
        nblk, excl, incl, basev = place(NE), place(NE), place(NE), place(NE)
        prod = place(NE * NE).rearrange("p (a b) -> p a b", a=NE)
        cmpb = place(NINFO * NE).rearrange("p (a b) -> p a b", b=NE)
        ctlf = place(64)
        slots = place(NT * 2).rearrange("p (t k) -> p t k", k=2)
        sloti = place(NT * 2).bitcast(I32).rearrange("p (t k) -> p t k", k=2)
        slotr = place(NT * 2).bitcast(I32).rearrange("p (t k) -> p t k", k=2)
        slotb = place(NT * 2).bitcast(I32).rearrange("p (t k) -> p t k", k=2)
        slotrf = place(NT * 2).rearrange("p (t k) -> p t k", k=2)
        slotbf = place(NT * 2).rearrange("p (t k) -> p t k", k=2)
        in_row = place(4 * P).rearrange("p (b c) -> p b c", b=4)
        in_block = place(4 * 2 * NINFO).rearrange("p (b a c) -> p b a c", b=4, a=2)
        rtop = top[0]
        assert rtop <= region
        dtop = [free_from]

        def dplace(n):
            dtop[0] += n
            return place(n, dtop[0] - n)
        wx = [dplace(EW) for _ in range(4)][::-1]
        assert rtop <= free_from + 2 * EW
        xg = dplace(4 * D).rearrange("p (b c) -> p b c", b=4)
        xgt = dplace(2 * D).rearrange("p (b k c) -> p b k c", b=2, k=KD)
        yb = dplace(4 * D).rearrange("p (b c) -> p b c", b=4)
        sil = dplace(FF).rearrange("p (b c) -> p b c", b=2)
        hd = dplace(FF).rearrange("p (b c) -> p b c", b=2)
        hdt = dplace(FF).rearrange("p (b c) -> p b c", b=2)

        def bank(n, a=0, b=512):
            return ps[:, n * 512 + a:n * 512 + b]
        o_ps = bank(5)

        def scores_at(u, width):
            return 0 if u % 2 == 0 else (1024 if width <= 512 else 1024 + 512 - KW)

        h2d = nc.dram_tensor("h2_rows", [ROWS, D], F32).ap()

        s_const = sem("constants_loaded")
        s_win = [sem(f"w_in{c}_loaded") for c in range(5)]
        s_xt = [sem(f"xt{j}_loaded") for j in range(2)]
        s_xr = [sem(f"xrow{j}_loaded") for j in range(2)]
        s_cache = sem("caches_loaded")
        s_maska = sem("mask_a_loaded")
        s_bload = sem("bias_and_mask_b_loaded")
        s_cload = sem("stage_c_weights_loaded")
        s_xc = [sem(f"residual{j}_loaded") for j in range(2)]
        s_rload = sem("routing_constants_loaded")
        s_xg = sem("xt_scaled")
        s_eps = sem("eps_ready")
        s_ss26 = sem("head_squares_summed")
        s_rs26 = sem("head_rstd_ready")
        s_ssx = sem("x_squares_summed")
        s_rsx = sem("x_rstd_ready")
        s_z = sem("z_chunks_made")
        s_zev = sem("z_chunks_copied")
        s_zn = sem("z_normed")
        s_tr = sem("z_transposed")
        s_tea = sem("transposes_copied_by_act")
        s_tev = sem("transposes_copied_by_dve")
        s_bm = sem("bias_masked")
        s_qk = sem("scores_made")
        s_sp = sem("scores_biased")
        s_p = sem("probs_ready")
        s_pt = sem("probs_transposed")
        s_ptv = sem("probs_t_copied_by_dve")
        s_pta = sem("probs_t_copied_by_act")
        s_pv = sem("heads_summed")
        s_es = sem("sinks_exp")
        s_nsk = sem("sinks_shifted")
        s_on = sem("mixer_out_divided")
        s_so = sem("mixer_squares_summed")
        s_og = sem("mixer_out_normed")
        s_t1 = sem("mixer_out_transposed")
        s_ota = sem("ot_copied_by_act")
        s_otv = sem("ot_copied_by_dve")
        s_op = sem("out_projected")
        s_x2 = sem("residual_added")
        s_s2 = sem("residual_squares_summed")
        s_h2 = sem("h2_ready")
        s_h2o = [sem(f"h2_stored{j}") for j in range(2)]
        s_t2 = sem("h2_transposed")
        s_h2a = sem("h2t_copied_by_act")
        s_h2v = sem("h2t_copied_by_dve")
        s_r = sem("logits_made")
        s_rv = sem("logits_copied")
        s_gx = sem("group_shifted")
        s_gxe = sem("group_exp")
        s_v12 = sem("top2_difference")
        s_v12e = sem("top2_exp")
        s_mb = sem("membership_ready")
        s_cum = sem("positions_counted")
        s_ctl = sem("block_experts_ready")
        s_in = sem("slot_masks_made")
        s_inv = sem("slot_masks_used")
        s_slot = sem("slot_tables_ready")
        s_x2o = sem("residual_stored")
        s_w = [[sem(f"expert{j}_{part}_loaded") for part in ("half0", "half1", "down")] for j in range(4)]
        s_g = [sem(f"rows_gathered{j}") for j in range(4)]
        s_gi = sem("indices_copied")
        s_xgz = sem("gather_buffers_cleared")
        s_bx = sem("rows_transposed")
        s_xa = sem("rows_t_copied_by_act")
        s_xv = sem("rows_t_copied_by_dve")
        s_gu = sem("gate_up_made")
        s_sil = sem("silu_ready")
        s_h = sem("hidden_ready")
        s_ht = sem("hidden_transposed")
        s_hta = sem("hidden_t_copied")
        s_y = sem("expert_out_made")
        s_ya = sem("expert_out_copied_by_act")
        s_yv = sem("expert_out_copied_by_dve")
        s_add = sem("expert_out_added")
        s_kv = sem("states_stored")
        s_dve = sem("dve_own")
        s_act = sem("act_own")
        s_pool = sem("pool_own")

        C_TR, C_H = 5, 3

        units = [(t, m, h) for t in range(NT) for m in (0, 1) for h in range(HEADS)]
        NU = len(units)

        def unit_info(u):
            t, m, h = units[u]
            segs = tile_keys(t)[m]
            tiles, c = [], 0
            for col, n in segs:
                for k in range(0, n, P):
                    tiles.append((c + k, (col + k) // P, min(P, n - k)))
                c += n
            return t, m, h, segs, tiles, c

        def first_bias(t, m):
            if t == NT - 1:
                return 0 if m == 0 else 2 * P
            return ((1 - min(t, 1)) if m == 0 else (4 - min(t, 4))) * P

        def pieces(do, u):
            for t in (u // 16 - 2, u // 16 - 1):
                if 0 <= t < NT:
                    do(t, u - 16 * (t + 1))

        block = ctx.enter_context(nc.Block())

        @block.sync
        def _(sp_):
            def load_x(t, j):
                sp_.dma_start(xt[:, j], d["xT"][t]).then_inc(s_xt[j], 16)
                sp_.dma_start(xr[:, j], d["x"][t]).then_inc(s_xr[j], 16)

            load_x(0, 0)
            with sp_.Fori(0, 4) as i:
                for j in range(2):
                    t = i * 2 + j
                    sp_.wait_ge(s_z, i * 10 + (5 * j + 1))
                    sp_.wait_ge(s_ssx, i * 10 + (5 * j + 1))
                    load_x(t + 1, 1 - j)
            sp_.wait_ge(s_z, 1 + 5 * NT)
            sp_.wait_ge(s_ssx, 1 + 5 * NT)
            sp_.wait_ge(s_zn, NT)
            sp_.wait_ge(s_tr, C_TR + 4 * NT)
            sp_.dma_start(maska, d["maska"]).then_inc(s_maska, 16)
            sp_.dma_start(bm, d["bias"]).then_inc(s_bload, 16)
            sp_.dma_start(maskb, d["maskb"]).then_inc(s_bload, 16)
            sp_.dma_start(g_o, d["g_o"].partition_broadcast(P)).then_inc(s_cload, 16)
            sp_.dma_start(w_out, d["w_out"]).then_inc(s_cload, 16)
            sp_.dma_start(g2, d["g2"].partition_broadcast(P)).then_inc(s_cload, 16)
            sp_.dma_start(wr, d["wr"]).then_inc(s_cload, 16)
            sp_.wait_ge(s_tea, 2 + 2 * NT)
            sp_.wait_ge(s_tev, 2 + 2 * NT)
            sp_.wait_ge(s_zev, 5 + 5 * NT)
            sp_.dma_start(o["kb_p"], ktb[:, :, SEQ - 512:SEQ]).then_inc(s_kv, 16)
            sp_.dma_start(o["ka_p"], kta[:, SEQ - P:SEQ]).then_inc(s_kv, 16)
            sp_.dma_start(o["vb_p"], vb[:, 4:8, :]).then_inc(s_kv, 16)
            sp_.dma_start(o["va_p"], va[:, 7, :]).then_inc(s_kv, 16)
            sp_.dma_start(o["kb_s"], ktb[:, :, SEQ:SEQ + DEC]).then_inc(s_kv, 16)
            sp_.dma_start(o["ka_s"], kta[:, SEQ:SEQ + DEC]).then_inc(s_kv, 16)
            sp_.dma_start(o["vb_s"], vb[0:DEC, 8, :]).then_inc(s_kv, 16)
            sp_.dma_start(o["va_s"], va[0:DEC, 8, :]).then_inc(s_kv, 16)
            def store_rows(t):
                sp_.wait_ge(s_x2, 2 * (t + 1))
                sp_.dma_start(o["y"][t * P:(t + 1) * P, :], row[:, t]).then_inc(s_x2o, 16)
                sp_.wait_ge(s_h2, t + 1)
                sp_.dma_start(h2d[t * P:(t + 1) * P, :], h2[:, t % 2]).then_inc(s_h2o[t % 2], 16)

            for t in range(NT):
                if t >= 2:
                    sp_.wait_ge(s_x2, 2 * (t - 1))
                sp_.dma_start(xc[:, t % 2], d["x"][t]).then_inc(s_xc[t % 2], 16)
                if t >= 1:
                    store_rows(t - 1)
            store_rows(NT - 1)
            sp_.wait_ge(s_pv, NU)
            sp_.wait_ge(s_kv, 16 * 8)
            for dst, name in ((c_tri32, "tri32"), (c_steps, "steps"), (c_block, "block"), (c_iota, "iota")):
                sp_.dma_start(dst, d[name].partition_broadcast(P)).then_inc(s_rload, 16)
            for dst, name in ((c_valid, "valid"), (c_far, "far"), (c_token, "token"), (tri, "tri"), (ones, "ones")):
                sp_.dma_start(dst, d[name]).then_inc(s_rload, 16)
            sp_.dma_start(c_row, d["row"].partition_broadcast(P)).then_inc(s_rload, 16)
            sp_.wait_ge(s_ctl, 1)
            nb = sp_.value_load(ctl[0:1, NINFO:NINFO + 1], min_val=17, max_val=NBLOCK)
            with sp_.Fori(0, NBLOCK // 4) as i:
                for j in range(4):
                    with sp_.If(i * 4 + j < nb):
                        e = sp_.value_load(ctl[0:1, bass.ds(i * 4 + j, 1)], min_val=0, max_val=NE - 1)
                        if j == 2:
                            sp_.wait_ge(s_slot, 1)
                        sp_.wait_ge(s_y, i * 8 + 2 * j + 2)
                        for part, (c0, c1) in enumerate(W_PART):
                            sp_.dma_start(wx[j][:, c0:c1], d["wexp"][bass.ds(e, 1), :, c0:c1].rearrange("a p c -> p (a c)")
                                          ).then_inc(s_w[j][part], 16)

        @block.gpsimd
        def _(pool):
            nc.gpsimd.memset(eps, EPS).then_inc(s_eps, 1)
            pool.wait_ge(s_const, 16 * 6)
            gain = g1.unsqueeze(2).broadcast_to([P, KD, P])

            def scale_x(wait, j):
                pool.wait_ge(s_xt[j], wait)
                nc.gpsimd.tensor_tensor(xt[:, j], xt[:, j], gain, ALU.mult).then_inc(s_xg, 1)

            scale_x(16, 0)
            with pool.Fori(0, 4) as i:
                scale_x(i * 16 + 16, 1)
                scale_x(i * 16 + 32, 0)
            pool.wait_ge(s_pv, NU)
            pool.wait_ge(s_rv, NT)
            pool.wait_ge(s_h2o[0], 16 * 5)
            pool.wait_ge(s_h2o[1], 16 * 4)
            nc.gpsimd.memset(xg, 0.0).then_inc(s_xgz, 1)
            pool.wait_ge(s_slot, 1)
            nb = pool.value_load(ctl[0:1, NINFO:NINFO + 1], min_val=17, max_val=NBLOCK)
            pool.wait_ge(s_xgz, 1)
            pool.dma_start(yb[:, 0], d["x"][0]).then_inc(s_add, 64)
            pool.wait_ge(s_add, 64)
            pool.wait_ge(s_x2o, 16 * NT)
            chain = Chain(pool, s_pool)
            row_bound = pool.to_reg(ROWS - 1)

            def gather(b, j):
                chain.link(nc.gpsimd.tensor_copy(gidx[:, j:j + 1], slot_token[:, bass.ds(b, 1)]))
                pool.sem_inc(s_gi, 1)
                pool.indirect_dma_start(
                    out=xg[:, j], out_offset=None, in_=h2d,
                    in_offset=bass.IndirectOffsetOnAxis(ap=gidx[:, j:j + 1], axis=0),
                    bounds_check=row_bound, oob_is_err=False).then_inc(s_g[j], 16)

            for b in range(3):
                gather(b, b)
            with pool.Fori(0, NBLOCK // 4) as i:
                chain.enter(i, 8)
                for j in range(4):
                    b = i * 4 + j
                    with pool.If(b < nb):
                        pool.wait_ge(s_bx, b + 2)
                        gather(b + 3, (j + 3) % 4)
                        pool.wait_ge(s_ya, b + 2)
                        pool.wait_ge(s_yv, b + 2)
                        chain.link(nc.gpsimd.tensor_copy(sidx[:, j % 2:j % 2 + 1], slot_token[:, bass.ds(b, 1)]))
                        pool.wait_ge(s_add, i * 64 + (16 * j + 64))
                        pool.sem_inc(s_gi, 1)
                        pool.indirect_dma_start(
                            out=o["y"], out_offset=bass.IndirectOffsetOnAxis(ap=sidx[:, j % 2:j % 2 + 1], axis=0),
                            in_=yb[:, j], in_offset=None, bounds_check=row_bound,
                            oob_is_err=False, compute_op=ALU.add).then_inc(s_add, 16)
            added = pool.value_load(ctl[0:1, NINFO + 1:NINFO + 2], min_val=16, max_val=16 * (NBLOCK + 4))
            pool.wait_ge(s_add, added)
            pool.wait_ge(s_kv, 16 * 8)

        @block.scalar
        def _(act):
            for c in range(5):
                act.dma_start(w_in[:, CHUNK_AT[c]:CHUNK_AT[c] + KD * CHUNK[c]],
                              d["w_in"][:, CHUNK_AT[c]:CHUNK_AT[c] + KD * CHUNK[c]]).then_inc(s_win[c], 16)
                if c == 0:
                    act.dma_start(g1, d["g1"]).then_inc(s_const, 16)
                    act.dma_start(ident, d["ident"]).then_inc(s_const, 16)
                    act.dma_start(g64, d["g64"].partition_broadcast(P)).then_inc(s_const, 16)
                    act.dma_start(rope, d["rope"]).then_inc(s_const, 16)
                    act.dma_start(sinks, d["sinks"].partition_broadcast(P)).then_inc(s_const, 16)
                    act.dma_start(rbias, d["rbias"].partition_broadcast(P)).then_inc(s_const, 16)
            act.dma_start(ktb[:, :, ROWS:], d["ckb"]).then_inc(s_cache, 16)
            act.dma_start(kta[:, ROWS:], d["cka"]).then_inc(s_cache, 16)
            act.dma_start(vb[:, NT:, :], d["cvb"]).then_inc(s_cache, 16)
            act.dma_start(va[:, NT, :], d["cva"]).then_inc(s_cache, 16)
            chain = Chain(act, s_act)
            nc.scalar.preload_act_table_set("natural_log_exp_and_others")
            act.wait_ge(s_eps, 1)

            def rstd(out, ms):
                chain.link(nc.scalar.activation(out, ms, ACT.Ln, bias=eps))
                return nc.scalar.activation(out, out, ACT.Exp, scale=-0.5)

            act.sem_inc(s_zev, 5)
            act.sem_inc(s_tea, 2)
            act.sem_inc(s_ssx, 1)

            def square_x(wait, sq1, j):
                act.wait_ge(s_xr[j], wait)
                nc.scalar.activation(xr[:, j], xr[:, j], ACT.Square, scale=D ** -0.5,
                                     accum_out=ssx[:, j:j + 1]).then_inc(s_ssx, 5)
                act.wait_ge(s_ssx, sq1)
                rstd(rsx[:, j:j + 1], ssx[:, j:j + 1]).then_inc(s_rsx, 1)

            def chunks_out(t5, t4, t1, tt, j):
                act.wait_ge(s_rsx, t1)
                act.wait_ge(s_tr, t4)
                vbt = vb[:, tt, :] if isinstance(tt, int) else vb[:, bass.ds(tt, 1), :].rearrange("p a c -> p (a c)")
                vat = va[:, tt, :] if isinstance(tt, int) else va[:, bass.ds(tt, 1), :].rearrange("p a c -> p (a c)")
                for c, dst in enumerate((z[:, j, 0:512], None, z[:, j, 640:1152], z[:, j, 1152:1664], vbt)):
                    act.wait_ge(s_z, t5 + c + 2)
                    if c == 1:
                        nc.scalar.activation(z[:, j, 512:640], bank(1, 0, 128), ACT.Copy, scale=rsx[:, j:j + 1])
                        ins = nc.scalar.activation(vat, bank(1, 128, 256), ACT.Copy, scale=rsx[:, j:j + 1])
                    else:
                        ins = nc.scalar.activation(dst, bank(Z_BANK[c]), ACT.Copy, scale=rsx[:, j:j + 1])
                    ins.then_inc(s_zev, 1)

            def heads_rstd(t1):
                act.wait_ge(s_ss26, t1)
                rstd(rs26, ss26).then_inc(s_rs26, 1)

            def transposes_out(t4, tt, col):
                act.wait_ge(s_tr, t4 + C_TR + 1)
                q = qt[:, tt, 0:4, :] if isinstance(tt, int) else qt[:, bass.ds(tt, 1), 0:4, :].rearrange("p a g c -> p (a g) c")
                nc.scalar.activation(q, bank(5).rearrange("p (g c) -> p g c", g=4), ACT.Copy,
                                     scale=HD ** -0.5).then_inc(s_tea, 1)
                act.wait_ge(s_tr, t4 + C_TR + 2)
                nc.scalar.activation(ktb[:, :, bass.ds(col, P)], bank(6).rearrange("p (g c) -> p g c", g=4),
                                     ACT.Copy).then_inc(s_tea, 1)

            square_x(16, 6, 0)
            chunks_out(0, C_TR - 4, 1, 0, 0)
            heads_rstd(1)
            with act.Fori(0, 4) as i:
                chain.enter(i, 4)
                for j in range(2):
                    square_x(i * 16 + (16 if j == 0 else 32), i * 10 + (5 * j + 11), 1 - j)
                    chunks_out(i * 10 + 5 * (j + 1), i * 8 + (4 * j + C_TR), i * 2 + (j + 2), i * 2 + (j + 1), 1 - j)
                    transposes_out(i * 8 + 4 * j, i * 2 + j, i * 256 + j * P)
                    heads_rstd(i * 2 + (j + 2))
                chain.leave(4)
            transposes_out(4 * (NT - 1), NT - 1, (NT - 1) * P)

            def copy_pt(u):
                _, _, _, _, tiles, _ = unit_info(u)
                cut = (len(tiles) + 1) // 2
                act.wait_ge(s_pt, u + 1)
                rest = tiles[cut:]
                if not rest:
                    act.sem_inc(s_pta, 1)
                    return
                if u >= 2:
                    act.wait_ge(s_pv, u - 1)
                c0 = cut * P
                full = [x for x in rest if x[2] == P]
                ins = None
                if full:
                    c1 = c0 + len(full) * P
                    ins = nc.scalar.activation(pt[:, u % 2, c0:c1], bank(4, 0, c1 - c0), ACT.Copy)
                    c0 = c1
                if len(full) < len(rest):
                    n = rest[-1][2]
                    ins = nc.scalar.activation(pt[0:n, u % 2, c0:c0 + P], bank(4, len(full) * P, len(full) * P + P)[0:n],
                                               ACT.Copy)
                ins.then_inc(s_pta, 1)

            def squares_out(t, m):
                chain.link(nc.scalar.activation(junk[:, 0:512], row[:, t, 512 * m:512 * m + 512], ACT.Square,
                                                scale=512 ** -0.5, accum_out=sso[:, m:m + 1]))
                rstd(rso[:, m:m + 1], sso[:, m:m + 1]).then_inc(s_so, 1)

            def act_pieces(t, g):
                if g == 5:
                    act.wait_ge(s_t1, 2 * t + 1)
                    nc.scalar.activation(ot[:, 0:4], bank(6).rearrange("p (g c) -> p g c", g=4), ACT.Copy).then_inc(s_ota, 1)
                if g == 15:
                    act.wait_ge(s_x2, 2 * (t + 1))
                    chain.link(nc.scalar.activation(junk, row[:, t], ACT.Square, scale=D ** -0.5, accum_out=ss2))
                    rstd(rs2, ss2).then_inc(s_s2, 1)
                if g == 18:
                    act.wait_ge(s_t2, 2 * t + 1)
                    nc.scalar.activation(h2t[:, 0:4], bank(6).rearrange("p (g c) -> p g c", g=4), ACT.Copy).then_inc(s_h2a, 1)

            for u in range(NU):
                t, m, h, segs, tiles, width = unit_info(u)
                k = u % 16
                act.wait_ge(s_sp, u + 1)
                c = m * HEADS + h
                nc.scalar.activation(sp[:, u % 3, 0:width], sp[:, u % 3, 0:width], ACT.Exp,
                                     bias=negm[:, t % 2, c:c + 1], accum_out=psum_e[:, t % 2, c:c + 1]).then_inc(s_p, 1)
                if u >= 2:
                    copy_pt(u - 2)
                if k == 10:
                    act.wait_ge(s_on, 2 * t + 1)
                    squares_out(t, 0)
                if k == 7:
                    act.wait_ge(s_nsk, t + 1)
                    nc.scalar.activation(esink, esink, ACT.Exp).then_inc(s_es, 1)
                if k == 2 and t >= 1:
                    act.wait_ge(s_on, 2 * t)
                    squares_out(t - 1, 1)
                pieces(act_pieces, u)
            copy_pt(NU - 2)
            copy_pt(NU - 1)
            act.wait_ge(s_on, 2 * NT)
            squares_out(NT - 1, 1)
            for u in range(NU, NU + 21):
                pieces(act_pieces, u)

            act.wait_ge(s_gx, 1)
            nc.scalar.activation(gex, gex, ACT.Exp).then_inc(s_gxe, 1)
            act.wait_ge(s_v12, 1)
            nc.scalar.activation(e12, e12, ACT.Exp).then_inc(s_v12e, 1)

            act.sem_inc(s_ya, 1)
            nc.scalar.preload_act_table(ACT.Silu)
            act.wait_ge(s_slot, 1)
            nb = act.value_load(ctl[0:1, NINFO:NINFO + 1], min_val=17, max_val=NBLOCK)

            def rows_t_out(b3, jj):
                act.wait_ge(s_bx, b3)
                nc.scalar.activation(xgt[:, jj, 0:4], bank(2).rearrange("p (g c) -> p g c", g=4), ACT.Copy).then_inc(s_xa, 1)

            def hidden_t_out(made, f):
                act.wait_ge(s_ht, made)
                nc.scalar.activation(hdt[:, f], bank((4, 7)[f], 0, P), ACT.Copy).then_inc(s_hta, 1)

            rows_t_out(3, 0)
            with act.Fori(0, NBLOCK // 4) as i:
                for j in range(4):
                    b = i * 4 + j
                    with act.If(b < nb):
                        act.wait_ge(s_h, i * 8 + (2 * j + C_H))
                        for f in range(2):
                            act.wait_ge(s_gu, i * 8 + (2 * j + f + 1))
                            nc.scalar.activation(sil[:, f], bank(f, 0, P), ACT.Silu).then_inc(s_sil, 1)
                        hidden_t_out(i * 8 + (2 * j + 1), 0)
                        rows_t_out(i * 4 + (j + 4), (j + 1) % 2)
                        hidden_t_out(i * 8 + (2 * j + 2), 1)
                        act.wait_ge(s_y, i * 8 + (2 * j + 9))
                        act.wait_ge(s_add, i * 64 + (16 * j + 16))
                        nc.scalar.activation(yb[:, j, 0:512], bank(5), ACT.Copy).then_inc(s_ya, 1)

        @block.vector
        def _(dve):
            chain = Chain(dve, s_dve)
            link = chain.link
            dve.sem_inc(s_tev, 2)
            dve.wait_ge(s_const, 16 * 6)

            def norm_z(t5, tt, t1, j):
                dve.wait_ge(s_zev, t5 + 4 + 5)
                zj = z[:, j]
                zh = zj.rearrange("p (h c) -> p h c", c=HD)
                sqh = sq.rearrange("p (h c) -> p h c", c=HD)
                link(nc.vector.tensor_tensor(sq, zj, zj, ALU.mult))
                link(nc.vector.tensor_reduce(ss26, sqh, AXX, ALU.add))
                nc.vector.tensor_scalar(ss26, ss26, 1.0 / HD, None, ALU.mult).then_inc(s_ss26, 1)
                dve.wait_ge(s_rs26, t1)
                link(nc.vector.tensor_tensor(sqh, zh, rs26.unsqueeze(2).broadcast_to([P, 26, HD]), ALU.mult))
                for a, (h0, h1) in enumerate(((0, 8), (8, 10), (10, 18), (18, 26))):
                    ins = nc.vector.tensor_tensor(zh[:, h0:h1], sqh[:, h0:h1],
                                                  g64[:, a:a + 1, :].broadcast_to([P, h1 - h0, HD]), ALU.mult)
                link(ins)
                rp = rope[:, tt, :] if isinstance(tt, int) else rope[:, bass.ds(tt, 1), :].rearrange("p a c -> p (a c)")
                cos = rp[:, 0:8].unsqueeze(1).broadcast_to([P, 10, 8])
                sin = rp[:, 8:16].unsqueeze(1).broadcast_to([P, 10, 8])
                x1, x2 = zh[:, 0:10, 0:8], zh[:, 0:10, 8:16]
                tmp = sqh[:, 0:10]
                nc.vector.tensor_tensor(tmp[:, :, 0:8], x1, cos, ALU.mult)
                nc.vector.tensor_tensor(tmp[:, :, 8:16], x2, sin, ALU.mult)
                nc.vector.tensor_tensor(tmp[:, :, 16:24], x2, cos, ALU.mult)
                link(nc.vector.tensor_tensor(tmp[:, :, 24:32], x1, sin, ALU.mult))
                nc.vector.tensor_tensor(x1, tmp[:, :, 0:8], tmp[:, :, 8:16], ALU.subtract)
                nc.vector.tensor_tensor(x2, tmp[:, :, 16:24], tmp[:, :, 24:32], ALU.add).then_inc(s_zn, 1)

            def transposes_out(t4, tt, col):
                dve.wait_ge(s_tr, t4 + C_TR + 3)
                q = qt[:, tt, 4:8, :] if isinstance(tt, int) else qt[:, bass.ds(tt, 1), 4:8, :].rearrange("p a g c -> p (a g) c")
                nc.vector.tensor_scalar(q, bank(7).rearrange("p (g c) -> p g c", g=4), HD ** -0.5, None,
                                        ALU.mult).then_inc(s_tev, 1)
                dve.wait_ge(s_tr, t4 + C_TR + 4)
                nc.vector.tensor_copy(kta[:, bass.ds(col, P)], bank(4, 0, P)).then_inc(s_tev, 1)

            norm_z(0, 0, 1, 0)
            with dve.Fori(0, 4) as i:
                chain.enter(i, 10)
                for j in range(2):
                    dve.wait_ge(s_zn, i * 2 + (j + 1))
                    norm_z(i * 10 + 5 * (j + 1), i * 2 + (j + 1), i * 2 + (j + 2), 1 - j)
                    transposes_out(i * 8 + 4 * j, i * 2 + j, i * 256 + j * P)
                chain.leave(4)
            transposes_out(4 * (NT - 1), NT - 1, (NT - 1) * P)

            dve.wait_ge(s_maska, 16)

            def copy_pt(u):
                _, _, _, _, tiles, _ = unit_info(u)
                cut = (len(tiles) + 1) // 2
                dve.wait_ge(s_pt, u + 1)
                if u >= 2:
                    dve.wait_ge(s_pv, u - 1)
                full = [x for x in tiles[:cut] if x[2] == P]
                assert len(full) == cut
                nc.vector.tensor_copy(pt[:, u % 2, 0:cut * P], bank(3, 0, cut * P)).then_inc(s_ptv, 1)

            def divide(t, m):
                dve.wait_ge(s_pv, 16 * t + 8 * (m + 1))
                s8 = psum_e[:, t % 2, 8 * m:8 * m + 8]
                r8 = rden[:, 8 * m:8 * m + 8]
                if m == 0:
                    dve.wait_ge(s_es, t + 1)
                    link(nc.vector.tensor_tensor(r8, s8, esink, ALU.add))
                    link(nc.vector.reciprocal(r8, r8))
                else:
                    link(nc.vector.reciprocal(r8, s8))
                nc.vector.tensor_tensor(row[:, t, 512 * m:512 * m + 512].rearrange("p (h c) -> p h c", c=HD),
                                        o_ps.rearrange("p (h c) -> p h c", c=HD),
                                        r8.unsqueeze(2).broadcast_to([P, 8, HD]), ALU.mult).then_inc(s_on, 1)

            def norm_out(t, m):
                dve.wait_ge(s_so, 2 * t + m + 1)
                if t == 0 and m == 0:
                    dve.wait_ge(s_cload, 16 * 4)
                part = row[:, t, 512 * m:512 * m + 512]
                nc.vector.scalar_tensor_tensor(part, part, rso[:, m:m + 1], g_o[:, 512 * m:512 * m + 512],
                                               ALU.mult, ALU.mult).then_inc(s_og, 1)

            def dve_pieces(t, g):
                if g == 5:
                    dve.wait_ge(s_t1, 2 * t + 2)
                    nc.vector.tensor_copy(ot[:, 4:8], bank(7).rearrange("p (g c) -> p g c", g=4)).then_inc(s_otv, 1)
                if g in (10, 14):
                    n = (g - 10) // 4
                    dve.wait_ge(s_op, 2 * t + n + 1)
                    if n == 0:
                        dve.wait_ge(s_xc[t % 2], 16 * (t // 2 + 1))
                    nc.vector.tensor_tensor(row[:, t, 512 * n:512 * n + 512], bank(6 + n),
                                            xc[:, t % 2, 512 * n:512 * n + 512], ALU.add).then_inc(s_x2, 1)
                if g == 16:
                    dve.wait_ge(s_s2, t + 1)
                    if t >= 2:
                        dve.wait_ge(s_h2o[t % 2], 16 * (t // 2))
                        dve.wait_ge(s_t2, 2 * (t - 1))
                    nc.vector.scalar_tensor_tensor(h2[:, t % 2], row[:, t], rs2, g2, ALU.mult, ALU.mult).then_inc(s_h2, 1)
                if g == 18:
                    dve.wait_ge(s_t2, 2 * t + 2)
                    nc.vector.tensor_copy(h2t[:, 4:8], bank(7).rearrange("p (g c) -> p g c", g=4)).then_inc(s_h2v, 1)
                if g == 20:
                    dve.wait_ge(s_r, t + 1)
                    nc.vector.tensor_tensor(logits[:, t], bank(6, 0, NR), rbias, ALU.add).then_inc(s_rv, 1)

            for u in range(NU):
                t, m, h, segs, tiles, width = unit_info(u)
                k = u % 16
                c = m * HEADS + h
                if t == 0 and m == 1:
                    if h == 0:
                        dve.wait_ge(s_bload, 16 * 2)
                    link(nc.vector.tensor_tensor(bm[:, h], bm[:, h], maskb, ALU.add))
                if k == 10:
                    divide(t, 0)
                if k == 11:
                    norm_out(t, 0)
                if k == 2 and t >= 1:
                    divide(t - 1, 1)
                if k == 3 and t >= 1:
                    norm_out(t - 1, 1)
                dve.wait_ge(s_qk, u + 1)
                if u >= 3:
                    dve.wait_ge(s_pt, u - 2)
                b0 = first_bias(t, m)
                at = scores_at(u, width)
                add = bm[:, h, b0:b0 + width] if m else maska[:, b0:b0 + width]
                link(nc.vector.tensor_tensor_reduce(
                    out=sp[:, u % 3, 0:width], in0=ps[:, at:at + width], in1=add, scale=1.0,
                    scalar=sinks[:, h:h + 1] if m == 0 else -3e38, op0=ALU.add, op1=ALU.max,
                    accum_out=mx[:, u % 2:u % 2 + 1]))
                nc.vector.tensor_scalar(negm[:, t % 2, c:c + 1], mx[:, u % 2:u % 2 + 1], -1.0, None,
                                        ALU.mult).then_inc(s_sp, 1)
                if u >= 2:
                    copy_pt(u - 2)
                if k == 7:
                    if t >= 1:
                        dve.wait_ge(s_on, 2 * t)
                    dve.wait_ge(s_sp, u + 1)
                    nc.vector.tensor_tensor(esink, sinks, negm[:, t % 2, 0:8], ALU.add).then_inc(s_nsk, 1)
                pieces(dve_pieces, u)
            copy_pt(NU - 2)
            copy_pt(NU - 1)
            divide(NT - 1, 1)
            norm_out(NT - 1, 1)
            for u in range(NU, NU + 21):
                pieces(dve_pieces, u)

            dve.wait_ge(s_rload, 16 * 10)
            dve.wait_ge(s_rv, NT)
            tt_, ts_, red = nc.vector.tensor_tensor, nc.vector.tensor_scalar, nc.vector.tensor_reduce
            gl = logits[:, :, 0:NG]
            el = logits[:, :, NG:NR]
            iota4 = c_iota[:, 0:NG].unsqueeze(1).broadcast_to([P, NT, NG])
            iota32 = c_iota.unsqueeze(1).broadcast_to([P, NT, NE])

            def wide(x, n):
                return x.broadcast_to([P, NT, n])

            def top_one(values, best, scratch, hot, iota, n):
                link(red(best, values, AXX, ALU.max))
                link(tt_(scratch, values, wide(best, n), ALU.is_lt))
                link(ts_(scratch, scratch, 1000.0, None, ALU.mult))
                link(tt_(scratch, scratch, iota, ALU.add))
                link(red(idx, scratch, AXX, ALU.min))
                link(tt_(hot, iota, wide(idx, n), ALU.is_equal))

            top_one(gl, gmx, geq, goh, iota4, NG)
            tt_(gex, gl, wide(gmx, NG), ALU.subtract).then_inc(s_gx, 1)
            link(ts_(geq, goh, BIG, -BIG, ALU.mult, ALU.add))
            e4 = el.rearrange("p t (g e) -> p t g e", g=NG)
            m4 = m32.rearrange("p t (g e) -> p t g e", g=NG)
            for g in range(NG):
                ins = tt_(m4[:, :, g], e4[:, :, g], wide(goh[:, :, g:g + 1], 8), ALU.mult)
            link(ins)
            for g in range(NG):
                ins = tt_(m4[:, :, g], m4[:, :, g], wide(geq[:, :, g:g + 1], 8), ALU.add)
            link(ins)
            top_one(m32, v1, eq, oh1, iota32, NE)
            link(ts_(m2, oh1, -2 * BIG, None, ALU.mult))
            link(tt_(m2, m2, m32, ALU.add))
            top_one(m2, v2, eq, oh2, iota32, NE)
            tt_(e12, v2, v1, ALU.subtract).then_inc(s_v12, 1)
            link(tt_(eq, oh1, oh2, ALU.add))
            tt_(mb, eq, wide(c_valid.unsqueeze(2), NE), ALU.mult).then_inc(s_mb, 1)
            dve.wait_ge(s_cum, 1)
            link(nc.vector.tensor_copy(cntv, ps[:, NT * NE:NT * NE + NE]))
            link(tt_(cmp9, cntv.unsqueeze(2).broadcast_to([P, NE, 9]),
                     c_steps.unsqueeze(1).broadcast_to([P, NE, 9]), ALU.is_gt))
            link(red(nblk, cmp9, AXX, ALU.add))
            link(tt_(prod, c_tri32, nblk.unsqueeze(1).broadcast_to([P, NE, NE]), ALU.mult))
            link(red(excl, prod, AXX, ALU.add))
            link(tt_(incl, excl, nblk, ALU.add))
            link(tt_(cmpb[0:1], incl[0:1].unsqueeze(1).broadcast_to([1, NINFO, NE]),
                     c_block[0:1].unsqueeze(2).broadcast_to([1, NINFO, NE]), ALU.is_le))
            link(red(ctlf[0:1, 0:NINFO], cmpb[0:1], AXX, ALU.add))
            link(ts_(ctlf[0:1, 0:NINFO], ctlf[0:1, 0:NINFO], NE - 1.0, None, ALU.min))
            link(nc.vector.tensor_copy(ctlf[0:1, NINFO:NINFO + 1], incl[0:1, NE - 1:NE]))
            link(ts_(ctlf[0:1, NINFO + 1:NINFO + 2], incl[0:1, NE - 1:NE], 16.0, 64.0, ALU.mult, ALU.add))
            nc.vector.tensor_copy(ctl[0:1, 0:NINFO + 2], ctlf[0:1, 0:NINFO + 2]).then_inc(s_ctl, 1)
            link(ts_(basev, excl, float(P), None, ALU.mult))
            pos = ps[:, 0:NT * NE].rearrange("p (t c) -> p t c", t=NT)
            link(tt_(m32, pos, basev.unsqueeze(1).broadcast_to([P, NT, NE]), ALU.add))
            for k, oh in enumerate((oh1, oh2)):
                link(tt_(eq, oh, m32, ALU.mult))
                link(red(slots[:, :, k:k + 1], eq, AXX, ALU.add))
                link(tt_(slots[:, :, k:k + 1], slots[:, :, k:k + 1], c_far.unsqueeze(2), ALU.add))
            link(nc.vector.tensor_copy(sloti, slots))
            ts_(slotr, sloti, P - 1, None, ALU.bitwise_and)
            link(ts_(slotb, sloti, 7, None, ALU.logical_shift_right))
            nc.vector.tensor_copy(slotrf, slotr)
            link(nc.vector.tensor_copy(slotbf, slotb))
            dve.wait_ge(s_gxe, 1)
            link(red(gsum, gex, AXX, ALU.add))
            link(nc.vector.reciprocal(gp, gsum))
            dve.wait_ge(s_v12e, 1)
            link(ts_(v1, e12, 1.0, None, ALU.add))
            link(nc.vector.reciprocal(v1, v1))
            link(tt_(v1, v1, gp, ALU.mult))
            link(tt_(v2, v1, e12, ALU.mult))
            for n in range(2 * NT):
                t, k = divmod(n, 2)
                if n >= 4:
                    dve.wait_ge(s_inv, n - 3)
                ts_(in_row[:, n % 4], c_row, slotrf[:, t, k:k + 1], None, ALU.is_equal)
                ts_(in_block[:, n % 4, 0], c_block, slotbf[:, t, k:k + 1], c_token[:, t, k:k + 1], ALU.is_equal, ALU.mult)
                ts_(in_block[:, n % 4, 1], c_block, slotbf[:, t, k:k + 1], (v1, v2)[k][:, t], ALU.is_equal,
                    ALU.mult).then_inc(s_in, 1)
            dve.wait_ge(s_inv, 2 * NT)
            ts_(slot_token, bank(1, 0, NINFO), float(FAR), None, ALU.add)
            nc.vector.tensor_copy(slot_weight, bank(1, NINFO, 2 * NINFO)).then_inc(s_slot, 1)

            dve.sem_inc(s_yv, 1)
            dve.sem_inc(s_h, C_H)
            dve.wait_ge(s_slot, 1)
            nb = dve.value_load(ctl[0:1, NINFO:NINFO + 1], min_val=17, max_val=NBLOCK)

            def rows_t_out(b3, jj):
                dve.wait_ge(s_bx, b3)
                nc.vector.tensor_copy(xgt[:, jj, 4:8], bank(3).rearrange("p (g c) -> p g c", g=4)).then_inc(s_xv, 1)

            rows_t_out(3, 0)
            with dve.Fori(0, NBLOCK // 4) as i:
                for j in range(4):
                    b = i * 4 + j
                    with dve.If(b < nb):
                        gate = slot_weight[:, bass.ds(b, 1)]
                        for f in range(2):
                            dve.wait_ge(s_sil, i * 8 + (2 * j + f + 1))
                            nc.vector.scalar_tensor_tensor(hd[:, f], bank(f, P, 2 * P), gate,
                                                           sil[:, f], ALU.mult, ALU.mult).then_inc(s_h, 1)
                        rows_t_out(i * 4 + (j + 4), (j + 1) % 2)
                        dve.wait_ge(s_y, i * 8 + (2 * j + 10))
                        dve.wait_ge(s_add, i * 64 + (16 * j + 16))
                        nc.vector.tensor_copy(yb[:, j, 512:1024], bank(6)).then_inc(s_yv, 1)

        @block.tensor
        def _(pe):
            mm = nc.tensor.matmul
            pe.sem_inc(s_z, 1)
            pe.sem_inc(s_tr, C_TR)

            def project(t5, t1, j, first=False):
                pe.wait_ge(s_xg, t1)
                for c in range(5):
                    if first:
                        pe.wait_ge(s_win[c], 16)
                    pe.wait_ge(s_zev, t5 + {1: 5, 4: 7}.get(c, c + 1))
                    for k in range(KD):
                        a = CHUNK_AT[c] + k * CHUNK[c]
                        ins = mm(bank(Z_BANK[c], 0, CHUNK[c]), xt[:, j, k, :], w_in[:, a:a + CHUNK[c]],
                                 start=(k == 0), stop=(k == KD - 1))
                    ins.then_inc(s_z, 1)

            def transposes(t2, t1, j):
                pe.wait_ge(s_zn, t1)
                for c0, n, bk, at, freed, v in ((0, 4, 5, 0, s_tea, 1), (1152, 4, 6, 0, s_tea, 2),
                                                (640, 4, 7, 0, s_tev, 1), (512, 1, 4, 0, s_tev, 2)):
                    pe.wait_ge(freed, t2 + v)
                    for g in range(n):
                        ins = nc.tensor.transpose(bank(bk, at + g * P, at + g * P + P), z[:, j, c0 + g * P:c0 + g * P + P], ident)
                    ins.then_inc(s_tr, 1)

            project(0, 1, 0, first=True)
            pe.wait_ge(s_const, 16 * 6)
            with pe.Fori(0, 4) as i:
                for j in range(2):
                    project(i * 10 + 5 * (j + 1), i * 2 + (j + 2), 1 - j)
                    transposes(i * 4 + 2 * j, i * 2 + (j + 1), j)
            transposes(2 * (NT - 1), NT, 0)

            def scores(u):
                if u >= NU:
                    return
                t, m, h, segs, tiles, width = unit_info(u)
                if u >= 2:
                    pe.wait_ge(s_sp, u - 1)
                half, g = (h // 4, h % 4) if m == 0 else (h % 2, 4 + h // 2)
                a = half * HD
                q = qt[a:a + HD, t, g, :]
                kt = kta[a:a + HD] if m == 0 else ktb[a:a + HD, g - 4]
                out0 = scores_at(u, width)
                c, runs = 0, []
                for col, n in segs:
                    k = 0
                    while k < n:
                        at = out0 + c + k
                        step = min(n - k, 512 - at % 512)
                        runs.append((at, step, col + k))
                        k += step
                    c += n
                for at, step, col in sorted(runs, key=lambda r: r[0] // 512 == 1):
                    if at // 512 == 1 and u >= 1:
                        pe.wait_ge(s_sp, u)
                    ins = mm(ps[:, at:at + step], q, kt[:, col:col + step], start=True, stop=True)
                ins.then_inc(s_qk, 1)

            def transpose_probs(u):
                t, m, h, segs, tiles, width = unit_info(u)
                pe.wait_ge(s_p, u + 1)
                if u >= 1:
                    pe.wait_ge(s_ptv, u)
                    pe.wait_ge(s_pta, u)
                cut = (len(tiles) + 1) // 2
                for i, (c, _, n) in enumerate(tiles):
                    dst = bank(3, i * P, i * P + P) if i < cut else bank(4, (i - cut) * P, (i - cut) * P + P)
                    ins = nc.tensor.transpose(dst[0:n], sp[:, u % 3, c:c + n], ident)
                ins.then_inc(s_pt, 1)

            def values(u):
                t, m, h, segs, tiles, width = unit_info(u)
                pe.wait_ge(s_ptv, u + 1)
                pe.wait_ge(s_pta, u + 1)
                if h == 0 and u >= 1:
                    pe.wait_ge(s_on, 2 * t + m)
                for i, (c, vt, n) in enumerate(tiles):
                    v = va[0:n, vt, (h // 4) * HD:(h // 4 + 1) * HD] if m == 0 else vb[0:n, vt, h * HD:(h + 1) * HD]
                    ins = mm(o_ps[:, h * HD:(h + 1) * HD], pt[0:n, u % 2, i * P:i * P + P], v,
                             start=(i == 0), stop=(i == len(tiles) - 1))
                ins.then_inc(s_pv, 1)

            def pe_pieces(t, g):
                if g == 4:
                    pe.wait_ge(s_og, 2 * (t + 1))
                    if t >= 1:
                        pe.wait_ge(s_rv, t)
                    for c in range(KD):
                        ins = nc.tensor.transpose(bank(6 + c // 4, c % 4 * P, c % 4 * P + P), row[:, t, c * P:c * P + P], ident)
                        if c % 4 == 3:
                            ins.then_inc(s_t1, 1)
                if 6 <= g < 14:
                    n, quarter = (g - 6) // 4, (g - 6) % 4
                    if g == 6:
                        pe.wait_ge(s_cload, 16 * 4)
                        pe.wait_ge(s_ota, t + 1)
                        pe.wait_ge(s_otv, t + 1)
                    for c in range(2 * quarter, 2 * quarter + 2):
                        ins = mm(bank(6 + n), ot[:, c], w_out[:, c, 512 * n:512 * n + 512], start=(c == 0), stop=(c == KD - 1))
                    if quarter == 3:
                        ins.then_inc(s_op, 1)
                if g == 17:
                    pe.wait_ge(s_h2, t + 1)
                    for c in range(KD):
                        ins = nc.tensor.transpose(bank(6 + c // 4, c % 4 * P, c % 4 * P + P), h2[:, t % 2, c * P:c * P + P], ident)
                        if c % 4 == 3:
                            ins.then_inc(s_t2, 1)
                if g == 19:
                    pe.wait_ge(s_h2a, t + 1)
                    pe.wait_ge(s_h2v, t + 1)
                    for c in range(KD):
                        ins = mm(bank(6, 0, NR), h2t[:, c], wr[:, c], start=(c == 0), stop=(c == KD - 1))
                    ins.then_inc(s_r, 1)

            pe.wait_ge(s_cache, 16 * 4)
            pe.wait_ge(s_tea, 2 + 2 * NT)
            pe.wait_ge(s_tev, 2 + 2 * NT)
            scores(0)
            for u in range(NU):
                scores(u + 1)
                if u >= 1:
                    transpose_probs(u - 1)
                if u >= 2:
                    values(u - 2)
                pieces(pe_pieces, u)
            transpose_probs(NU - 1)
            values(NU - 2)
            values(NU - 1)
            for u in range(NU, NU + 21):
                pieces(pe_pieces, u)

            pe.wait_ge(s_mb, 1)
            pe.wait_ge(s_rv, NT)
            for t in range(NT):
                for s in range(t + 1):
                    mm(ps[:, t * NE:t * NE + NE], tri if s == t else ones, mb[:, s], start=(s == 0), stop=(s == t))
            for s in range(NT):
                ins = mm(ps[:, NT * NE:NT * NE + NE], ones, mb[:, s], start=(s == 0), stop=(s == NT - 1))
            ins.then_inc(s_cum, 1)
            for n in range(2 * NT):
                pe.wait_ge(s_in, n + 1)
                mm(bank(1, 0, 2 * NINFO), in_row[:, n % 4], in_block[:, n % 4].rearrange("p a c -> p (a c)"),
                   start=(n == 0), stop=(n == 2 * NT - 1)).then_inc(s_inv, 1)

            pe.sem_inc(s_y, 8)
            pe.sem_inc(s_bx, 2)
            pe.wait_ge(s_slot, 1)
            nb = pe.value_load(ctl[0:1, NINFO:NINFO + 1], min_val=17, max_val=NBLOCK)

            def rows_t(wait, jj):
                pe.wait_ge(s_g[jj], wait)
                for g in range(8):
                    ins = nc.tensor.transpose(bank(2 + g // 4, g % 4 * P, g % 4 * P + P), xg[:, jj, g * P:g * P + P], ident)
                ins.then_inc(s_bx, 1)

            def hidden_t(made, f):
                pe.wait_ge(s_h, made)
                nc.tensor.transpose(bank((4, 7)[f], 0, P), hd[:, f], ident).then_inc(s_ht, 1)

            rows_t(16, 0)
            with pe.Fori(0, NBLOCK // 4) as i:
                for j in range(4):
                    b = i * 4 + j
                    with pe.If(b < nb):
                        w = wx[j]
                        pe.wait_ge(s_xa, i * 4 + (j + 1))
                        pe.wait_ge(s_xv, i * 4 + (j + 1))
                        pe.wait_ge(s_h, i * 8 + (2 * j + C_H))
                        for f in range(2):
                            pe.wait_ge(s_w[j][f], i * 16 + 16)
                            for k in range(KD):
                                a = (f * KD + k) * FF
                                ins = mm(bank(f, 0, FF), xgt[:, j % 2, k], w[:, a:a + FF],
                                         start=(k == 0), stop=(k == KD - 1))
                            ins.then_inc(s_gu, 1)
                        hidden_t(i * 8 + (2 * j + 1 + C_H), 0)
                        rows_t(i * 16 + (32 if j == 3 else 16), (j + 1) % 4)
                        hidden_t(i * 8 + (2 * j + 2 + C_H), 1)
                        pe.wait_ge(s_w[j][2], i * 16 + 16)
                        pe.wait_ge(s_ya, i * 4 + (j + 1))
                        pe.wait_ge(s_yv, i * 4 + (j + 1))
                        for f in range(2):
                            pe.wait_ge(s_hta, i * 8 + (2 * j + 1 + f))
                            for n in range(2):
                                a = 2 * KD * FF + f * D + n * 512
                                ins = mm(bank(5 + n), hdt[:, f], w[:, a:a + 512], start=(f == 0), stop=(f == 1))
                                if f == 1:
                                    ins.then_inc(s_y, 1)


INS = ["xT", "x", "w_in", "g1", "ident", "g64", "rope", "sinks", "rbias", "ckb", "cka", "cvb", "cva", "bias", "maskb",
       "maska", "g_o", "w_out", "g2", "wr", "tri32", "steps", "block", "iota", "valid", "far", "token", "row",
       "tri", "ones", "wexp"]
OUTS = {"y": [ROWS, D], "ka_p": [P, P], "va_p": [P, P], "kb_p": [P, 4, 512], "vb_p": [P, 4, 512],
        "ka_s": [P, DEC], "va_s": [DEC, P], "kb_s": [P, 4, DEC], "vb_s": [DEC, 512]}


def kernel(**inputs):
    import ml_dtypes
    import concourse.bacc as bacc
    from concourse.bass_utils import run_bass_kernel_spmd

    a = {k: np.asarray(v) for k, v in inputs.items()}
    f32 = np.float32
    L = {}
    x = np.zeros((ROWS, D), f32)
    x[:SEQ] = a["x_prompt"][0]
    x[SEQ:SEQ + DEC] = a["x_sample"][0]
    L["x"] = x.reshape(NT, P, D)
    L["xT"] = np.ascontiguousarray(L["x"].reshape(NT, P, KD, P).transpose(0, 3, 2, 1))
    w = a["w_in"][0]
    pair = [p + 4 * s for p in range(4) for s in range(2)]
    wqa = w[:, 0:512].reshape(D, 8, HD)[:, pair].reshape(D, 512)
    parts = [wqa, w[:, 512:768], w[:, 768:1280], w[:, 1280:1792], w[:, 1792:2304]]
    L["w_in"] = np.concatenate([c.reshape(KD, P, -1).transpose(1, 0, 2).reshape(P, -1) for c in parts], axis=1)
    L["g1"] = a["norm1"][0].reshape(KD, P).T
    L["ident"] = np.eye(P, dtype=f32)
    L["g64"] = np.stack([a["q_norm_a"][0], a["k_norm_a"][0], a["q_norm_b"][0], a["k_norm_b"][0]])
    inv = f32(500000.0) ** (-np.arange(8, dtype=f32) / f32(8))
    pos = np.zeros(ROWS, f32)
    pos[:SEQ] = np.arange(SEQ)
    pos[SEQ:SEQ + DEC] = 256 + np.arange(DEC)
    ang = (pos[:, None] * inv[None, :]).astype(f32)
    L["rope"] = np.concatenate([np.cos(ang), np.sin(ang)], axis=1).astype(f32).reshape(NT, P, 16).transpose(1, 0, 2)
    L["sinks"] = a["sinks_a"][0]
    L["rbias"] = np.concatenate([a["b_router_group"][0], a["b_router_expert"][0].reshape(-1)])
    L["ckb"] = a["cache_b_k"][0, 0].reshape(CACHE_B, 4, P).transpose(2, 1, 0)
    L["cka"] = a["cache_a_k"][0, 0].reshape(CACHE_A, P).T
    L["cvb"] = a["cache_b_v"][0, 0].reshape(2, P, 512).transpose(1, 0, 2)
    L["cva"] = a["cache_a_v"][0, 0].reshape(P, P)
    dist = np.clip(np.arange(KW)[None, :] - 4 * P - np.arange(P)[:, None], -128, 128) + 128
    L["bias"] = a["rel_bias_b"][0][:, dist].transpose(1, 0, 2)
    late_q = (np.arange(P) >= 64)[:, None]
    old = late_q & (np.arange(P) < 64)[None, :]
    new = ~late_q & (np.arange(P) >= 64)[None, :]
    none = np.zeros((P, 3 * P), bool)
    L["maskb"] = np.where(np.concatenate([old, none, new], axis=1), f32(-BIG), f32(0))
    L["maska"] = np.where(np.concatenate([old, new], axis=1), f32(-BIG), f32(0))
    L["g_o"] = np.concatenate([a["out_norm_a"][0], a["out_norm_b"][0]])
    L["w_out"] = a["w_out"][0].reshape(KD, P, D).transpose(1, 0, 2)
    L["g2"] = a["norm2"][0]
    wr = np.concatenate([a["w_router_group"][0]] + [a["w_router_expert"][0, g] for g in range(NG)], axis=1)
    L["wr"] = wr.reshape(KD, P, NR).transpose(1, 0, 2)
    L["tri32"] = np.tril(np.ones((NE, NE), f32), -1)
    L["steps"] = np.arange(9, dtype=f32) * P
    L["block"] = np.arange(NINFO, dtype=f32)
    L["iota"] = np.arange(NE, dtype=f32)
    tok = np.arange(NT)[None, :] * P + np.arange(P)[:, None]
    real = tok < SEQ + DEC
    L["valid"] = real.astype(f32)
    L["far"] = np.where(real, 0, FAR).astype(f32)
    L["token"] = np.stack([tok - FAR, tok - FAR], axis=2).astype(f32)
    L["row"] = np.arange(P, dtype=f32)
    L["tri"] = np.triu(np.ones((P, P), f32), 1).astype(ml_dtypes.bfloat16)
    L["ones"] = np.ones((P, P), ml_dtypes.bfloat16)
    gu = [a[n][0].reshape(NE, KD, P, 2, P) for n in ("w_gate", "w_up")]
    gu = np.stack(gu, axis=4).transpose(0, 2, 3, 1, 4, 5).reshape(NE, P, -1)
    dn = a["w_down"][0].reshape(NE, 2, P, D).transpose(0, 2, 1, 3).reshape(NE, P, -1)
    L["wexp"] = np.concatenate([gu, dn], axis=2)

    nc = bacc.Bacc("TRN2", target_bir_lowering=False, num_devices=1)
    arrays, d, o = {}, {}, {}
    for name in INS:
        arr = np.ascontiguousarray(L[name])
        arrays["in_" + name] = arr
        d[name] = nc.dram_tensor("in_" + name, arr.shape, mybir.dt.from_np(arr.dtype), kind="ExternalInput").ap()
    for name, shape in OUTS.items():
        o[name] = nc.dram_tensor("out_" + name, shape, F32, kind="ExternalOutput").ap()
    build(nc, d, o)
    res = run_bass_kernel_spmd(nc, [arrays], core_ids=[0]).results[0]
    r = {name: np.asarray(res["out_" + name]).reshape(shape) for name, shape in OUTS.items()}

    def keys_b(k, n):
        return np.ascontiguousarray(k.transpose(2, 1, 0)).reshape(1, 1, n, 8, HD)

    return (r["y"][None, :SEQ], r["y"][None, SEQ:SEQ + DEC],
            np.ascontiguousarray(r["ka_p"].T).reshape(1, 1, P, 2, HD), r["va_p"].reshape(1, 1, P, 2, HD),
            keys_b(r["kb_p"], 512), np.ascontiguousarray(r["vb_p"].transpose(1, 0, 2)).reshape(1, 1, 512, 8, HD),
            np.ascontiguousarray(r["ka_s"].T).reshape(1, 1, DEC, 2, HD), r["va_s"].reshape(1, 1, DEC, 2, HD),
            keys_b(r["kb_s"], DEC), r["vb_s"].reshape(1, 1, DEC, 8, HD))
```

```python
import numpy as np
import concourse.bass as bass
from concourse import mybir
from contextlib import ExitStack

F32 = mybir.dt.float32
BF16 = mybir.dt.bfloat16
I32 = mybir.dt.int32
ALU = mybir.AluOpType
ACT = mybir.ActivationFunctionType
AXX = mybir.AxisListType.X

D = 1024
P = 128
KD = D // P
SEQ, DEC = 1024, 32
NT = SEQ // P + 1
ROWS = NT * P
HD = 64
HEADS = 8
CACHE_A, CACHE_B = 128, 256
EPS = 1e-6
NG, NE, FF = 4, 32, 256
NR = NG + NE
NBLOCK = 48
NINFO = NBLOCK + 3
KW = 5 * P
EW = 2 * KD * FF + 2 * D
W_PART = ((0, KD * FF), (KD * FF, 2 * KD * FF), (2 * KD * FF, EW))
FAR = 1 << 20
BIG = 1e30

CHUNK = (512, 256, 512, 512, 512)
Z_BANK = (0, 1, 2, 3, 1)
CHUNK_AT = (0, 4096, 6144, 10240, 14336)


class Chain:

    def __init__(self, eng, sem):
        self.eng, self.sem, self.base, self.k, self.i, self.per = eng, sem, 0, 0, None, 0

    def enter(self, i, per):
        self.i, self.per, self.k, self.base = i, per, 0, self.base + self.k

    def leave(self, times):
        assert self.k == self.per, (self.k, self.per)
        self.base, self.k, self.i = self.base + times * self.per, 0, None

    def link(self, ins):
        ins.then_inc(self.sem, 1)
        self.k += 1
        v = self.base + self.k
        v = v if self.i is None else self.i * self.per + v
        self.eng.wait_ge(self.sem, v)


def tile_keys(t):
    if t == NT - 1:
        return ([(ROWS, CACHE_A), (SEQ, DEC)], [(ROWS, CACHE_B), (SEQ, DEC)])
    a, b = max(0, t - 1), max(0, t - 4)
    return ([(a * P, (t + 1 - a) * P)], [(b * P, (t + 1 - b) * P)])


def build(nc, d, o):
    ctx = ExitStack()
    with ctx:
        def sem(name):
            return ctx.enter_context(nc.semaphore(name))

        arena = ctx.enter_context(nc.sbuf_tensor("arena", [P, 52700], F32))
        ps = ctx.enter_context(nc.psum_tensor("ps", [P, 8 * 512], F32))
        top = [0]

        def place(n, at=None):
            a = top[0] if at is None else at
            if at is None:
                top[0] += n
            assert a + n <= 52700, (a, n)
            return arena[:, a:a + n]

        ident = place(P)
        g1 = place(KD)
        g64 = place(4 * HD).rearrange("p (a d) -> p a d", d=HD)
        rope = place(NT * 16).rearrange("p (t c) -> p t c", c=16)
        sinks = place(HEADS)
        rbias = place(NR)
        logits = place(NT * NR).rearrange("p (t c) -> p t c", c=NR)
        sum_a = logits.rearrange("p t c -> p (t c)")[:, 0:P]
        ssx, rsx = place(2), place(2)
        eps = place(1)
        ss26, rs26 = place(26), place(26)
        negm = place(2 * 16).rearrange("p (b c) -> p b c", b=2)
        mx = place(2)
        psum_e = place(2 * 16).rearrange("p (b c) -> p b c", b=2)
        esink = place(HEADS)
        rden = place(16)
        sso, rso = place(2), place(2)
        ss2, rs2 = place(1), place(1)
        ctl = place(64).bitcast(I32)
        slot_token = place(NINFO).bitcast(I32)
        slot_weight = place(NINFO)
        gidx = place(4).bitcast(I32)
        sidx = place(2).bitcast(I32)
        qt = place(NT * D).rearrange("p (t g c) -> p t g c", t=NT, g=8)
        row = qt.rearrange("p t g c -> p t (g c)")
        maskb = place(KW)
        maska = place(2 * P)
        free_from = top[0]
        KC = ROWS + CACHE_B
        ktb = place(4 * KC).rearrange("p (g c) -> p g c", g=4)
        KCA = ROWS + CACHE_A
        kta = place(KCA)
        vb = place((NT + 2) * 512).rearrange("p (t c) -> p t c", t=NT + 2)
        va = place((NT + 1) * P).rearrange("p (t c) -> p t c", t=NT + 1)
        region = top[0]
        w_in = place(KD * sum(CHUNK))
        xt = place(2 * D).rearrange("p (b k c) -> p b k c", b=2, k=KD)
        xr = place(2 * D).rearrange("p (b c) -> p b c", b=2)
        z = place(2 * 1664).rearrange("p (b c) -> p b c", b=2)
        sq = place(1664)
        parts = xr[:, 1].rearrange("p (b c) -> p b c", b=2)
        top[0] = region
        bm = place(HEADS * KW).rearrange("p (h c) -> p h c", h=HEADS)
        w_out = place(KD * D).rearrange("p (k c) -> p k c", k=KD)
        sp = place(4 * KW).rearrange("p (b c) -> p b c", b=4)
        pt = place(2 * KW).rearrange("p (b c) -> p b c", b=2)
        ot = place(D).rearrange("p (k c) -> p k c", k=KD)
        h2 = place(2 * D).rearrange("p (b c) -> p b c", b=2)
        h2t = place(D).rearrange("p (k c) -> p k c", k=KD)
        xc = place(2 * D).rearrange("p (b c) -> p b c", b=2)
        g_o = place(D)
        g2 = place(D)
        wr = place(KD * NR).rearrange("p (k c) -> p k c", k=KD)
        lt = place(P)
        sum_c = place(P)
        junk = place(D)
        top[0] = free_from
        c_tri32 = place(NE * NE).rearrange("p (a b) -> p a b", a=NE)
        c_steps = place(9)
        c_block = place(NINFO)
        c_iota = place(NE)
        c_valid = place(NT)
        c_far = place(NT)
        c_token = place(NT * 2).rearrange("p (t k) -> p t k", k=2)
        c_row, c_part = place(P), place(1)
        tri = place(64).bitcast(BF16)
        ones = place(64).bitcast(BF16)

        def rt(n):
            return place(NT * n).rearrange("p (t c) -> p t c", t=NT)
        gmx, gsum, gp, idx, v1, v2, e12 = (rt(1) for _ in range(7))
        w12 = rt(2)
        geq, goh, gex = rt(NG), rt(NG), rt(NG)
        m32, eq, oh1, oh2, m2 = (rt(NE) for _ in range(5))
        mb = place(NT * NE // 2).bitcast(BF16).rearrange("p (t c) -> p t c", t=NT)
        cntv = place(NE)
        cmp9 = place(NE * 9).rearrange("p (a b) -> p a b", b=9)
        nblk, excl, incl, basev = place(NE), place(NE), place(NE), place(NE)
        prod = place(NE * NE).rearrange("p (a b) -> p a b", a=NE)
        cmpb, bexp = place(NE), place(1)
        ctlf = place(64)
        slots = place(NT * 2).rearrange("p (t k) -> p t k", k=2)
        sloti = place(NT * 2).bitcast(I32).rearrange("p (t k) -> p t k", k=2)
        slotr = place(NT * 2).bitcast(I32).rearrange("p (t k) -> p t k", k=2)
        slotb = place(NT * 2).bitcast(I32).rearrange("p (t k) -> p t k", k=2)
        slotrf = place(NT * 2).rearrange("p (t k) -> p t k", k=2)
        slotbf = place(NT * 2).rearrange("p (t k) -> p t k", k=2)
        in_row = place(2 * NT * P).rearrange("p (n c) -> p n c", n=2 * NT)
        in_block = place(2 * NT * 2 * NINFO).rearrange("p (n a c) -> p n a c", n=2 * NT, a=2)
        hot_block = place(2 * NT * NINFO).rearrange("p (n c) -> p n c", n=2 * NT)
        rtop = top[0]
        assert rtop <= region
        dtop = [free_from]

        def dplace(n):
            dtop[0] += n
            return place(n, dtop[0] - n)
        wx = [dplace(EW) for _ in range(4)][::-1]
        assert rtop <= free_from + 2 * EW
        xg = dplace(4 * D).rearrange("p (b c) -> p b c", b=4)
        xgt = dplace(2 * D).rearrange("p (b k c) -> p b k c", b=2, k=KD)
        yb = dplace(4 * D).rearrange("p (b c) -> p b c", b=4)
        sil = dplace(FF).rearrange("p (b c) -> p b c", b=2)
        hd = dplace(FF).rearrange("p (b c) -> p b c", b=2)
        hdt = dplace(FF).rearrange("p (b c) -> p b c", b=2)

        def bank(n, a=0, b=512):
            return ps[:, n * 512 + a:n * 512 + b]
        o_ps = bank(5)
        SCORES_AT = (0, 512)

        h2d = nc.dram_tensor("h2_rows", [ROWS, D], F32).ap()

        s_const = sem("constants_loaded")
        s_win = [sem(f"w_in{c}_loaded") for c in range(5)]
        s_win0b = sem("w_in0_second_half_loaded")
        s_gain = sem("norm1_loaded")
        s_suma = sem("sum_matrix_loaded")
        s_xt = [sem(f"xt{j}_loaded") for j in range(2)]
        s_xr = [sem(f"xrow{j}_loaded") for j in range(2)]
        s_cache = sem("caches_loaded")
        s_mask = sem("masks_loaded")
        s_bload = sem("bias_loaded")
        s_cload = sem("stage_c_weights_loaded")
        s_xc = [sem(f"residual{j}_loaded") for j in range(2)]
        s_rload = sem("routing_constants_loaded")
        s_xg = sem("xt_scaled")
        s_eps = sem("eps_ready")
        s_ss26 = sem("head_squares_summed")
        s_rs26 = sem("head_rstd_ready")
        s_ssx = sem("x_squares_summed")
        s_rsx = sem("x_rstd_ready")
        s_z = sem("z_chunks_made")
        s_zev = sem("z_chunks_copied")
        s_zq = [sem(f"sample_z_part{q}_made") for q in range(4)]
        s_zpc = sem("sample_z_parts_copied")
        s_zn = sem("z_normed")
        s_tr = sem("z_transposed")
        s_tea = sem("transposes_copied_by_act")
        s_tev = sem("transposes_copied_by_dve")
        s_qk = sem("scores_made")
        s_sp = sem("scores_biased")
        s_p = sem("probs_ready")
        s_pt = sem("probs_transposed")
        s_ptv = sem("probs_t_copied_by_dve")
        s_pta = sem("probs_t_copied_by_act")
        s_pv = sem("heads_summed")
        s_es = sem("sinks_exp")
        s_nsk = sem("sinks_shifted")
        s_on = sem("mixer_out_divided")
        s_so = sem("mixer_squares_summed")
        s_og = sem("mixer_out_normed")
        s_t1 = sem("mixer_out_transposed")
        s_ota = sem("ot_copied_by_act")
        s_otv = sem("ot_copied_by_dve")
        s_pq = [sem(f"sample_part{q}_projected") for q in range(4)]
        s_ppa = sem("sample_parts_copied_by_act")
        s_ppv = sem("sample_parts_copied_by_dve")
        s_op = sem("out_projected")
        s_x2 = sem("residual_added")
        s_s2 = sem("residual_squares_summed")
        s_h2 = sem("h2_ready")
        s_h2o = [sem(f"h2_stored{j}") for j in range(2)]
        s_t2 = sem("h2_transposed")
        s_h2a = sem("h2t_copied_by_act")
        s_h2v = sem("h2t_copied_by_dve")
        s_r = sem("logits_t_made")
        s_lt = sem("logits_t_copied")
        s_lg = sem("logits_transposed")
        s_rv = sem("logits_copied")
        s_gx = sem("group_shifted")
        s_gxe = sem("group_exp")
        s_v12 = sem("top2_difference")
        s_v12e = sem("top2_exp")
        s_mb = sem("membership_ready")
        s_cum = sem("positions_counted")
        s_ctl = sem("block_experts_ready")
        s_bx1 = sem("block_experts_counted")
        s_bx2 = sem("block_experts_in_a_row")
        s_in = sem("slot_masks_made")
        s_tab = sem("slot_tables_made")
        s_slot = sem("slot_tables_ready")
        s_x2o = sem("residual_stored")
        s_w = [[sem(f"expert{j}_{part}_loaded") for part in ("half0", "half1", "down")] for j in range(4)]
        s_g = [sem(f"rows_gathered{j}") for j in range(4)]
        s_gi = sem("indices_copied")
        s_xgz = sem("gather_buffers_cleared")
        s_bx = sem("rows_transposed")
        s_xa = sem("rows_t_copied_by_act")
        s_xv = sem("rows_t_copied_by_dve")
        s_gu = sem("gate_up_made")
        s_sil = sem("silu_ready")
        s_h = sem("hidden_ready")
        s_ht = sem("hidden_transposed")
        s_hta = sem("hidden_t_copied")
        s_y = sem("expert_out_made")
        s_ya = sem("expert_out_copied_by_act")
        s_yv = sem("expert_out_copied_by_dve")
        s_add = sem("expert_out_added")
        s_kv = sem("states_stored")
        s_dve = sem("dve_own")
        s_act = sem("act_own")
        s_pool = sem("pool_own")

        C_TR, C_H = 5, 3

        units = [(t, m, h) for t in range(NT) for h in range(HEADS) for m in (0, 1)]
        NU = len(units)

        def unit_info(u):
            t, m, h = units[u]
            segs = tile_keys(t)[m]
            tiles, c = [], 0
            for col, n in segs:
                for k in range(0, n, P):
                    tiles.append((c + k, (col + k) // P, min(P, n - k)))
                c += n
            return t, m, h, segs, tiles, c

        def stat_at(m, h):
            return h // 4 * 8 + m * 4 + h % 4

        CHOICE_AFTER = (NU + 15, NU + 16, NU + 18)

        def first_bias(t, m):
            if t == NT - 1:
                return 0 if m == 0 else 2 * P
            return ((1 - min(t, 1)) if m == 0 else (4 - min(t, 4))) * P

        def pieces(do, u):
            for t in (u // 16 - 2, u // 16 - 1):
                if 0 <= t < NT:
                    do(t, u - 16 * (t + 1))

        block = ctx.enter_context(nc.Block())

        @block.sync
        def _(sp_):
            def load_x(t, j):
                sp_.dma_start(xt[:, j], d["xT"][t]).then_inc(s_xt[j], 16)
                sp_.dma_start(xr[:, j], d["x"][t]).then_inc(s_xr[j], 16)

            load_x(0, 0)
            with sp_.Fori(0, 4) as i:
                for j in range(2):
                    t = i * 2 + j
                    sp_.wait_ge(s_z, i * 10 + (5 * j + 1))
                    sp_.wait_ge(s_ssx, i * 10 + (5 * j + 1))
                    load_x(t + 1, 1 - j)
            sp_.wait_ge(s_z, 1 + 5 * (NT - 1) + 2)
            sp_.dma_start(bm, d["bias"]).then_inc(s_bload, 16)
            sp_.wait_ge(s_z, 1 + 5 * NT)
            sp_.wait_ge(s_ssx, 1 + 5 * NT)
            sp_.wait_ge(s_zn, NT)
            sp_.wait_ge(s_tr, C_TR + 4 * NT)
            sp_.dma_start(g_o, d["g_o"].partition_broadcast(P)).then_inc(s_cload, 16)
            sp_.dma_start(w_out, d["w_out"]).then_inc(s_cload, 16)
            sp_.dma_start(g2, d["g2"].partition_broadcast(P)).then_inc(s_cload, 16)
            sp_.dma_start(wr, d["wr"]).then_inc(s_cload, 16)
            sp_.dma_start(sum_c, d["sum4"]).then_inc(s_cload, 16)
            sp_.wait_ge(s_tea, 2 + 2 * NT)
            sp_.wait_ge(s_tev, 2 + 2 * NT)
            sp_.wait_ge(s_zev, 5 + 5 * NT)
            sp_.dma_start(o["kb_p"], ktb[:, :, SEQ - 512:SEQ]).then_inc(s_kv, 16)
            sp_.dma_start(o["ka_p"], kta[:, SEQ - P:SEQ]).then_inc(s_kv, 16)
            sp_.dma_start(o["vb_p"], vb[:, 4:8, :]).then_inc(s_kv, 16)
            sp_.dma_start(o["va_p"], va[:, 7, :]).then_inc(s_kv, 16)
            sp_.dma_start(o["kb_s"], ktb[:, :, SEQ:SEQ + DEC]).then_inc(s_kv, 16)
            sp_.dma_start(o["ka_s"], kta[:, SEQ:SEQ + DEC]).then_inc(s_kv, 16)
            sp_.dma_start(o["vb_s"], vb[0:DEC, 8, :]).then_inc(s_kv, 16)
            sp_.dma_start(o["va_s"], va[0:DEC, 8, :]).then_inc(s_kv, 16)
            def store_rows(t):
                sp_.wait_ge(s_x2, 2 * (t + 1))
                sp_.dma_start(o["y"][t * P:(t + 1) * P, :], row[:, t]).then_inc(s_x2o, 16)
                sp_.wait_ge(s_h2, t + 1)
                sp_.dma_start(h2d[t * P:(t + 1) * P, :], h2[:, t % 2]).then_inc(s_h2o[t % 2], 16)

            for t in range(NT):
                if t >= 2:
                    sp_.wait_ge(s_x2, 2 * (t - 1))
                sp_.dma_start(xc[:, t % 2], d["x"][t]).then_inc(s_xc[t % 2], 16)
                if t >= 1:
                    store_rows(t - 1)
            sp_.wait_ge(s_pv, NU)
            sp_.wait_ge(s_kv, 16 * 8)
            for dst, name in ((c_tri32, "tri32"), (c_steps, "steps"), (c_block, "block"), (c_iota, "iota")):
                sp_.dma_start(dst, d[name].partition_broadcast(P)).then_inc(s_rload, 16)
            for dst, name in ((c_valid, "valid"), (c_far, "far"), (c_token, "token"), (tri, "tri"), (ones, "ones")):
                sp_.dma_start(dst, d[name]).then_inc(s_rload, 16)
            sp_.dma_start(c_row, d["row"].partition_broadcast(P)).then_inc(s_rload, 16)
            sp_.dma_start(c_part, d["part"]).then_inc(s_rload, 16)
            store_rows(NT - 1)
            sp_.wait_ge(s_ctl, 1)
            nb = sp_.value_load(ctl[0:1, NINFO:NINFO + 1], min_val=17, max_val=NBLOCK)
            with sp_.Fori(0, NBLOCK // 4) as i:
                for j in range(4):
                    with sp_.If(i * 4 + j < nb):
                        e = sp_.value_load(ctl[0:1, bass.ds(i * 4 + j, 1)], min_val=0, max_val=NE - 1)
                        if j == 2:
                            sp_.wait_ge(s_slot, 1)
                            sp_.wait_ge(s_g[1], 16)
                        sp_.wait_ge(s_y, i * 8 + 2 * j + 2)
                        for part, (c0, c1) in enumerate(W_PART):
                            sp_.dma_start(wx[j][:, c0:c1], d["wexp"][bass.ds(e, 1), :, c0:c1].rearrange("a p c -> p (a c)")
                                          ).then_inc(s_w[j][part], 16)

        @block.gpsimd
        def _(pool):
            nc.gpsimd.memset(eps, EPS).then_inc(s_eps, 1)
            pool.wait_ge(s_gain, 16)
            gain = g1.unsqueeze(2).broadcast_to([P, KD, P])

            def scale_x(wait, j):
                pool.wait_ge(s_xt[j], wait)
                nc.gpsimd.tensor_tensor(xt[:, j], xt[:, j], gain, ALU.mult).then_inc(s_xg, 1)

            scale_x(16, 0)
            with pool.Fori(0, 4) as i:
                scale_x(i * 16 + 16, 1)
                scale_x(i * 16 + 32, 0)
            pool.wait_ge(s_pv, NU)
            pool.wait_ge(s_rv, NT)
            pool.wait_ge(s_h2o[0], 16 * 5)
            pool.wait_ge(s_h2o[1], 16 * 4)
            nc.gpsimd.memset(xg, 0.0).then_inc(s_xgz, 1)
            pool.dma_start(yb[:, 0], d["x"][0]).then_inc(s_add, 64)
            pool.wait_ge(s_add, 64)
            pool.wait_ge(s_slot, 1)
            nb = pool.value_load(ctl[0:1, NINFO:NINFO + 1], min_val=17, max_val=NBLOCK)
            pool.wait_ge(s_xgz, 1)
            pool.wait_ge(s_x2o, 16 * NT)
            chain = Chain(pool, s_pool)
            row_bound = pool.to_reg(ROWS - 1)

            def gather(b, j):
                chain.link(nc.gpsimd.tensor_copy(gidx[:, j:j + 1], slot_token[:, bass.ds(b, 1)]))
                pool.sem_inc(s_gi, 1)
                pool.indirect_dma_start(
                    out=xg[:, j], out_offset=None, in_=h2d,
                    in_offset=bass.IndirectOffsetOnAxis(ap=gidx[:, j:j + 1], axis=0),
                    bounds_check=row_bound, oob_is_err=False).then_inc(s_g[j], 16)

            for b in range(3):
                gather(b, b)
            with pool.Fori(0, NBLOCK // 4) as i:
                chain.enter(i, 8)
                for j in range(4):
                    b = i * 4 + j
                    with pool.If(b < nb):
                        pool.wait_ge(s_bx, b + 2)
                        gather(b + 3, (j + 3) % 4)
                        pool.wait_ge(s_ya, b + 2)
                        pool.wait_ge(s_yv, b + 2)
                        chain.link(nc.gpsimd.tensor_copy(sidx[:, j % 2:j % 2 + 1], slot_token[:, bass.ds(b, 1)]))
                        pool.wait_ge(s_add, i * 64 + (16 * j + 64))
                        pool.sem_inc(s_gi, 1)
                        pool.indirect_dma_start(
                            out=o["y"], out_offset=bass.IndirectOffsetOnAxis(ap=sidx[:, j % 2:j % 2 + 1], axis=0),
                            in_=yb[:, j], in_offset=None, bounds_check=row_bound,
                            oob_is_err=False, compute_op=ALU.add).then_inc(s_add, 16)
            added = pool.value_load(ctl[0:1, NINFO + 1:NINFO + 2], min_val=16, max_val=16 * (NBLOCK + 4))
            pool.wait_ge(s_add, added)
            pool.wait_ge(s_kv, 16 * 8)

        @block.scalar
        def _(act):
            act.dma_start(g1, d["g1"]).then_inc(s_gain, 16)
            for c in range(5):
                a, n = CHUNK_AT[c], KD * CHUNK[c]
                if c == 0:
                    act.dma_start(w_in[:, 0:n // 2], d["w_in"][:, 0:n // 2]).then_inc(s_win[0], 16)
                    act.dma_start(w_in[:, n // 2:n], d["w_in"][:, n // 2:n]).then_inc(s_win0b, 16)
                else:
                    act.dma_start(w_in[:, a:a + n], d["w_in"][:, a:a + n]).then_inc(s_win[c], 16)
                if c == 0:
                    act.dma_start(ident, d["ident"]).then_inc(s_const, 16)
                    act.dma_start(g64, d["g64"].partition_broadcast(P)).then_inc(s_const, 16)
                    act.dma_start(rope, d["rope"]).then_inc(s_const, 16)
                    act.dma_start(sinks, d["sinks"].partition_broadcast(P)).then_inc(s_const, 16)
                    act.dma_start(rbias, d["rbias"].partition_broadcast(P)).then_inc(s_const, 16)
            act.dma_start(sum_a, d["sum4"]).then_inc(s_suma, 16)
            act.dma_start(maska, d["maska"]).then_inc(s_mask, 16)
            act.dma_start(maskb, d["maskb"]).then_inc(s_mask, 16)
            act.dma_start(ktb[:, :, ROWS:], d["ckb"]).then_inc(s_cache, 16)
            act.dma_start(kta[:, ROWS:], d["cka"]).then_inc(s_cache, 16)
            act.dma_start(vb[:, NT:, :], d["cvb"]).then_inc(s_cache, 16)
            act.dma_start(va[:, NT, :], d["cva"]).then_inc(s_cache, 16)
            chain = Chain(act, s_act)
            nc.scalar.preload_act_table_set("natural_log_exp_and_others")
            act.wait_ge(s_eps, 1)

            def rstd(out, ms):
                chain.link(nc.scalar.activation(out, ms, ACT.Ln, bias=eps))
                return nc.scalar.activation(out, out, ACT.Exp, scale=-0.5)

            act.sem_inc(s_zev, 5)
            act.sem_inc(s_tea, 2)
            act.sem_inc(s_ssx, 1)

            def square_x(wait, sq1, j):
                act.wait_ge(s_xr[j], wait)
                nc.scalar.activation(xr[:, j], xr[:, j], ACT.Square, scale=D ** -0.5,
                                     accum_out=ssx[:, j:j + 1]).then_inc(s_ssx, 5)
                act.wait_ge(s_ssx, sq1)
                rstd(rsx[:, j:j + 1], ssx[:, j:j + 1]).then_inc(s_rsx, 1)

            def part_out(c):
                for q in range(4):
                    act.wait_ge(s_zq[q], c + 1)
                if c >= 2:
                    act.wait_ge(s_z, 5 * (NT - 1) + c)
                nc.scalar.activation(parts[:, c % 2, 0:CHUNK[c]], bank(5 + c % 2, 0, CHUNK[c]), ACT.Copy).then_inc(s_zpc, 1)

            def chunks_out(t5, t4, t1, tt, j):
                act.wait_ge(s_rsx, t1)
                act.wait_ge(s_tr, t4)
                vbt = vb[:, tt, :] if isinstance(tt, int) else vb[:, bass.ds(tt, 1), :].rearrange("p a c -> p (a c)")
                vat = va[:, tt, :] if isinstance(tt, int) else va[:, bass.ds(tt, 1), :].rearrange("p a c -> p (a c)")
                for c, dst in enumerate((z[:, j, 0:512], None, z[:, j, 640:1152], z[:, j, 1152:1664], vbt)):
                    if isinstance(tt, int) and tt == NT - 1:
                        for n in ((0, 1) if c == 0 else (c + 1,)):
                            if n < 5:
                                part_out(n)
                    act.wait_ge(s_z, t5 + c + 2)
                    if c == 1:
                        nc.scalar.activation(z[:, j, 512:640], bank(1, 0, 128), ACT.Copy, scale=rsx[:, j:j + 1])
                        ins = nc.scalar.activation(vat, bank(1, 128, 256), ACT.Copy, scale=rsx[:, j:j + 1])
                    else:
                        ins = nc.scalar.activation(dst, bank(Z_BANK[c]), ACT.Copy, scale=rsx[:, j:j + 1])
                    ins.then_inc(s_zev, 1)

            def heads_rstd(t1):
                act.wait_ge(s_ss26, t1)
                rstd(rs26, ss26).then_inc(s_rs26, 1)

            def transposes_out(t4, tt, col):
                act.wait_ge(s_tr, t4 + C_TR + 1)
                q = qt[:, tt, 0:4, :] if isinstance(tt, int) else qt[:, bass.ds(tt, 1), 0:4, :].rearrange("p a g c -> p (a g) c")
                nc.scalar.activation(q, bank(5).rearrange("p (g c) -> p g c", g=4), ACT.Copy,
                                     scale=HD ** -0.5).then_inc(s_tea, 1)
                act.wait_ge(s_tr, t4 + C_TR + 2)
                nc.scalar.activation(ktb[:, :, bass.ds(col, P)], bank(6).rearrange("p (g c) -> p g c", g=4),
                                     ACT.Copy).then_inc(s_tea, 1)

            square_x(16, 6, 0)
            chunks_out(0, C_TR - 4, 1, 0, 0)
            heads_rstd(1)

            def two_tiles(i):
                for j in range(2):
                    square_x(i * 16 + (16 if j == 0 else 32), i * 10 + (5 * j + 11), 1 - j)
                    chunks_out(i * 10 + 5 * (j + 1), i * 8 + (4 * j + C_TR), i * 2 + (j + 2), i * 2 + (j + 1), 1 - j)
                    transposes_out(i * 8 + 4 * j, i * 2 + j, i * 256 + j * P)
                    heads_rstd(i * 2 + (j + 2))

            with act.Fori(0, 3) as i:
                chain.enter(i, 4)
                two_tiles(i)
                chain.leave(3)
            two_tiles(3)
            transposes_out(4 * (NT - 1), NT - 1, (NT - 1) * P)

            def copy_pt(u):
                _, _, _, _, tiles, _ = unit_info(u)
                cut = (len(tiles) + 1) // 2
                act.wait_ge(s_pt, u + 1)
                rest = tiles[cut:]
                if not rest:
                    act.sem_inc(s_pta, 1)
                    return
                if u >= 2:
                    act.wait_ge(s_pv, u - 1)
                c0 = cut * P
                full = [x for x in rest if x[2] == P]
                ins = None
                if full:
                    c1 = c0 + len(full) * P
                    ins = nc.scalar.activation(pt[:, u % 2, c0:c1], bank(4, 0, c1 - c0), ACT.Copy)
                    c0 = c1
                if len(full) < len(rest):
                    n = rest[-1][2]
                    ins = nc.scalar.activation(pt[0:n, u % 2, c0:c0 + P], bank(4, len(full) * P, len(full) * P + P)[0:n],
                                               ACT.Copy)
                ins.then_inc(s_pta, 1)

            def squares_out(t):
                act.wait_ge(s_on, 2 * (t + 1))
                if t >= 1:
                    act.wait_ge(s_og, 2 * t)
                for m in range(2):
                    ins = nc.scalar.activation(junk[:, 512 * m:512 * m + 512], row[:, t, 512 * m:512 * m + 512], ACT.Square,
                                               scale=512 ** -0.5, accum_out=sso[:, m:m + 1])
                chain.link(ins)
                rstd(rso, sso).then_inc(s_so, 1)

            def act_pieces(t, g):
                if g == 6:
                    act.wait_ge(s_t1, 2 * t + 1)
                    nc.scalar.activation(ot[:, 0:4], bank(6).rearrange("p (g c) -> p g c", g=4), ACT.Copy).then_inc(s_ota, 1)
                if t == NT - 1 and g == 7:
                    for q in range(4):
                        act.wait_ge(s_pq[q], 1)
                    nc.scalar.activation(junk[:, 0:512], bank(6), ACT.Copy).then_inc(s_ppa, 1)
                if g == 15:
                    act.wait_ge(s_x2, 2 * (t + 1))
                    chain.link(nc.scalar.activation(junk, row[:, t], ACT.Square, scale=D ** -0.5, accum_out=ss2))
                    rstd(rs2, ss2).then_inc(s_s2, 1)
                if g == 18:
                    act.wait_ge(s_t2, 2 * t + 1)
                    nc.scalar.activation(h2t[:, 0:4], bank(6).rearrange("p (g c) -> p g c", g=4), ACT.Copy).then_inc(s_h2a, 1)

            for u in range(NU):
                t, m, h, segs, tiles, width = unit_info(u)
                k = u % 16
                if u >= 3:
                    copy_pt(u - 3)
                act.wait_ge(s_sp, u + 1)
                c = stat_at(m, h)
                nc.scalar.activation(sp[:, u % 4, 0:width], sp[:, u % 4, 0:width], ACT.Exp,
                                     bias=negm[:, t % 2, c:c + 1], accum_out=psum_e[:, t % 2, c:c + 1]).then_inc(s_p, 1)
                if k % 8 == 7:
                    half = k // 8
                    act.wait_ge(s_nsk, 2 * t + half + 1)
                    part = esink[:, 4 * half:4 * half + 4]
                    nc.scalar.activation(part, part, ACT.Exp).then_inc(s_es, 1)
                if k == 3 and t >= 1:
                    squares_out(t - 1)
                pieces(act_pieces, u)
            for u in range(NU - 3, NU):
                copy_pt(u)
            squares_out(NT - 1)
            for u in range(NU, NU + 22):
                pieces(act_pieces, u)

            for n, (t0, t1) in enumerate(((0, NT - 1), (NT - 1, NT))):
                act.wait_ge(s_gx, n + 1)
                nc.scalar.activation(gex[:, t0:t1], gex[:, t0:t1], ACT.Exp).then_inc(s_gxe, 1)
                act.wait_ge(s_v12, n + 1)
                nc.scalar.activation(e12[:, t0:t1], e12[:, t0:t1], ACT.Exp).then_inc(s_v12e, 1)

            act.sem_inc(s_ya, 1)
            nc.scalar.preload_act_table(ACT.Silu)
            act.wait_ge(s_slot, 1)
            nb = act.value_load(ctl[0:1, NINFO:NINFO + 1], min_val=17, max_val=NBLOCK)

            def rows_t_out(b3, jj):
                act.wait_ge(s_bx, b3)
                nc.scalar.activation(xgt[:, jj, 0:4], bank(2).rearrange("p (g c) -> p g c", g=4), ACT.Copy).then_inc(s_xa, 1)

            def hidden_t_out(made, f):
                act.wait_ge(s_ht, made)
                nc.scalar.activation(hdt[:, f], bank((4, 7)[f], 0, P), ACT.Copy).then_inc(s_hta, 1)

            rows_t_out(3, 0)
            with act.Fori(0, NBLOCK // 4) as i:
                for j in range(4):
                    b = i * 4 + j
                    with act.If(b < nb):
                        act.wait_ge(s_h, i * 8 + (2 * j + C_H))
                        for f in range(2):
                            act.wait_ge(s_gu, i * 8 + (2 * j + f + 1))
                            nc.scalar.activation(sil[:, f], bank(f, 0, P), ACT.Silu).then_inc(s_sil, 1)
                        hidden_t_out(i * 8 + (2 * j + 1), 0)
                        rows_t_out(i * 4 + (j + 4), (j + 1) % 2)
                        hidden_t_out(i * 8 + (2 * j + 2), 1)
                        act.wait_ge(s_y, i * 8 + (2 * j + 9))
                        act.wait_ge(s_add, i * 64 + (16 * j + 16))
                        nc.scalar.activation(yb[:, j, 0:512], bank(5), ACT.Copy).then_inc(s_ya, 1)

        @block.vector
        def _(dve):
            chain = Chain(dve, s_dve)
            link = chain.link
            dve.sem_inc(s_tev, 2)
            dve.wait_ge(s_const, 16 * 5)

            def norm_z(t5, tt, t1, j):
                dve.wait_ge(s_zev, t5 + 4 + 5)
                zj = z[:, j]
                zh = zj.rearrange("p (h c) -> p h c", c=HD)
                sqh = sq.rearrange("p (h c) -> p h c", c=HD)
                link(nc.vector.tensor_tensor(sq, zj, zj, ALU.mult))
                link(nc.vector.tensor_reduce(ss26, sqh, AXX, ALU.add))
                nc.vector.tensor_scalar(ss26, ss26, 1.0 / HD, None, ALU.mult).then_inc(s_ss26, 1)
                dve.wait_ge(s_rs26, t1)
                link(nc.vector.tensor_tensor(sqh, zh, rs26.unsqueeze(2).broadcast_to([P, 26, HD]), ALU.mult))
                for a, (h0, h1) in enumerate(((0, 8), (8, 10), (10, 18), (18, 26))):
                    ins = nc.vector.tensor_tensor(zh[:, h0:h1], sqh[:, h0:h1],
                                                  g64[:, a:a + 1, :].broadcast_to([P, h1 - h0, HD]), ALU.mult)
                link(ins)
                rp = rope[:, tt, :] if isinstance(tt, int) else rope[:, bass.ds(tt, 1), :].rearrange("p a c -> p (a c)")
                cos = rp[:, 0:8].unsqueeze(1).broadcast_to([P, 10, 8])
                sin = rp[:, 8:16].unsqueeze(1).broadcast_to([P, 10, 8])
                x1, x2 = zh[:, 0:10, 0:8], zh[:, 0:10, 8:16]
                tmp = sqh[:, 0:10]
                nc.vector.tensor_tensor(tmp[:, :, 0:8], x1, cos, ALU.mult)
                nc.vector.tensor_tensor(tmp[:, :, 8:16], x2, sin, ALU.mult)
                nc.vector.tensor_tensor(tmp[:, :, 16:24], x2, cos, ALU.mult)
                link(nc.vector.tensor_tensor(tmp[:, :, 24:32], x1, sin, ALU.mult))
                nc.vector.tensor_tensor(x1, tmp[:, :, 0:8], tmp[:, :, 8:16], ALU.subtract)
                nc.vector.tensor_tensor(x2, tmp[:, :, 16:24], tmp[:, :, 24:32], ALU.add).then_inc(s_zn, 1)

            def transposes_out(t4, tt, col):
                dve.wait_ge(s_tr, t4 + C_TR + 3)
                q = qt[:, tt, 4:8, :] if isinstance(tt, int) else qt[:, bass.ds(tt, 1), 4:8, :].rearrange("p a g c -> p (a g) c")
                nc.vector.tensor_scalar(q, bank(7).rearrange("p (g c) -> p g c", g=4), HD ** -0.5, None,
                                        ALU.mult).then_inc(s_tev, 1)
                dve.wait_ge(s_tr, t4 + C_TR + 4)
                nc.vector.tensor_copy(kta[:, bass.ds(col, P)], bank(4, 0, P)).then_inc(s_tev, 1)

            norm_z(0, 0, 1, 0)

            def two_tiles(i):
                for j in range(2):
                    dve.wait_ge(s_zn, i * 2 + (j + 1))
                    norm_z(i * 10 + 5 * (j + 1), i * 2 + (j + 1), i * 2 + (j + 2), 1 - j)
                    transposes_out(i * 8 + 4 * j, i * 2 + j, i * 256 + j * P)

            with dve.Fori(0, 3) as i:
                chain.enter(i, 10)
                two_tiles(i)
                chain.leave(3)
            two_tiles(3)
            transposes_out(4 * (NT - 1), NT - 1, (NT - 1) * P)

            dve.wait_ge(s_mask, 16 * 2)

            def copy_pt(u):
                _, _, _, _, tiles, _ = unit_info(u)
                cut = (len(tiles) + 1) // 2
                dve.wait_ge(s_pt, u + 1)
                if u >= 2:
                    dve.wait_ge(s_pv, u - 1)
                full = [x for x in tiles[:cut] if x[2] == P]
                assert len(full) == cut
                nc.vector.tensor_copy(pt[:, u % 2, 0:cut * P], bank(3, 0, cut * P)).then_inc(s_ptv, 1)

            def reciprocals(t, half):
                dve.wait_ge(s_p, 16 * t + 8 * (half + 1))
                dve.wait_ge(s_es, 2 * t + half + 1)
                s8 = psum_e[:, t % 2, 8 * half:8 * half + 8]
                r8 = rden[:, 8 * half:8 * half + 8]
                nc.vector.tensor_copy(r8[:, 4:8], s8[:, 4:8])
                link(nc.vector.tensor_tensor(r8[:, 0:4], s8[:, 0:4], esink[:, 4 * half:4 * half + 4], ALU.add))
                link(nc.vector.reciprocal(r8, r8))

            def divide(t, half):
                dve.wait_ge(s_pv, 16 * t + 8 * (half + 1))
                for m in range(2):
                    a, c = 512 * m + 256 * half, 8 * half + 4 * m
                    ins = nc.vector.tensor_tensor(row[:, t, a:a + 256].rearrange("p (h c) -> p h c", c=HD),
                                                  o_ps[:, 256 * m:256 * m + 256].rearrange("p (h c) -> p h c", c=HD),
                                                  rden[:, c:c + 4].unsqueeze(2).broadcast_to([P, 4, HD]), ALU.mult)
                ins.then_inc(s_on, 1)

            def norm_out(t):
                dve.wait_ge(s_so, t + 1)
                if t == 0:
                    dve.wait_ge(s_cload, 16 * 5)
                for m in range(2):
                    part = row[:, t, 512 * m:512 * m + 512]
                    nc.vector.scalar_tensor_tensor(part, part, rso[:, m:m + 1], g_o[:, 512 * m:512 * m + 512],
                                                   ALU.mult, ALU.mult).then_inc(s_og, 1)

            def dve_pieces(t, g):
                if g == 6:
                    dve.wait_ge(s_t1, 2 * t + 2)
                    nc.vector.tensor_copy(ot[:, 4:8], bank(7).rearrange("p (g c) -> p g c", g=4)).then_inc(s_otv, 1)
                if t == NT - 1 and g == 7:
                    for q in range(4):
                        dve.wait_ge(s_pq[q], 2)
                    nc.vector.tensor_copy(junk[:, 512:1024], bank(7)).then_inc(s_ppv, 1)
                if g in (11, 15):
                    n = (g - 11) // 4
                    dve.wait_ge(s_op, 2 * t + n + 1)
                    if n == 0:
                        dve.wait_ge(s_xc[t % 2], 16 * (t // 2 + 1))
                    nc.vector.tensor_tensor(row[:, t, 512 * n:512 * n + 512], bank(6 + n),
                                            xc[:, t % 2, 512 * n:512 * n + 512], ALU.add).then_inc(s_x2, 1)
                if g == 16:
                    dve.wait_ge(s_s2, t + 1)
                    if t >= 2:
                        dve.wait_ge(s_h2o[t % 2], 16 * (t // 2))
                        dve.wait_ge(s_t2, 2 * (t - 1))
                    nc.vector.scalar_tensor_tensor(h2[:, t % 2], row[:, t], rs2, g2, ALU.mult, ALU.mult).then_inc(s_h2, 1)
                if g == 18:
                    dve.wait_ge(s_t2, 2 * t + 2)
                    nc.vector.tensor_copy(h2t[:, 4:8], bank(7).rearrange("p (g c) -> p g c", g=4)).then_inc(s_h2v, 1)
                if g == 20:
                    dve.wait_ge(s_r, t + 1)
                    nc.vector.tensor_copy(lt[0:NR], bank(6, 0, P)[0:NR]).then_inc(s_lt, 1)
                if g == 21:
                    dve.wait_ge(s_lg, t + 1)
                    nc.vector.tensor_tensor(logits[:, t], bank(7, 0, NR), rbias, ALU.add).then_inc(s_rv, 1)

            for u in range(NU):
                t, m, h, segs, tiles, width = unit_info(u)
                k = u % 16
                c = stat_at(m, h)
                if t == 0 and m == 1:
                    if h == 0:
                        dve.wait_ge(s_bload, 16)
                    link(nc.vector.tensor_tensor(bm[:, h], bm[:, h], maskb, ALU.add))
                if u >= 3:
                    copy_pt(u - 3)
                dve.wait_ge(s_qk, u + 1)
                if u >= 4:
                    dve.wait_ge(s_pt, u - 3)
                b0 = first_bias(t, m)
                at = SCORES_AT[m]
                add = bm[:, h, b0:b0 + width] if m else maska[:, b0:b0 + width]
                link(nc.vector.tensor_tensor_reduce(
                    out=sp[:, u % 4, 0:width], in0=ps[:, at:at + width], in1=add, scale=1.0,
                    scalar=sinks[:, h:h + 1] if m == 0 else -3e38, op0=ALU.add, op1=ALU.max,
                    accum_out=mx[:, u % 2:u % 2 + 1]))
                nc.vector.tensor_scalar(negm[:, t % 2, c:c + 1], mx[:, u % 2:u % 2 + 1], -1.0, None,
                                        ALU.mult).then_inc(s_sp, 1)
                if k == 11:
                    divide(t, 0)
                if k == 3 and t >= 1:
                    divide(t - 1, 1)
                if k == 4 and t >= 1:
                    norm_out(t - 1)
                if k % 8 == 7:
                    half = k // 8
                    dve.wait_ge(s_sp, u + 1)
                    nc.vector.tensor_tensor(esink[:, 4 * half:4 * half + 4], sinks[:, 4 * half:4 * half + 4],
                                            negm[:, t % 2, 8 * half:8 * half + 4], ALU.add).then_inc(s_nsk, 1)
                if k == 9:
                    reciprocals(t, 0)
                if k == 1 and t >= 1:
                    reciprocals(t - 1, 1)
                pieces(dve_pieces, u)
            for u in range(NU - 3, NU):
                copy_pt(u)
            reciprocals(NT - 1, 1)
            divide(NT - 1, 1)
            norm_out(NT - 1)
            for u in range(NU, NU + 8):
                pieces(dve_pieces, u)

            dve.wait_ge(s_rload, 16 * 11)
            tt_, ts_, red = nc.vector.tensor_tensor, nc.vector.tensor_scalar, nc.vector.tensor_reduce

            def wide(x, n):
                return x.broadcast_to([P, x.shape[1], n])

            def top_one(values, best, scratch, at, hot, iota, n):
                link(red(best, values, AXX, ALU.max))
                link(tt_(scratch, values, wide(best, n), ALU.is_lt))
                link(ts_(scratch, scratch, 1000.0, None, ALU.mult))
                link(tt_(scratch, scratch, iota, ALU.add))
                link(red(at, scratch, AXX, ALU.min))
                link(tt_(hot, iota, wide(at, n), ALU.is_equal))

            def choose_group(t0, t1):
                dve.wait_ge(s_rv, t1)
                n = t1 - t0
                logit, gmx_, geq_, idx_, goh_, gex_, m32_ = (x[:, t0:t1] for x in (logits, gmx, geq, idx, goh, gex, m32))
                gl, el = logit[:, :, 0:NG], logit[:, :, NG:NR]
                top_one(gl, gmx_, geq_, idx_, goh_, c_iota[:, 0:NG].unsqueeze(1).broadcast_to([P, n, NG]), NG)
                tt_(gex_, gl, wide(gmx_, NG), ALU.subtract).then_inc(s_gx, 1)
                link(ts_(geq_, goh_, BIG, -BIG, ALU.mult, ALU.add))
                e4 = el.rearrange("p t (g e) -> p t g e", g=NG)
                m4 = m32_.rearrange("p t (g e) -> p t g e", g=NG)
                for g in range(NG):
                    ins = tt_(m4[:, :, g], e4[:, :, g], wide(goh_[:, :, g:g + 1], 8), ALU.mult)
                link(ins)
                for g in range(NG):
                    ins = tt_(m4[:, :, g], m4[:, :, g], wide(geq_[:, :, g:g + 1], 8), ALU.add)
                link(ins)

            def choose_first(t0, t1):
                m32_, v1_, eq_, idx_, oh1_, m2_ = (x[:, t0:t1] for x in (m32, v1, eq, idx, oh1, m2))
                top_one(m32_, v1_, eq_, idx_, oh1_, c_iota.unsqueeze(1).broadcast_to([P, t1 - t0, NE]), NE)
                link(ts_(m2_, oh1_, -2 * BIG, None, ALU.mult))
                link(tt_(m2_, m2_, m32_, ALU.add))

            def choose_second(t0, t1):
                v1_, eq_, idx_, oh1_, m2_, v2_, oh2_, e12_ = (x[:, t0:t1] for x in (v1, eq, idx, oh1, m2, v2, oh2, e12))
                top_one(m2_, v2_, eq_, idx_, oh2_, c_iota.unsqueeze(1).broadcast_to([P, t1 - t0, NE]), NE)
                tt_(e12_, v2_, v1_, ALU.subtract).then_inc(s_v12, 1)
                link(tt_(eq_, oh1_, oh2_, ALU.add))
                tt_(mb[:, t0:t1], eq_, wide(c_valid[:, t0:t1].unsqueeze(2), NE), ALU.mult).then_inc(s_mb, 1)

            for u in range(NU + 8, NU + 22):
                pieces(dve_pieces, u)
                if u in CHOICE_AFTER:
                    (choose_group, choose_first, choose_second)[CHOICE_AFTER.index(u)](0, NT - 1)
            for choose in (choose_group, choose_first, choose_second):
                choose(NT - 1, NT)
            dve.wait_ge(s_cum, 1)
            link(nc.vector.tensor_copy(cntv, ps[:, NT * NE:NT * NE + NE]))
            link(tt_(cmp9, cntv.unsqueeze(2).broadcast_to([P, NE, 9]),
                     c_steps.unsqueeze(1).broadcast_to([P, NE, 9]), ALU.is_gt))
            link(red(nblk, cmp9, AXX, ALU.add))
            link(tt_(prod, c_tri32, nblk.unsqueeze(1).broadcast_to([P, NE, NE]), ALU.mult))
            link(red(excl, prod, AXX, ALU.add))
            link(tt_(incl, excl, nblk, ALU.add))
            link(ts_(cmpb, incl, c_part, None, ALU.is_le))
            red(bexp, cmpb, AXX, ALU.add).then_inc(s_bx1, 1)
            dve.wait_ge(s_bx2, 1)
            link(ts_(ctlf[0:1, 0:NINFO], ps[0:1, 512:512 + NINFO], NE - 1.0, None, ALU.min))
            link(nc.vector.tensor_copy(ctlf[0:1, NINFO:NINFO + 1], incl[0:1, NE - 1:NE]))
            link(ts_(ctlf[0:1, NINFO + 1:NINFO + 2], incl[0:1, NE - 1:NE], 16.0, 64.0, ALU.mult, ALU.add))
            nc.vector.tensor_copy(ctl[0:1, 0:NINFO + 2], ctlf[0:1, 0:NINFO + 2]).then_inc(s_ctl, 1)
            link(ts_(basev, excl, float(P), None, ALU.mult))
            pos = ps[:, 0:NT * NE].rearrange("p (t c) -> p t c", t=NT)
            link(tt_(m32, pos, basev.unsqueeze(1).broadcast_to([P, NT, NE]), ALU.add))
            for k, oh in enumerate((oh1, oh2)):
                link(tt_(eq, oh, m32, ALU.mult))
                link(red(slots[:, :, k:k + 1], eq, AXX, ALU.add))
                link(tt_(slots[:, :, k:k + 1], slots[:, :, k:k + 1], c_far.unsqueeze(2), ALU.add))
            link(nc.vector.tensor_copy(sloti, slots))
            ts_(slotr, sloti, P - 1, None, ALU.bitwise_and)
            link(ts_(slotb, sloti, 7, None, ALU.logical_shift_right))
            nc.vector.tensor_copy(slotrf, slotr)
            link(nc.vector.tensor_copy(slotbf, slotb))
            dve.wait_ge(s_gxe, 2)
            link(red(gsum, gex, AXX, ALU.add))
            link(nc.vector.reciprocal(gp, gsum))
            dve.wait_ge(s_v12e, 2)
            link(ts_(v1, e12, 1.0, None, ALU.add))
            link(nc.vector.reciprocal(v1, v1))
            link(tt_(w12[:, :, 0:1], v1, gp, ALU.mult))
            link(tt_(w12[:, :, 1:2], w12[:, :, 0:1], e12, ALU.mult))
            for n0, n1 in ((0, NT - 1), (NT - 1, 2 * NT)):
                n = n1 - n0

                def pairs(x, c):
                    return x.rearrange("p t k -> p (t k)")[:, n0:n1].unsqueeze(2).broadcast_to([P, n, c])
                hot = hot_block[:, n0:n1]
                tt_(in_row[:, n0:n1], pairs(slotrf, P), c_row.unsqueeze(1).broadcast_to([P, n, P]), ALU.is_equal)
                link(tt_(hot, pairs(slotbf, NINFO), c_block.unsqueeze(1).broadcast_to([P, n, NINFO]), ALU.is_equal))
                tt_(in_block[:, n0:n1, 0], hot, pairs(c_token, NINFO), ALU.mult)
                tt_(in_block[:, n0:n1, 1], hot, pairs(w12, NINFO), ALU.mult).then_inc(s_in, 1)
            dve.wait_ge(s_tab, 1)
            ts_(slot_token, bank(1, 0, NINFO), float(FAR), None, ALU.add)
            nc.vector.tensor_copy(slot_weight, bank(1, NINFO, 2 * NINFO)).then_inc(s_slot, 1)

            dve.sem_inc(s_yv, 1)
            dve.sem_inc(s_h, C_H)
            dve.wait_ge(s_slot, 1)
            nb = dve.value_load(ctl[0:1, NINFO:NINFO + 1], min_val=17, max_val=NBLOCK)

            def rows_t_out(b3, jj):
                dve.wait_ge(s_bx, b3)
                nc.vector.tensor_copy(xgt[:, jj, 4:8], bank(3).rearrange("p (g c) -> p g c", g=4)).then_inc(s_xv, 1)

            rows_t_out(3, 0)
            with dve.Fori(0, NBLOCK // 4) as i:
                for j in range(4):
                    b = i * 4 + j
                    with dve.If(b < nb):
                        gate = slot_weight[:, bass.ds(b, 1)]
                        for f in range(2):
                            dve.wait_ge(s_sil, i * 8 + (2 * j + f + 1))
                            nc.vector.scalar_tensor_tensor(hd[:, f], bank(f, P, 2 * P), gate,
                                                           sil[:, f], ALU.mult, ALU.mult).then_inc(s_h, 1)
                        rows_t_out(i * 4 + (j + 4), (j + 1) % 2)
                        dve.wait_ge(s_y, i * 8 + (2 * j + 10))
                        dve.wait_ge(s_add, i * 64 + (16 * j + 16))
                        nc.vector.tensor_copy(yb[:, j, 512:1024], bank(6)).then_inc(s_yv, 1)

        @block.tensor
        def _(pe):
            mm = nc.tensor.matmul
            pe.sem_inc(s_z, 1)
            pe.sem_inc(s_tr, C_TR)
            pe.sem_inc(s_y, 8)
            pe.sem_inc(s_bx, 2)

            def project(t5, t1, j, first=False):
                pe.wait_ge(s_xg, t1)
                for c in range(5):
                    if first:
                        pe.wait_ge(s_win[c], 16)
                    pe.wait_ge(s_zev, t5 + {1: 5, 4: 7}.get(c, c + 1))
                    for k in range(KD):
                        if first and c == 0 and k == KD // 2:
                            pe.wait_ge(s_win0b, 16)
                        a = CHUNK_AT[c] + k * CHUNK[c]
                        ins = mm(bank(Z_BANK[c], 0, CHUNK[c]), xt[:, j, k, :], w_in[:, a:a + CHUNK[c]],
                                 start=(k == 0), stop=(k == KD - 1))
                    ins.then_inc(s_z, 1)

            def project_sample():
                pe.wait_ge(s_xg, NT)
                pe.wait_ge(s_suma, 16)
                pe.wait_ge(s_tea, 2 * NT - 2)

                def parts_of(c):
                    if c >= 2:
                        pe.wait_ge(s_zpc, c - 1)
                    for k in range(KD):
                        a, q = CHUNK_AT[c] + k * CHUNK[c], k % 4 * DEC
                        ins = mm(bank(5 + c % 2, 0, CHUNK[c])[q:q + DEC], xt[:, 0, k, 0:DEC], w_in[:, a:a + CHUNK[c]],
                                 start=(k < 4), stop=(k >= 4), tile_position=(0, q))
                        if k >= 4:
                            ins.then_inc(s_zq[k - 4], 1)

                def sum_of(c):
                    pe.wait_ge(s_zpc, c + 1)
                    pe.wait_ge(s_zev, 5 * (NT - 1) + {1: 5, 4: 7}.get(c, c + 1))
                    mm(bank(Z_BANK[c], 0, CHUNK[c]), sum_a, parts[:, c % 2, 0:CHUNK[c]], start=True, stop=True).then_inc(s_z, 1)

                parts_of(0)
                for c in range(5):
                    if c < 4:
                        parts_of(c + 1)
                    sum_of(c)

            def transposes(t2, t1, j):
                pe.wait_ge(s_zn, t1)
                for c0, n, bk, at, freed, v in ((0, 4, 5, 0, s_tea, 1), (1152, 4, 6, 0, s_tea, 2),
                                                (640, 4, 7, 0, s_tev, 1), (512, 1, 4, 0, s_tev, 2)):
                    pe.wait_ge(freed, t2 + v)
                    for g in range(n):
                        ins = nc.tensor.transpose(bank(bk, at + g * P, at + g * P + P), z[:, j, c0 + g * P:c0 + g * P + P], ident)
                    ins.then_inc(s_tr, 1)

            project(0, 1, 0, first=True)
            pe.wait_ge(s_const, 16 * 5)
            with pe.Fori(0, 3) as i:
                for j in range(2):
                    project(i * 10 + 5 * (j + 1), i * 2 + (j + 2), 1 - j)
                    transposes(i * 4 + 2 * j, i * 2 + (j + 1), j)
            project(5 * (NT - 2), NT - 1, 1)
            transposes(2 * (NT - 3), NT - 2, 0)
            project_sample()
            transposes(2 * (NT - 2), NT - 1, 1)
            transposes(2 * (NT - 1), NT, 0)

            def scores(u):
                if u >= NU:
                    return
                t, m, h, segs, tiles, width = unit_info(u)
                if u >= 2:
                    pe.wait_ge(s_sp, u - 1)
                half, g = (h // 4, h % 4) if m == 0 else (h % 2, 4 + h // 2)
                a = half * HD
                q = qt[a:a + HD, t, g, :]
                kt = kta[a:a + HD] if m == 0 else ktb[a:a + HD, g - 4]
                out0 = SCORES_AT[m]
                c, runs = 0, []
                for col, n in segs:
                    k = 0
                    while k < n:
                        at = out0 + c + k
                        step = min(n - k, 512 - at % 512)
                        runs.append((at, step, col + k))
                        k += step
                    c += n
                for at, step, col in runs:
                    ins = mm(ps[:, at:at + step], q, kt[:, col:col + step], start=True, stop=True)
                ins.then_inc(s_qk, 1)

            def transpose_probs(u):
                t, m, h, segs, tiles, width = unit_info(u)
                pe.wait_ge(s_p, u + 1)
                if u >= 1:
                    pe.wait_ge(s_ptv, u)
                    pe.wait_ge(s_pta, u)
                cut = (len(tiles) + 1) // 2
                for i, (c, _, n) in enumerate(tiles):
                    dst = bank(3, i * P, i * P + P) if i < cut else bank(4, (i - cut) * P, (i - cut) * P + P)
                    ins = nc.tensor.transpose(dst[0:n], sp[:, u % 4, c:c + n], ident)
                ins.then_inc(s_pt, 1)

            def values(u):
                t, m, h, segs, tiles, width = unit_info(u)
                pe.wait_ge(s_ptv, u + 1)
                pe.wait_ge(s_pta, u + 1)
                if u % 8 == 0 and u >= 8:
                    pe.wait_ge(s_on, u // 8)
                at = 256 * m + h % 4 * HD
                for i, (c, vt, n) in enumerate(tiles):
                    v = va[0:n, vt, (h // 4) * HD:(h // 4 + 1) * HD] if m == 0 else vb[0:n, vt, h * HD:(h + 1) * HD]
                    ins = mm(o_ps[:, at:at + HD], pt[0:n, u % 2, i * P:i * P + P], v,
                             start=(i == 0), stop=(i == len(tiles) - 1))
                ins.then_inc(s_pv, 1)

            def pe_pieces(t, g):
                if g == 5:
                    pe.wait_ge(s_og, 2 * (t + 1))
                    if t >= 1:
                        pe.wait_ge(s_lt, t)
                    for c in range(KD):
                        if c == 4 and t >= 1:
                            pe.wait_ge(s_rv, t)
                        ins = nc.tensor.transpose(bank(6 + c // 4, c % 4 * P, c % 4 * P + P), row[:, t, c * P:c * P + P], ident)
                        if c % 4 == 3:
                            ins.then_inc(s_t1, 1)
                if t == NT - 1 and g == 7:
                    pe.wait_ge(s_ota, t + 1)
                    pe.wait_ge(s_otv, t + 1)
                    for n in range(2):
                        for c in range(KD):
                            q = c % 4 * DEC
                            ins = mm(bank(6 + n)[q:q + DEC], ot[:, c, 0:DEC], w_out[:, c, 512 * n:512 * n + 512],
                                     start=(c < 4), stop=(c >= 4), tile_position=(0, q))
                            if c >= 4:
                                ins.then_inc(s_pq[c - 4], 1)
                    for n in range(2):
                        pe.wait_ge((s_ppa, s_ppv)[n], 1)
                        mm(bank(6 + n), sum_c, junk[:, 512 * n:512 * n + 512], start=True, stop=True).then_inc(s_op, 1)
                if t < NT - 1 and 7 <= g < 15:
                    n, quarter = (g - 7) // 4, (g - 7) % 4
                    if g == 7:
                        pe.wait_ge(s_cload, 16 * 5)
                        pe.wait_ge(s_ota, t + 1)
                        pe.wait_ge(s_otv, t + 1)
                    for c in range(2 * quarter, 2 * quarter + 2):
                        ins = mm(bank(6 + n), ot[:, c], w_out[:, c, 512 * n:512 * n + 512], start=(c == 0), stop=(c == KD - 1))
                    if quarter == 3:
                        ins.then_inc(s_op, 1)
                if g == 17:
                    pe.wait_ge(s_h2, t + 1)
                    for c in range(KD):
                        ins = nc.tensor.transpose(bank(6 + c // 4, c % 4 * P, c % 4 * P + P), h2[:, t % 2, c * P:c * P + P], ident)
                        if c % 4 == 3:
                            ins.then_inc(s_t2, 1)
                if g == 19:
                    pe.wait_ge(s_h2a, t + 1)
                    pe.wait_ge(s_h2v, t + 1)
                    for c in range(KD):
                        ins = mm(bank(6, 0, P)[0:NR], wr[:, c], h2t[:, c], start=(c == 0), stop=(c == KD - 1))
                    ins.then_inc(s_r, 1)
                if g == 20:
                    pe.wait_ge(s_lt, t + 1)
                    nc.tensor.transpose(bank(7, 0, NR), lt[0:NR], ident[0:NR, 0:NR]).then_inc(s_lg, 1)

            pe.wait_ge(s_cache, 16 * 4)
            scores(0)
            for u in range(NU):
                scores(u + 1)
                if u >= 2:
                    transpose_probs(u - 2)
                if u >= 3:
                    values(u - 3)
                pieces(pe_pieces, u)
            for u in range(NU, NU + 3):
                if u < NU + 2:
                    transpose_probs(u - 2)
                values(u - 3)
            for u in range(NU, NU + 22):
                pieces(pe_pieces, u)

            pe.wait_ge(s_mb, 2)
            pe.wait_ge(s_rv, NT)
            for t in range(NT):
                for s in range(t + 1):
                    mm(ps[:, t * NE:t * NE + NE], tri if s == t else ones, mb[:, s], start=(s == 0), stop=(s == t))
            for s in range(NT):
                ins = mm(ps[:, NT * NE:NT * NE + NE], ones, mb[:, s], start=(s == 0), stop=(s == NT - 1))
            ins.then_inc(s_cum, 1)
            pe.wait_ge(s_bx1, 1)
            mm(ps[0:1, 512:512 + P], bexp, ident, start=True, stop=True).then_inc(s_bx2, 1)
            for n in range(2 * NT):
                if n in (0, NT - 1):
                    pe.wait_ge(s_in, 1 if n == 0 else 2)
                ins = mm(bank(1, 0, 2 * NINFO), in_row[:, n], in_block[:, n].rearrange("p a c -> p (a c)"),
                         start=(n == 0), stop=(n == 2 * NT - 1))
            ins.then_inc(s_tab, 1)

            pe.wait_ge(s_slot, 1)
            nb = pe.value_load(ctl[0:1, NINFO:NINFO + 1], min_val=17, max_val=NBLOCK)

            def rows_t(wait, jj):
                pe.wait_ge(s_g[jj], wait)
                for g in range(8):
                    ins = nc.tensor.transpose(bank(2 + g // 4, g % 4 * P, g % 4 * P + P), xg[:, jj, g * P:g * P + P], ident)
                ins.then_inc(s_bx, 1)

            def hidden_t(made, f):
                pe.wait_ge(s_h, made)
                nc.tensor.transpose(bank((4, 7)[f], 0, P), hd[:, f], ident).then_inc(s_ht, 1)

            rows_t(16, 0)
            with pe.Fori(0, NBLOCK // 4) as i:
                for j in range(4):
                    b = i * 4 + j
                    with pe.If(b < nb):
                        w = wx[j]
                        pe.wait_ge(s_xa, i * 4 + (j + 1))
                        pe.wait_ge(s_xv, i * 4 + (j + 1))
                        pe.wait_ge(s_h, i * 8 + (2 * j + C_H))
                        for f in range(2):
                            pe.wait_ge(s_w[j][f], i * 16 + 16)
                            for k in range(KD):
                                a = (f * KD + k) * FF
                                ins = mm(bank(f, 0, FF), xgt[:, j % 2, k], w[:, a:a + FF],
                                         start=(k == 0), stop=(k == KD - 1))
                            ins.then_inc(s_gu, 1)
                        hidden_t(i * 8 + (2 * j + 1 + C_H), 0)
                        rows_t(i * 16 + (32 if j == 3 else 16), (j + 1) % 4)
                        hidden_t(i * 8 + (2 * j + 2 + C_H), 1)
                        pe.wait_ge(s_w[j][2], i * 16 + 16)
                        pe.wait_ge(s_ya, i * 4 + (j + 1))
                        pe.wait_ge(s_yv, i * 4 + (j + 1))
                        for f in range(2):
                            pe.wait_ge(s_hta, i * 8 + (2 * j + 1 + f))
                            for n in range(2):
                                a = 2 * KD * FF + f * D + n * 512
                                ins = mm(bank(5 + n), hdt[:, f], w[:, a:a + 512], start=(f == 0), stop=(f == 1))
                                if f == 1:
                                    ins.then_inc(s_y, 1)


INS = ["xT", "x", "w_in", "g1", "ident", "g64", "rope", "sinks", "rbias", "ckb", "cka", "cvb", "cva", "bias", "maskb",
       "maska", "g_o", "w_out", "g2", "wr", "tri32", "steps", "block", "iota", "valid", "far", "token", "row", "part", "sum4",
       "tri", "ones", "wexp"]
OUTS = {"y": [ROWS, D], "ka_p": [P, P], "va_p": [P, P], "kb_p": [P, 4, 512], "vb_p": [P, 4, 512],
        "ka_s": [P, DEC], "va_s": [DEC, P], "kb_s": [P, 4, DEC], "vb_s": [DEC, 512]}


def kernel(**inputs):
    import ml_dtypes
    import concourse.bacc as bacc
    from concourse.bass_utils import run_bass_kernel_spmd

    a = {k: np.asarray(v) for k, v in inputs.items()}
    f32 = np.float32
    L = {}
    x = np.zeros((ROWS, D), f32)
    x[:SEQ] = a["x_prompt"][0]
    x[SEQ:SEQ + DEC] = a["x_sample"][0]
    L["x"] = x.reshape(NT, P, D)
    L["xT"] = np.ascontiguousarray(L["x"].reshape(NT, P, KD, P).transpose(0, 3, 2, 1))
    w = a["w_in"][0]
    pair = [p + 4 * s for p in range(4) for s in range(2)]
    wqa = w[:, 0:512].reshape(D, 8, HD)[:, pair].reshape(D, 512)
    parts = [wqa, w[:, 512:768], w[:, 768:1280], w[:, 1280:1792], w[:, 1792:2304]]
    L["w_in"] = np.concatenate([c.reshape(KD, P, -1).transpose(1, 0, 2).reshape(P, -1) for c in parts], axis=1)
    L["g1"] = a["norm1"][0].reshape(KD, P).T
    L["ident"] = np.eye(P, dtype=f32)
    L["g64"] = np.stack([a["q_norm_a"][0], a["k_norm_a"][0], a["q_norm_b"][0], a["k_norm_b"][0]])
    inv = f32(500000.0) ** (-np.arange(8, dtype=f32) / f32(8))
    pos = np.zeros(ROWS, f32)
    pos[:SEQ] = np.arange(SEQ)
    pos[SEQ:SEQ + DEC] = 256 + np.arange(DEC)
    ang = (pos[:, None] * inv[None, :]).astype(f32)
    L["rope"] = np.concatenate([np.cos(ang), np.sin(ang)], axis=1).astype(f32).reshape(NT, P, 16).transpose(1, 0, 2)
    L["sinks"] = a["sinks_a"][0]
    L["rbias"] = np.concatenate([a["b_router_group"][0], a["b_router_expert"][0].reshape(-1)])
    L["ckb"] = a["cache_b_k"][0, 0].reshape(CACHE_B, 4, P).transpose(2, 1, 0)
    L["cka"] = a["cache_a_k"][0, 0].reshape(CACHE_A, P).T
    L["cvb"] = a["cache_b_v"][0, 0].reshape(2, P, 512).transpose(1, 0, 2)
    L["cva"] = a["cache_a_v"][0, 0].reshape(P, P)
    dist = np.clip(np.arange(KW)[None, :] - 4 * P - np.arange(P)[:, None], -128, 128) + 128
    L["bias"] = a["rel_bias_b"][0][:, dist].transpose(1, 0, 2)
    late_q = (np.arange(P) >= 64)[:, None]
    old = late_q & (np.arange(P) < 64)[None, :]
    new = ~late_q & (np.arange(P) >= 64)[None, :]
    none = np.zeros((P, 3 * P), bool)
    L["maskb"] = np.where(np.concatenate([old, none, new], axis=1), f32(-BIG), f32(0))
    L["maska"] = np.where(np.concatenate([old, new], axis=1), f32(-BIG), f32(0))
    L["g_o"] = np.concatenate([a["out_norm_a"][0], a["out_norm_b"][0]])
    L["w_out"] = a["w_out"][0].reshape(KD, P, D).transpose(1, 0, 2)
    L["g2"] = a["norm2"][0]
    wr = np.concatenate([a["w_router_group"][0]] + [a["w_router_expert"][0, g] for g in range(NG)], axis=1)
    L["wr"] = wr.reshape(KD, P, NR).transpose(1, 0, 2)
    L["tri32"] = np.tril(np.ones((NE, NE), f32), -1)
    L["steps"] = np.arange(9, dtype=f32) * P
    L["block"] = np.arange(NINFO, dtype=f32)
    L["iota"] = np.arange(NE, dtype=f32)
    tok = np.arange(NT)[None, :] * P + np.arange(P)[:, None]
    real = tok < SEQ + DEC
    L["valid"] = real.astype(f32)
    L["far"] = np.where(real, 0, FAR).astype(f32)
    L["token"] = np.stack([tok - FAR, tok - FAR], axis=2).astype(f32)
    L["row"] = np.arange(P, dtype=f32)
    L["sum4"] = (np.arange(P)[:, None] % DEC == np.arange(P)[None, :]).astype(f32)
    L["part"] = np.arange(P, dtype=f32)[:, None]
    L["tri"] = np.triu(np.ones((P, P), f32), 1).astype(ml_dtypes.bfloat16)
    L["ones"] = np.ones((P, P), ml_dtypes.bfloat16)
    gu = [a[n][0].reshape(NE, KD, P, 2, P) for n in ("w_gate", "w_up")]
    gu = np.stack(gu, axis=4).transpose(0, 2, 3, 1, 4, 5).reshape(NE, P, -1)
    dn = a["w_down"][0].reshape(NE, 2, P, D).transpose(0, 2, 1, 3).reshape(NE, P, -1)
    L["wexp"] = np.concatenate([gu, dn], axis=2)

    nc = bacc.Bacc("TRN2", target_bir_lowering=False, num_devices=1)
    arrays, d, o = {}, {}, {}
    for name in INS:
        arr = np.ascontiguousarray(L[name])
        arrays["in_" + name] = arr
        d[name] = nc.dram_tensor("in_" + name, arr.shape, mybir.dt.from_np(arr.dtype), kind="ExternalInput").ap()
    for name, shape in OUTS.items():
        o[name] = nc.dram_tensor("out_" + name, shape, F32, kind="ExternalOutput").ap()
    build(nc, d, o)
    res = run_bass_kernel_spmd(nc, [arrays], core_ids=[0]).results[0]
    r = {name: np.asarray(res["out_" + name]).reshape(shape) for name, shape in OUTS.items()}

    def keys_b(k, n):
        return np.ascontiguousarray(k.transpose(2, 1, 0)).reshape(1, 1, n, 8, HD)

    return (r["y"][None, :SEQ], r["y"][None, SEQ:SEQ + DEC],
            np.ascontiguousarray(r["ka_p"].T).reshape(1, 1, P, 2, HD), r["va_p"].reshape(1, 1, P, 2, HD),
            keys_b(r["kb_p"], 512), np.ascontiguousarray(r["vb_p"].transpose(1, 0, 2)).reshape(1, 1, 512, 8, HD),
            np.ascontiguousarray(r["ka_s"].T).reshape(1, 1, DEC, 2, HD), r["va_s"].reshape(1, 1, DEC, 2, HD),
            keys_b(r["kb_s"], DEC), r["vb_s"].reshape(1, 1, DEC, 8, HD))
```
